# Optimizing a Trainium2 kernel written in Bass

```python
import jax, jax.numpy as jnp
from jax import lax
import numpy as np
import math

D_MODEL = 1024
BATCH = 1
SEQ = 256
DEPTH = 2

N_A = DEPTH // 2
N_B = DEPTH - N_A
N_DENSE = (DEPTH + 1) // 2
N_MOE = DEPTH // 2

GLA_HEADS = 4
GLA_DK = D_MODEL // 2 // GLA_HEADS
GLA_DV = D_MODEL // GLA_HEADS
GLA_QK = GLA_HEADS * GLA_DK
GLA_V = GLA_HEADS * GLA_DV
GLA_GATE_RANK = 16
GLA_GATE_NORM = 16.0
GLA_CHUNK = 64
GLA_IN = 2 * GLA_QK + GLA_V + GLA_GATE_RANK + GLA_V

SB_HEADS = 8
SB_HEAD_DIM = D_MODEL // SB_HEADS
SB_BLOCK = 128

FFN_DIM = 2816
N_EXPERTS = 8
TOP_K = 2
EXPERT_DIM = 3584

RMS_EPS = 1e-6


def rms_norm(x, g):
    xf = x.astype(jnp.float32)
    y = xf * lax.rsqrt(jnp.mean(xf * xf, axis=-1, keepdims=True) + RMS_EPS)
    return (y * g.astype(jnp.float32)).astype(x.dtype)

def swiglu(h, w_gate, w_up, w_down):
    return (jax.nn.silu(h @ w_gate) * (h @ w_up)) @ w_down

def gla_mixer(h, w_in, w_gate_up, b_gate, g_head, w_out):
    B, S, _ = h.shape
    H, dk, dv, C = GLA_HEADS, GLA_DK, GLA_DV, GLA_CHUNK
    nc = S // C
    proj = h @ w_in
    q, k, v, g_lr, r = jnp.split(
        proj, [GLA_QK, 2 * GLA_QK, 2 * GLA_QK + GLA_V, 2 * GLA_QK + GLA_V + GLA_GATE_RANK], axis=-1)
    log_a = jax.nn.log_sigmoid((g_lr @ w_gate_up + b_gate).astype(jnp.float32)) / GLA_GATE_NORM

    def to_chunks(t, d):
        return t.reshape(B, nc, C, H, d).transpose(1, 0, 3, 2, 4).astype(jnp.float32)

    qc = to_chunks(q, dk) * (dk ** -0.5)
    kc = to_chunks(k, dk)
    vc = to_chunks(v, dv)
    gc = to_chunks(log_a, dk)
    b = jnp.cumsum(gc, axis=3)
    b_end = b[:, :, :, -1:, :]
    q_dec = qc * jnp.exp(b)
    k_inv = kc * jnp.exp(-b)
    k_end = kc * jnp.exp(b_end - b)
    decay_end = jnp.exp(b_end[:, :, :, 0, :])

    tri = jnp.tril(jnp.ones((C, C), dtype=bool))
    attn = jnp.where(tri, jnp.einsum('nbhid,nbhjd->nbhij', q_dec, k_inv), 0.0)
    o_intra = jnp.einsum('nbhij,nbhjv->nbhiv', attn, vc)

    def step(state, inp):
        q_n, k_n, v_n, dec_n = inp
        o_n = jnp.einsum('bhid,bhdv->bhiv', q_n, state)
        state = dec_n[..., None] * state + jnp.einsum('bhid,bhiv->bhdv', k_n, v_n)
        return state, o_n

    state0 = jnp.zeros((B, H, dk, dv), dtype=jnp.float32)
    _, o_inter = lax.scan(step, state0, (q_dec, k_end, vc, decay_end))
    o = (o_inter + o_intra).transpose(1, 0, 3, 2, 4).reshape(B, S, H, dv)
    o = rms_norm(o, g_head).reshape(B, S, GLA_V)
    o = (o * jax.nn.silu(r.astype(jnp.float32))).astype(h.dtype)
    return o @ w_out

def stick_breaking_mixer(h, k, v, w_q, w_out):
    B, S, _ = h.shape
    H, hd = SB_HEADS, SB_HEAD_DIM
    q = (h @ w_q).reshape(B, S, H, hd).transpose(0, 2, 1, 3)
    scale = hd ** -0.5
    outs = []
    for blk in range(S // SB_BLOCK):
        t0 = blk * SB_BLOCK
        t1 = t0 + SB_BLOCK
        qb = q[:, :, t0:t1]
        kb = k[:, :, :t1]
        vb = v[:, :, :t1]
        z = jnp.einsum('bhtd,bhsd->bhts', qb, kb).astype(jnp.float32) * scale
        t_idx = t0 + jnp.arange(SB_BLOCK)[:, None]
        s_idx = jnp.arange(t1)[None, :]
        causal = s_idx < t_idx
        log_beta = jax.nn.log_sigmoid(z)
        log_keep = jnp.where(causal, jax.nn.log_sigmoid(-z), 0.0)
        log_stay = lax.cumsum(log_keep, axis=3, reverse=True) - log_keep
        w = jnp.where(causal, jnp.exp(log_beta + log_stay), 0.0)
        outs.append(jnp.einsum('bhts,bhsd->bhtd', w.astype(vb.dtype), vb))
    o = jnp.concatenate(outs, axis=2).transpose(0, 2, 1, 3).reshape(B, S, H * hd)
    return o @ w_out

def moe_swiglu(h, w_router, w_gate, w_up, w_down):
    logits = (h @ w_router).astype(jnp.float32)
    top_val, top_idx = lax.top_k(logits, TOP_K)
    top_w = jax.nn.softmax(top_val, axis=-1)
    gates = jnp.sum(jax.nn.one_hot(top_idx, N_EXPERTS, dtype=jnp.float32) * top_w[..., None], axis=-2)
    out = jnp.zeros_like(h)
    for e in range(N_EXPERTS):
        y = swiglu(h, w_gate[e], w_up[e], w_down[e])
        out = out + gates[..., e:e + 1].astype(h.dtype) * y
    return out

def first_inputs(seed: int = 0) -> dict:
    key = jax.random.key(seed)
    ks = jax.random.split(key, 20)
    D = D_MODEL

    def w(k, shape, fan_in):
        return jax.random.normal(k, shape, dtype=jnp.float32) * (fan_in ** -0.5)

    def gain(k, shape):
        return 1.0 + 0.02 * jax.random.normal(k, shape, dtype=jnp.float32)

    return {
        "x": jax.random.normal(ks[0], (BATCH, SEQ, D), dtype=jnp.float32),
        "attn_norm": gain(ks[1], (DEPTH, D)),
        "ffn_norm": gain(ks[2], (DEPTH, D)),
        "kv_norm": gain(ks[3], (D,)),
        "final_norm": gain(ks[4], (D,)),
        "gla_w_in": w(ks[5], (N_A, D, GLA_IN), D),
        "gla_w_gate_up": w(ks[6], (N_A, GLA_GATE_RANK, GLA_QK), GLA_GATE_RANK),
        "gla_b_gate": 0.1 * jax.random.normal(ks[7], (N_A, GLA_QK), dtype=jnp.float32),
        "gla_head_norm": gain(ks[8], (N_A, GLA_DV)),
        "gla_w_out": w(ks[9], (N_A, GLA_V, D), GLA_V),
        "sb_w_kv": w(ks[10], (D, 2 * SB_HEADS * SB_HEAD_DIM), D),
        "sb_w_q": w(ks[11], (N_B, D, SB_HEADS * SB_HEAD_DIM), D),
        "sb_w_out": w(ks[12], (N_B, SB_HEADS * SB_HEAD_DIM, D), SB_HEADS * SB_HEAD_DIM),
        "ffn_w_gate": w(ks[13], (N_DENSE, D, FFN_DIM), D),
        "ffn_w_up": w(ks[14], (N_DENSE, D, FFN_DIM), D),
        "ffn_w_down": w(ks[15], (N_DENSE, FFN_DIM, D), FFN_DIM),
        "moe_w_router": w(ks[16], (N_MOE, D, N_EXPERTS), D),
        "moe_w_gate": w(ks[17], (N_MOE, N_EXPERTS, D, EXPERT_DIM), D),
        "moe_w_up": w(ks[18], (N_MOE, N_EXPERTS, D, EXPERT_DIM), D),
        "moe_w_down": w(ks[19], (N_MOE, N_EXPERTS, EXPERT_DIM, D), EXPERT_DIM),
    }

def first_block(x, attn_norm, ffn_norm, kv_norm, final_norm, gla_w_in, gla_w_gate_up, gla_b_gate,
              gla_head_norm, gla_w_out, sb_w_kv, sb_w_q, sb_w_out, ffn_w_gate, ffn_w_up, ffn_w_down,
              moe_w_router, moe_w_gate, moe_w_up, moe_w_down):
    B, S, D = x.shape
    h = x
    k_shared = None
    v_shared = None
    for layer in range(DEPTH):
        if layer < N_A:
            h = h + gla_mixer(rms_norm(h, attn_norm[layer]), gla_w_in[layer], gla_w_gate_up[layer],
                              gla_b_gate[layer], gla_head_norm[layer], gla_w_out[layer])
        else:
            if layer == N_A:
                kv = rms_norm(h, kv_norm) @ sb_w_kv
                k_s, v_s = jnp.split(kv, 2, axis=-1)
                k_shared = k_s.reshape(B, S, SB_HEADS, SB_HEAD_DIM).transpose(0, 2, 1, 3)
                v_shared = v_s.reshape(B, S, SB_HEADS, SB_HEAD_DIM).transpose(0, 2, 1, 3)
            ib = layer - N_A
            h = h + stick_breaking_mixer(rms_norm(h, attn_norm[layer]), k_shared, v_shared,
                                         sb_w_q[ib], sb_w_out[ib])
        hn = rms_norm(h, ffn_norm[layer])
        if layer % 2 == 0:
            i = layer // 2
            h = h + swiglu(hn, ffn_w_gate[i], ffn_w_up[i], ffn_w_down[i])
        else:
            i = layer // 2
            h = h + moe_swiglu(hn, moe_w_router[i], moe_w_gate[i], moe_w_up[i], moe_w_down[i])
    return rms_norm(h, final_norm)


CTX_LEN = 256
GRID_W = 64
N_EVEN = (DEPTH + 1) // 2
N_ODD = DEPTH // 2

A_GROUPS = 4
A_GROUP_DIM = 128
A_WIDTH = A_GROUPS * A_GROUP_DIM
A_CHUNK = 128
B_HEADS = 4
B_HEAD_DIM = 128
B_WIDTH = B_HEADS * B_HEAD_DIM
B_CONV = 3
GDN_CHUNK = 64
AB_SPLITS = (A_WIDTH, 2 * A_WIDTH, 2 * A_WIDTH + 3 * B_WIDTH, 2 * A_WIDTH + 4 * B_WIDTH,
             2 * A_WIDTH + 4 * B_WIDTH + 2 * B_HEADS)
AB_IN = 2 * A_WIDTH + 4 * B_WIDTH + 4 * B_HEADS
AB_MIX = A_WIDTH + B_WIDTH
C_HEADS = 8
C_NOPE = 128
C_ROPE = 64
C_VDIM = 128
C_Q_LORA = 384
C_KV_LORA = 256
C_IN = C_Q_LORA + C_KV_LORA + C_ROPE
Q_BLOCK = 128
ROPE_THETA = 10000.0
D_FF = 2816
FFN_CONV = 3
EPS = 1e-6


def rms_norm_2(x, g):
    xf = x.astype(jnp.float32)
    y = xf * lax.rsqrt(jnp.mean(xf * xf, axis=-1, keepdims=True) + EPS)
    return (y * g.astype(jnp.float32)).astype(x.dtype)

def layer_norm(x, g, b):
    xf = x.astype(jnp.float32)
    mu = jnp.mean(xf, axis=-1, keepdims=True)
    var = jnp.mean(jnp.square(xf - mu), axis=-1, keepdims=True)
    y = (xf - mu) * lax.rsqrt(var + EPS) * g.astype(jnp.float32) + b.astype(jnp.float32)
    return y.astype(x.dtype)

def modulate(h, shift, scale):
    return h * (1 + scale) + shift

def ada_mod(cond, w, b):
    m = (jax.nn.silu(cond) @ w + b)[..., None, :]
    return jnp.split(m, 6, axis=-1)

def dwconv(x, w):
    k = w.shape[0]
    return lax.conv_general_dilated(x, w[:, None, :], (1,), [(k // 2, k // 2)],
                                    dimension_numbers=('NWC', 'WIO', 'NWC'),
                                    feature_group_count=x.shape[-1])

def axial_rope(n, rot_dim):
    rows = n // GRID_W
    row = jnp.repeat(jnp.arange(rows, dtype=jnp.float32), GRID_W)
    col = jnp.tile(jnp.arange(GRID_W, dtype=jnp.float32), rows)
    n_freq = rot_dim // 4
    inv = ROPE_THETA ** (-jnp.arange(n_freq, dtype=jnp.float32) / n_freq)
    ang = jnp.concatenate([row[:, None] * inv, col[:, None] * inv], axis=-1)
    return jnp.cos(ang), jnp.sin(ang)

def apply_rope(x, cos, sin):
    h = x.shape[-1] // 2
    x1, x2 = x[..., :h], x[..., h:]
    cos = cos.astype(x.dtype)
    sin = sin.astype(x.dtype)
    return jnp.concatenate([x1 * cos - x2 * sin, x2 * cos + x1 * sin], axis=-1)

def chunk_gmlp(u, v, ln_g, ln_b, ws, bs):
    u = jax.nn.gelu(u, approximate=False)
    v = layer_norm(jax.nn.gelu(v, approximate=False), ln_g, ln_b)
    bn, l, _ = v.shape
    vc = v.reshape(bn, l // A_CHUNK, A_CHUNK, A_GROUPS, A_GROUP_DIM)
    s = jnp.einsum('gij,bnjgd->bnigd', ws, vc) + bs.T[None, None, :, :, None]
    return u * s.reshape(bn, l, A_WIDTH)

def gdn_chunked(q, k, v, g, beta, s0):
    bn, l, h, dk = q.shape
    cs = GDN_CHUNK
    n = l // cs
    to_c = lambda t: t.reshape(bn, n, cs, h, t.shape[-1]).transpose(1, 0, 3, 2, 4)
    qc, kc, vc = to_c(q), to_c(k), to_c(v)
    gc = g.reshape(bn, n, cs, h).transpose(1, 0, 3, 2)
    bc = beta.reshape(bn, n, cs, h).transpose(1, 0, 3, 2)
    gcum = jnp.cumsum(gc, axis=-1)
    tri_incl = jnp.tril(jnp.ones((cs, cs), bool))
    tri_strict = jnp.tril(jnp.ones((cs, cs), bool), -1)
    diff = gcum[..., :, None] - gcum[..., None, :]
    decay = jnp.exp(jnp.where(tri_incl, diff, -jnp.inf))
    kb = kc * bc[..., None]
    vb = vc * bc[..., None]
    a_mat = jnp.where(tri_strict, jnp.einsum('nbhid,nbhjd->nbhij', kb, kc) * decay, 0.0)
    eye = jnp.eye(cs, dtype=jnp.float32)
    t_mat = lax.linalg.triangular_solve(eye + a_mat, jnp.broadcast_to(eye, a_mat.shape),
                                        left_side=True, lower=True, unit_diagonal=True)
    u = jnp.einsum('nbhij,nbhjd->nbhid', t_mat, vb)
    w = jnp.einsum('nbhij,nbhjd->nbhid', t_mat, kb * jnp.exp(gcum)[..., None])
    attn = jnp.einsum('nbhid,nbhjd->nbhij', qc, kc) * decay
    qg = qc * jnp.exp(gcum)[..., None]
    kdec = kc * jnp.exp(gcum[..., -1:] - gcum)[..., None]
    gend = jnp.exp(gcum[..., -1])

    def step(s, xs):
        u_i, w_i, qg_i, kd_i, at_i, ge_i = xs
        v_new = u_i - jnp.einsum('bhck,bhkv->bhcv', w_i, s)
        o_i = jnp.einsum('bhck,bhkv->bhcv', qg_i, s) + jnp.einsum('bhij,bhjv->bhiv', at_i, v_new)
        s = s * ge_i[..., None, None] + jnp.einsum('bhck,bhcv->bhkv', kd_i, v_new)
        return s, o_i

    s_fin, o = lax.scan(step, s0, (u, w, qg, kdec, attn, gend))
    o = o.transpose(1, 0, 3, 2, 4).reshape(bn, l, h, v.shape[-1])
    return o, s_fin

def gated_deltanet(qkv, gate, alpha_raw, beta_raw, conv_w, a_log, dt_bias, norm_g, s0_pair):
    bn, l, _ = qkv.shape
    hq = jax.nn.silu(dwconv(qkv, conv_w)).astype(jnp.float32)
    q, k, v = jnp.split(hq, 3, axis=-1)
    l2 = lambda t: t * lax.rsqrt(jnp.sum(t * t, axis=-1, keepdims=True) + EPS)
    q = l2(q.reshape(bn, l, B_HEADS, B_HEAD_DIM)) * (B_HEAD_DIM ** -0.5)
    k = l2(k.reshape(bn, l, B_HEADS, B_HEAD_DIM))
    v = v.reshape(bn, l, B_HEADS, B_HEAD_DIM)
    a = alpha_raw.astype(jnp.float32).reshape(bn, l, 2, B_HEADS)
    beta = jax.nn.sigmoid(beta_raw.astype(jnp.float32).reshape(bn, l, 2, B_HEADS))
    log_alpha = -jnp.exp(a_log.astype(jnp.float32)) * jax.nn.softplus(a + dt_bias.astype(jnp.float32))
    o_f, s_f = gdn_chunked(q, k, v, log_alpha[:, :, 0], beta[:, :, 0], s0_pair[0])
    flip = lambda t: jnp.flip(t, axis=1)
    o_b, s_b = gdn_chunked(flip(q), flip(k), flip(v), flip(log_alpha[:, :, 1]), flip(beta[:, :, 1]), s0_pair[1])
    o = o_f + flip(o_b)
    o = rms_norm_2(o, norm_g) * jax.nn.silu(gate.astype(jnp.float32).reshape(bn, l, B_HEADS, B_HEAD_DIM))
    return o.reshape(bn, l, B_WIDTH).astype(qkv.dtype), (s_f, s_b)

def ab_mixer(h_ctx, h_lat, w_in, a_ln_g, a_ln_b, a_ws, a_bs, conv_w, a_log, dt_bias, norm_g, w_out,
             need_ctx_out):
    def run(h, state0, want_out):
        a_u, a_v, qkv, gate, alpha_raw, beta_raw = jnp.split(h @ w_in, AB_SPLITS, axis=-1)
        y_b, state = gated_deltanet(qkv, gate, alpha_raw, beta_raw, conv_w, a_log, dt_bias, norm_g, state0)
        if not want_out:
            return None, state
        y_a = chunk_gmlp(a_u, a_v, a_ln_g, a_ln_b, a_ws, a_bs)
        return jnp.concatenate([y_a, y_b], axis=-1) @ w_out, state

    zero = jnp.zeros((h_ctx.shape[0], B_HEADS, B_HEAD_DIM, B_HEAD_DIM), jnp.float32)
    y_ctx, ctx_state = run(h_ctx, (zero, zero), need_ctx_out)
    y_lat, _ = run(h_lat, ctx_state, True)
    return y_ctx, y_lat

def block_attention(qn, qr, kn, kr, v):
    bn, l, h, _ = qn.shape
    nb = l // Q_BLOCK
    scale = (C_NOPE + C_ROPE) ** -0.5
    blocks = lambda t: t.reshape(bn, nb, Q_BLOCK, h, t.shape[-1]).transpose(1, 0, 2, 3, 4)

    def one(blk):
        qn_b, qr_b = blk
        s = jnp.einsum('bqhd,bkhd->bhqk', qn_b, kn) + jnp.einsum('bqhd,bkd->bhqk', qr_b, kr)
        p = jax.nn.softmax(s.astype(jnp.float32) * scale, axis=-1).astype(v.dtype)
        return jnp.einsum('bhqk,bkhd->bqhd', p, v)

    o = lax.map(one, (blocks(qn), blocks(qr)))
    return o.transpose(1, 0, 2, 3, 4).reshape(bn, l, h * v.shape[-1])

def mla_mixer(h_ctx, h_lat, w_in, q_norm_g, kv_norm_g, w_uq, w_ukv, w_out, need_ctx_out):
    n_lat = h_lat.shape[1]
    cos, sin = axial_rope(n_lat, C_ROPE)
    rot_q = lambda t: apply_rope(t, cos[:, None, :], sin[:, None, :])
    rot_k = lambda t: apply_rope(t, cos, sin)
    no_rot = lambda t: t

    def queries(cq, rot):
        bn, l, _ = cq.shape
        q = (rms_norm_2(cq, q_norm_g) @ w_uq).reshape(bn, l, C_HEADS, C_NOPE + C_ROPE)
        return q[..., :C_NOPE], rot(q[..., C_NOPE:])

    def keys(kv_part, rot):
        bn, l, _ = kv_part.shape
        ckv, kr = jnp.split(kv_part, [C_KV_LORA], axis=-1)
        kv = (rms_norm_2(ckv, kv_norm_g) @ w_ukv).reshape(bn, l, C_HEADS, C_NOPE + C_VDIM)
        return kv[..., :C_NOPE], rot(kr), kv[..., C_NOPE:]

    z_lat = h_lat @ w_in
    kn_l, kr_l, v_l = keys(z_lat[..., C_Q_LORA:], rot_k)
    qn_l, qr_l = queries(z_lat[..., :C_Q_LORA], rot_q)
    if need_ctx_out:
        z_ctx = h_ctx @ w_in
        kv_ctx = z_ctx[..., C_Q_LORA:]
    else:
        kv_ctx = h_ctx @ w_in[:, C_Q_LORA:]
    kn_c, kr_c, v_c = keys(kv_ctx, no_rot)
    kn = jnp.concatenate([kn_c, kn_l], axis=1)
    kr = jnp.concatenate([kr_c, kr_l], axis=1)
    v = jnp.concatenate([v_c, v_l], axis=1)
    y_lat = block_attention(qn_l, qr_l, kn, kr, v) @ w_out
    y_ctx = None
    if need_ctx_out:
        qn_c, qr_c = queries(z_ctx[..., :C_Q_LORA], no_rot)
        y_ctx = block_attention(qn_c, qr_c, kn_c, kr_c, v_c) @ w_out
    return y_ctx, y_lat

def conv_ffn(h, w_up, conv_w, w_down):
    g, u = jnp.split(dwconv(h @ w_up, conv_w), 2, axis=-1)
    return (jax.nn.silu(g) * u) @ w_down

def second_inputs(seed: int = 0) -> dict:
    key = jax.random.key(seed)
    ks = iter(jax.random.split(key, 32))
    nrm = lambda shape, s: jax.random.normal(next(ks), shape, jnp.float32) * s
    gain = lambda shape: 1.0 + nrm(shape, 0.02)
    d = D_MODEL
    a_log = jnp.log(jax.random.uniform(next(ks), (N_EVEN, 2, B_HEADS), jnp.float32, 1.0, 16.0))
    dt = jnp.exp(jax.random.uniform(next(ks), (N_EVEN, 2, B_HEADS), jnp.float32,
                                    math.log(1e-3), math.log(1e-1)))
    dt_bias = dt + jnp.log(-jnp.expm1(-dt))
    return {
        'x': nrm((BATCH, SEQ, d), 1.0),
        'c': nrm((BATCH, d), 1.0),
        'ctx': nrm((BATCH, CTX_LEN, d), 1.0),
        'c_ctx': nrm((d,), 1.0),
        'ada_w': nrm((DEPTH, d, 6 * d), d ** -0.5),
        'ada_b': nrm((DEPTH, 6 * d), 0.01),
        'norm1_g': gain((DEPTH, d)),
        'norm2_g': gain((DEPTH, d)),
        'ab_w_in': nrm((N_EVEN, d, AB_IN), d ** -0.5),
        'a_ln_g': gain((N_EVEN, A_WIDTH)),
        'a_ln_b': nrm((N_EVEN, A_WIDTH), 0.01),
        'a_ws': nrm((N_EVEN, A_GROUPS, A_CHUNK, A_CHUNK), 0.5 * A_CHUNK ** -0.5),
        'a_bs': 1.0 + nrm((N_EVEN, A_GROUPS, A_CHUNK), 0.1),
        'b_conv_w': nrm((N_EVEN, B_CONV, 3 * B_WIDTH), B_CONV ** -0.5),
        'b_a_log': a_log,
        'b_dt_bias': dt_bias,
        'b_norm_g': gain((N_EVEN, B_HEAD_DIM)),
        'ab_w_out': nrm((N_EVEN, AB_MIX, d), AB_MIX ** -0.5),
        'mla_w_in': nrm((N_ODD, d, C_IN), d ** -0.5),
        'mla_q_norm_g': gain((N_ODD, C_Q_LORA)),
        'mla_kv_norm_g': gain((N_ODD, C_KV_LORA)),
        'mla_w_uq': nrm((N_ODD, C_Q_LORA, C_HEADS * (C_NOPE + C_ROPE)), C_Q_LORA ** -0.5),
        'mla_w_ukv': nrm((N_ODD, C_KV_LORA, C_HEADS * (C_NOPE + C_VDIM)), C_KV_LORA ** -0.5),
        'mla_w_out': nrm((N_ODD, C_HEADS * C_VDIM, d), (C_HEADS * C_VDIM) ** -0.5),
        'ffn_w_up': nrm((DEPTH, d, 2 * D_FF), d ** -0.5),
        'ffn_conv_w': nrm((DEPTH, FFN_CONV, 2 * D_FF), FFN_CONV ** -0.5),
        'ffn_w_down': nrm((DEPTH, D_FF, d), D_FF ** -0.5),
        'final_g': gain((d,)),
    }

def second_block(x, c, ctx, c_ctx, ada_w, ada_b, norm1_g, norm2_g, ab_w_in, a_ln_g, a_ln_b, a_ws, a_bs,
              b_conv_w, b_a_log, b_dt_bias, b_norm_g, ab_w_out, mla_w_in, mla_q_norm_g, mla_kv_norm_g,
              mla_w_uq, mla_w_ukv, mla_w_out, ffn_w_up, ffn_conv_w, ffn_w_down, final_g):
    lat, cx = x, ctx
    for i in range(DEPTH):
        last = i == DEPTH - 1
        j = i // 2
        sh1, sc1, g1, sh2, sc2, g2 = ada_mod(c, ada_w[i], ada_b[i])
        csh1, csc1, cg1, csh2, csc2, cg2 = ada_mod(c_ctx, ada_w[i], ada_b[i])
        h_lat = modulate(rms_norm_2(lat, norm1_g[i]), sh1, sc1)
        h_ctx = modulate(rms_norm_2(cx, norm1_g[i]), csh1, csc1)
        if i % 2 == 0:
            y_ctx, y_lat = ab_mixer(h_ctx, h_lat, ab_w_in[j], a_ln_g[j], a_ln_b[j], a_ws[j], a_bs[j],
                                    b_conv_w[j], b_a_log[j], b_dt_bias[j], b_norm_g[j], ab_w_out[j],
                                    not last)
        else:
            y_ctx, y_lat = mla_mixer(h_ctx, h_lat, mla_w_in[j], mla_q_norm_g[j], mla_kv_norm_g[j],
                                     mla_w_uq[j], mla_w_ukv[j], mla_w_out[j], not last)
        lat = lat + g1 * y_lat
        lat = lat + g2 * conv_ffn(modulate(rms_norm_2(lat, norm2_g[i]), sh2, sc2),
                                  ffn_w_up[i], ffn_conv_w[i], ffn_w_down[i])
        if not last:
            cx = cx + cg1 * y_ctx
            cx = cx + cg2 * conv_ffn(modulate(rms_norm_2(cx, norm2_g[i]), csh2, csc2),
                                     ffn_w_up[i], ffn_conv_w[i], ffn_w_down[i])
    return rms_norm_2(lat, final_g)


def setup_inputs(seed=0):
    out = dict(first_inputs(seed))
    for name, value in second_inputs(seed + 1).items():
        if name != "x":
            out[name + "_2"] = value
    return out


def reference(
    x, attn_norm, ffn_norm, kv_norm, final_norm, gla_w_in, gla_w_gate_up, gla_b_gate,
    gla_head_norm, gla_w_out, sb_w_kv, sb_w_q, sb_w_out, ffn_w_gate, ffn_w_up, ffn_w_down,
    moe_w_router, moe_w_gate, moe_w_up, moe_w_down, c_2, ctx_2, c_ctx_2, ada_w_2, ada_b_2,
    norm1_g_2, norm2_g_2, ab_w_in_2, a_ln_g_2, a_ln_b_2, a_ws_2, a_bs_2, b_conv_w_2, b_a_log_2,
    b_dt_bias_2, b_norm_g_2, ab_w_out_2, mla_w_in_2, mla_q_norm_g_2, mla_kv_norm_g_2,
    mla_w_uq_2, mla_w_ukv_2, mla_w_out_2, ffn_w_up_2, ffn_conv_w_2, ffn_w_down_2, final_g_2,
):
    x = first_block(
        x, attn_norm, ffn_norm, kv_norm, final_norm, gla_w_in, gla_w_gate_up, gla_b_gate,
        gla_head_norm, gla_w_out, sb_w_kv, sb_w_q, sb_w_out, ffn_w_gate, ffn_w_up, ffn_w_down,
        moe_w_router, moe_w_gate, moe_w_up, moe_w_down,
    )
    return second_block(
        x, c_2, ctx_2, c_ctx_2, ada_w_2, ada_b_2, norm1_g_2, norm2_g_2, ab_w_in_2, a_ln_g_2,
        a_ln_b_2, a_ws_2, a_bs_2, b_conv_w_2, b_a_log_2, b_dt_bias_2, b_norm_g_2, ab_w_out_2,
        mla_w_in_2, mla_q_norm_g_2, mla_kv_norm_g_2, mla_w_uq_2, mla_w_ukv_2, mla_w_out_2,
        ffn_w_up_2, ffn_conv_w_2, ffn_w_down_2, final_g_2,
    )


_drawn_inputs = setup_inputs


def setup_inputs(seed=0):
    import zlib

    import numpy as np

    out = dict(_drawn_inputs(seed))
    spreads = {}
    factors = {'ada_b_2': 2.747,
     'norm1_g_2': 4.412,
     'norm2_g_2': 3.21,
     'a_ln_g_2': 8.0,
     'a_ln_b_2': 24.552,
     'b_norm_g_2': 8.0,
     'mla_q_norm_g_2': 8.0,
     'mla_kv_norm_g_2': 8.0,
     'final_g_2': 8.034}
    for name, (base, spread) in spreads.items():
        noise = np.random.default_rng([zlib.crc32(name.encode()), seed]).standard_normal(out[name].shape)
        drawn = base * np.exp(spread * noise) if base else spread * noise
        out[name] = __import__('jax').numpy.asarray(drawn.astype(out[name].dtype))
    for name, factor in factors.items():
        out[name] = (out[name] * factor).astype(out[name].dtype)
    return out
```

```python
from contextlib import ExitStack

import numpy as np

import concourse.bass as bass
from concourse import mybir

F32 = mybir.dt.float32
U32 = mybir.dt.uint32
ALU = mybir.AluOpType
ACT = mybir.ActivationFunctionType
AXX = mybir.AxisListType.X

P = 128
D = 1024
KT = D // P
SEQ = 256
TT = SEQ // P
TILE = 2048
RING = 7
CHUNK = 64
H1, DV1 = 4, 256
SBH = 8
EXPERTS = 8
F_MOE = 3584 // P
F_FFN = 2816 // P
FF = 2816
EPS = 1e-6
GH = 4
MH = 8
BANKS_PLAIN = [0, 1, 2, 3, 0, 1, 2]
BANKS_CONV = [0, 1, 2, 0, 1, 2, 1]


def since(pattern, s):
    n = len(pattern)
    return next(d for d in range(1, n + 1) if pattern[(s - d) % n] == pattern[s])


class Done:

    def __init__(self, sem):
        self.sem, self.n = sem, 0

    def by(self, ins):
        ins.then_inc(self.sem, 1)
        self.n += 1
        return self.n


def build(nc, stream, params, where, out):
    n_tiles = stream.shape[0]
    width = params.shape[1]
    with ExitStack() as ctx:
        def sb(name, shape, dt=F32):
            return ctx.enter_context(nc.sbuf_tensor(name, shape, dt))

        def sem(name):
            return ctx.enter_context(nc.semaphore(name))

        ring = sb("ring", [P, RING, TILE])
        par = sb("par", [P, width])
        h = sb("h", [P, TT, D])
        cx = sb("cx", [P, TT, D])
        hT = sb("hT", [P, KT, 2 * SEQ])
        ARENA = 20096
        arena = sb("arena", [P, ARENA])
        ada = sb("ada", [P, 2, 48, 2])
        small = sb("small", [P, 512])
        ps = ctx.enter_context(nc.psum_tensor("ps", [P, 8, 512], F32))

        landed = [sem(f"landed{i}") for i in range(RING)]
        params_in = sem("params_in")
        x_in = sem("x_in")
        stored = sem("stored")
        tile_used = Done(sem("tile_used"))
        pe_done = Done(sem("pe_done"))
        act_done = Done(sem("act_done"))
        dve_done = Done(sem("dve_done"))
        pool_done = Done(sem("pool_done"))
        everyone = (tile_used, pe_done, act_done, dve_done, pool_done)

        def after_all(eng):
            for d in everyone:
                if d.n:
                    eng.wait_ge(d.sem, d.n)

        def link(eng, done, ins):
            eng.wait_ge(done.sem, done.by(ins))

        def c(name, a=0, b=None):
            off, n = where[name]
            return par[:, off + a:off + (n if b is None else b)]

        cur = [0]

        def reset(at=0):
            cur[0] = at

        def take(*shape):
            n = int(np.prod(shape))
            assert cur[0] + n <= ARENA, (cur[0], n)
            v = arena[:, cur[0]:cur[0] + n]
            cur[0] += n
            if len(shape) == 2:
                v = v.rearrange("p (a b) -> p a b", a=shape[0])
            if len(shape) == 3:
                v = v.rearrange("p (a b c) -> p a b c", a=shape[0], b=shape[1])
            return v

        ident, ones = c("ident"), c("ones")
        block = ctx.enter_context(nc.Block())

        @block.sync
        def _(sp):
            sp.dma_start(par[:, :], params).then_inc(params_in, 16)
            for t in range(RING):
                sp.dma_start(ring[:, t, :], stream[t]).then_inc(landed[t], 16)
            with sp.Fori(1, n_tiles // RING) as turn:
                for s in range(RING):
                    sp.wait_ge(tile_used.sem, turn * RING + (s - RING + 1))
                    sp.dma_start(ring[:, s, :], stream[turn * RING + s]).then_inc(landed[s], 16)
            for t in range(n_tiles // RING * RING, n_tiles):
                sp.wait_ge(tile_used.sem, t - RING + 1)
                sp.dma_start(ring[:, t % RING, :], stream[t]).then_inc(landed[t % RING], 16)

        def weights(pe, ahead=0):
            t = tile_used.n + ahead
            pe.wait_ge(landed[t % RING], 16 * (t // RING + 1))
            return ring[:, t % RING, :]

        freed = [[] for _ in range(8)]

        def claim(pe, *banks):
            for b in banks:
                for d, n in freed[b]:
                    pe.wait_ge(d.sem, n)
                freed[b] = []

        def feature_tile(banks, src, tok0, ntok):
            @block.tensor
            def _(pe):
                w = weights(pe).rearrange("p (k n) -> p k n", k=KT)
                claim(pe, *set(banks))
                for half in range(2):
                    o = ps[:, banks[half], :]
                    if banks[0] == banks[1]:
                        o = ps[:, banks[0], half * 256:half * 256 + 256]
                    for k in range(KT):
                        last = nc.tensor.matmul(o[:, 0:ntok], w[:, k, half * P:half * P + P],
                                                src[:, k, tok0:tok0 + ntok],
                                                start=(k == 0), stop=(k == KT - 1))
                tile_used.by(last)
            return tile_used.n

        def token_rows(banks, src, tok0, ktiles, cols=512, kper=4):
            @block.tensor
            def _(pe):
                claim(pe, *banks)
                for t0 in range(0, ktiles, kper):
                    w = weights(pe).rearrange("p (k n) -> p k n", k=kper)
                    for n, b in enumerate(banks):
                        for k in range(t0, min(t0 + kper, ktiles)):
                            last = nc.tensor.matmul(ps[:, b, 0:cols],
                                                    src[:, k, tok0 + n * P:tok0 + n * P + P],
                                                    w[:, k - t0, 0:cols],
                                                    start=(k == 0), stop=(k == ktiles - 1))
                    tile_used.by(last)
            return tile_used.n

        def inverse_root(pool, out_, in_):
            link(pool, pool_done, nc.gpsimd.tensor_tensor(out_, in_, half_pow[:, 0:in_.shape[1]], ALU.pow))

        def norm_T(x, outs, tok0, scratch):
            for t in range(TT):
                @block.scalar
                def _(act):
                    after_all(act)
                    link(act, act_done, nc.scalar.activation(scratch[:, t, :], x[:, t, :], ACT.Square,
                                                             accum_out=small[:, t:t + 1]))

            @block.vector
            def _(dve):
                dve.wait_ge(act_done.sem, act_done.n)
                link(dve, dve_done, nc.vector.tensor_scalar(small[:, 2:4], small[:, 0:2], 1.0 / D, EPS,
                                                            ALU.mult, ALU.add))

            @block.gpsimd
            def _(pool):
                pool.wait_ge(dve_done.sem, dve_done.n)
                inverse_root(pool, small[:, 4:6], small[:, 2:4])

            for t in range(TT):
                @block.vector
                def _(dve):
                    dve.wait_ge(pool_done.sem, pool_done.n)
                    link(dve, dve_done, nc.vector.tensor_scalar(scratch[:, t, :], x[:, t, :],
                                                                small[:, 4 + t:5 + t], None, ALU.mult))
                for q in range(2):
                    b = (2 * t + q) % 4

                    @block.tensor
                    def _(pe):
                        claim(pe, b)
                        pe.wait_ge(dve_done.sem, dve_done.n)
                        for j in range(4):
                            last = nc.tensor.transpose(ps[:, b, j * P:j * P + P],
                                                       scratch[:, t, (4 * q + j) * P:(4 * q + j + 1) * P], ident)
                        pe_done.by(last)

                for q in range(2):
                    b = (2 * t + q) % 4

                    @block.vector
                    def _(dve):
                        dve.wait_ge(pe_done.sem, pe_done.n - 1 + q)
                        for dst, gain, shift in outs:
                            for j in range(4):
                                k = 4 * q + j
                                o = dst[:, k, tok0 + t * P:tok0 + t * P + P]
                                if shift is None:
                                    ins = nc.vector.tensor_scalar(o, ps[:, b, j * P:j * P + P], gain[:, k:k + 1],
                                                                  None, ALU.mult)
                                else:
                                    ins = nc.vector.tensor_scalar(o, ps[:, b, j * P:j * P + P], gain[:, k:k + 1],
                                                                  shift[:, k:k + 1], ALU.mult, ALU.add)
                        dve_done.by(ins)
                        freed[b] = [(dve_done, dve_done.n)]

        def copy_bank(b, dst, cols=slice(0, 512)):
            @block.vector
            def _(dve):
                dve.wait_ge(tile_used.sem, tile_used.n)
                dve.wait_ge(pe_done.sem, pe_done.n) if pe_done.n else None
                dve_done.by(nc.vector.tensor_copy(dst, ps[:, b, cols]))
                freed[b] = [(dve_done, dve_done.n)]

        def add_rows(banks, x, half, gate=None, scratch=None):
            @block.vector
            def _(dve):
                dve.wait_ge(tile_used.sem, tile_used.n)
                for n, b in enumerate(banks):
                    xs = x(n)[:, half * 512:half * 512 + 512]
                    if gate is None:
                        dve_done.by(nc.vector.tensor_tensor(xs, xs, ps[:, b, :], ALU.add))
                    else:
                        link(dve, dve_done, nc.vector.tensor_tensor(scratch[:, n, :], ps[:, b, :],
                                                                    gate(n)[:, half * 512:half * 512 + 512], ALU.mult))
                        dve_done.by(nc.vector.tensor_tensor(xs, xs, scratch[:, n, :], ALU.add))
                    freed[b] = [(dve_done, dve_done.n)]

        half_pow = small[:, 496:512]

        @block.scalar
        def _(act):
            for t in range(TT):
                act.dma_start(h[:, t, :], out["x"][t * P:t * P + P, :]).then_inc(x_in, 16)
                act.dma_start(cx[:, t, :], out["ctx"][t * P:t * P + P, :]).then_inc(x_in, 16)

        @block.gpsimd
        def _(pool):
            pool_done.by(nc.gpsimd.memset(half_pow, -0.5))

        for eng in (block.tensor, block.scalar, block.vector, block.gpsimd):
            @eng
            def _(e):
                e.wait_ge(params_in, 16)
                e.wait_ge(x_in, 16 * 2 * TT)

        @block.scalar
        def _(act):
            link(act, act_done, nc.scalar.activation(c("cond"), c("cond"), ACT.Silu))
        cond = c("cond").rearrange("p (k n) -> p k n", k=KT)

        def ada_tiles(tile0, n):
            @block.tensor
            def _(pe):
                claim(pe, 7)
                pe.wait_ge(act_done.sem, act_done.n)
                for t in range(n):
                    w = weights(pe).rearrange("p (k n) -> p k n", k=KT)
                    for half in range(2):
                        col = 2 * (2 * t + half)
                        for k in range(KT):
                            last = nc.tensor.matmul(ps[:, 7, col:col + 2], w[:, k, half * P:half * P + P],
                                                    cond[:, k, :], start=(k == 0), stop=(k == KT - 1))
                    tile_used.by(last)

            @block.vector
            def _(dve):
                dve.wait_ge(tile_used.sem, tile_used.n)
                a = ada.rearrange("p l n c -> p (l n c)")[:, 4 * tile0:4 * (tile0 + n)]
                dve_done.by(nc.vector.tensor_tensor(a, ps[:, 7, 0:4 * n],
                                                    c("ada_b", 4 * tile0, 4 * (tile0 + n)), ALU.add))
                freed[7] = [(dve_done, dve_done.n)]

        ada_tiles(0, 24)
        ada_tiles(24, 24)

        reset()
        xs = take(TT, D)
        norm_T(h, [(hT, c("attn0"), None)], 0, xs)
        reset()
        qdec, kinv, kend = take(H1, SEQ), take(H1, SEQ), take(H1, SEQ)
        q31, q30, q20 = take(H1, CHUNK), take(H1, CHUNK), take(H1, CHUNK)
        expb, expnb, expe = take(H1, SEQ), take(H1, SEQ), take(H1, SEQ)
        v = take(TT, D)
        rT = take(KT, SEQ)
        la = take(TT, 512)
        tmp = take(TT, 512)
        glr = take(SEQ)
        bend, de = take(16).rearrange("p (h n) -> p h n", h=H1), take(16).rearrange("p (h n) -> p h n", h=H1)
        e12 = take(H1)
        aT = take(H1, TT, SEQ)
        oo = take(TT, D)

        @block.tensor
        def _(pe):
            after_all(pe)
            wl = c("w_glr").rearrange("p (k n) -> p k n", k=KT)
            for k in range(KT):
                last = nc.tensor.matmul(ps[0:16, 0, 0:SEQ], wl[:, k, :], hT[:, k, 0:SEQ],
                                        start=(k == 0), stop=(k == KT - 1))
            pe_done.by(last)

        @block.vector
        def _(dve):
            after_all(dve)
            dve_done.by(nc.vector.tensor_copy(glr[0:16, :], ps[0:16, 0, 0:SEQ]))

        @block.tensor
        def _(pe):
            after_all(pe)
            for t in range(TT):
                nc.tensor.matmul(ps[:, 1 + t, :], glr[0:16, t * P:t * P + P], c("gate_up")[0:16, :],
                                 start=True, stop=False)
                last = nc.tensor.matmul(ps[:, 1 + t, :], ones[0:1, :], c("gate_b")[0:1, :],
                                        start=False, stop=True)
            pe_done.by(last)

        @block.scalar
        def _(act):
            after_all(act)
            link(act, act_done, nc.scalar.activation(tmp, ps[:, 1:3, :], ACT.Abs))
            link(act, act_done, nc.scalar.activation(tmp, tmp, ACT.Exp, scale=-1.0))
            link(act, act_done, nc.scalar.activation(tmp, tmp, ACT.Ln, bias=1.0))

        @block.vector
        def _(dve):
            after_all(dve)
            dve_done.by(nc.vector.scalar_tensor_tensor(la, ps[:, 1:3, :], 0.0, tmp, ALU.min, ALU.subtract))

        @block.tensor
        def _(pe):
            after_all(pe)
            for hh in range(H1):
                for t in range(TT):
                    last = nc.tensor.matmul(ps[:, hh // 2, (hh % 2) * SEQ + t * P:(hh % 2) * SEQ + t * P + P],
                                            la[:, t, hh * P:hh * P + P], c("gla_sum"), start=True, stop=True)
            pe_done.by(last)

        pb = ps[:, 0:2, :].rearrange("p b (h n c) -> p (b h) n c", h=2, c=CHUNK)

        @block.scalar
        def _(act):
            after_all(act)
            link(act, act_done, nc.scalar.activation(expb.rearrange("p h t -> p (h t)"), ps[:, 0:2, :], ACT.Exp))
            link(act, act_done, nc.scalar.activation(expnb.rearrange("p h t -> p (h t)"), ps[:, 0:2, :], ACT.Exp,
                                                     scale=-1.0))

        @block.vector
        def _(dve):
            after_all(dve)
            link(dve, dve_done, nc.vector.tensor_copy(bend, pb[:, :, :, CHUNK - 1]))
            for hh in range(H1):
                ins = nc.vector.tensor_tensor(
                    expe[:, hh, :].rearrange("p (n c) -> p n c", c=CHUNK),
                    bend[:, hh, :].unsqueeze(2).to_broadcast([P, 4, CHUNK]), pb[:, hh, :, :], ALU.subtract)
            dve_done.by(ins)

        @block.scalar
        def _(act):
            after_all(act)
            link(act, act_done, nc.scalar.activation(expe, expe, ACT.Exp))
            link(act, act_done, nc.scalar.activation(de, bend, ACT.Exp))

        for n in range(2):
            feature_tile([2 + n, 2 + n], hT, 0, SEQ)

            @block.vector
            def _(dve):
                after_all(dve)
                dve_done.by(nc.vector.scalar_tensor_tensor(
                    qdec[:, 2 * n:2 * n + 2, :].rearrange("p h t -> p (h t)"), ps[:, 2 + n, :], float(P) ** -0.5,
                    expb[:, 2 * n:2 * n + 2, :].rearrange("p h t -> p (h t)"), ALU.mult, ALU.mult))
                freed[2 + n] = [(dve_done, dve_done.n)]
        for n in range(2):
            feature_tile([4 + n, 4 + n], hT, 0, SEQ)

            @block.vector
            def _(dve):
                after_all(dve)
                kp = ps[:, 4 + n, :]
                nc.vector.tensor_tensor(kinv[:, 2 * n:2 * n + 2, :].rearrange("p h t -> p (h t)"), kp,
                                        expnb[:, 2 * n:2 * n + 2, :].rearrange("p h t -> p (h t)"), ALU.mult)
                dve_done.by(nc.vector.tensor_tensor(
                    kend[:, 2 * n:2 * n + 2, :].rearrange("p h t -> p (h t)"), kp,
                    expe[:, 2 * n:2 * n + 2, :].rearrange("p h t -> p (h t)"), ALU.mult))
                freed[4 + n] = [(dve_done, dve_done.n)]
        for n in range(2):
            token_rows([6, 7], hT, 0, KT)
            for t in range(TT):
                copy_bank(6 + t, v[:, t, n * 512:n * 512 + 512])
        for n in range(4):
            b = n % 4
            feature_tile([b, b], hT, 0, SEQ)

            @block.scalar
            def _(act):
                act.wait_ge(tile_used.sem, tile_used.n)
                act_done.by(nc.scalar.activation(rT[:, 2 * n:2 * n + 2, :].rearrange("p h t -> p (h t)"),
                                                 ps[:, b, :], ACT.Silu))
                freed[b] = [(act_done, act_done.n)]

        @block.vector
        def _(dve):
            after_all(dve)
            def spread(e):
                return e.unsqueeze(2).to_broadcast([P, H1, CHUNK])
            link(dve, dve_done, nc.vector.tensor_tensor(e12, de[:, :, 1], de[:, :, 2], ALU.mult))
            nc.vector.tensor_tensor(q20, qdec[:, :, 128:192], spread(de[:, :, 1]), ALU.mult)
            nc.vector.tensor_tensor(q31, qdec[:, :, 192:256], spread(de[:, :, 2]), ALU.mult)
            nc.vector.tensor_tensor(q30, qdec[:, :, 192:256], spread(e12), ALU.mult)
            dve_done.by(nc.vector.memset(aT, 0.0))

        for hh in range(H1):
            b = 4 + hh

            @block.tensor
            def _(pe):
                after_all(pe) if hh == 0 else None
                for t in range(TT):
                    nc.tensor.matmul(ps[:, b, t * P:t * P + P], kinv[:, hh, t * P:t * P + P],
                                     qdec[:, hh, t * P:t * P + P], start=True, stop=True)
                ch = lambda x, n: x[:, hh, n * CHUNK:n * CHUNK + CHUNK]
                pairs = [(0, 256, ch(kend, 0), ch(qdec, 1)), (0, 320, ch(kend, 0), q20[:, hh, :]),
                         (0, 384, ch(kend, 0), q30[:, hh, :]), (64, 320, ch(kend, 1), ch(qdec, 2)),
                         (64, 384, ch(kend, 1), q31[:, hh, :]), (0, 448, ch(kend, 2), ch(qdec, 3))]
                for row, col, lhs, rhs in pairs:
                    last = nc.tensor.matmul(ps[row:row + 64, b, col:col + 64], lhs, rhs, start=True, stop=True)
                pe_done.by(last)

            @block.vector
            def _(dve):
                after_all(dve)
                for t in range(TT):
                    last = nc.vector.tensor_tensor(aT[:, hh, t, t * P:t * P + P], ps[:, b, t * P:t * P + P],
                                                   c("gla_mask"), ALU.mult)
                link(dve, dve_done, last)
                nc.vector.tensor_copy(aT[0:64, hh, 0, 64:256], ps[0:64, b, 256:448])
                nc.vector.tensor_copy(aT[64:128, hh, 0, 128:256], ps[64:128, b, 320:448])
                dve_done.by(nc.vector.tensor_copy(aT[0:64, hh, 1, 192:256], ps[0:64, b, 448:512]))

        @block.tensor
        def _(pe):
            after_all(pe)
            for hh in range(H1):
                for t in range(TT):
                    for j in range(t + 1):
                        last = nc.tensor.matmul(ps[:, 2 * t + hh // 2, (hh % 2) * DV1:(hh % 2) * DV1 + DV1],
                                                aT[:, hh, j, t * P:t * P + P], v[:, j, hh * DV1:hh * DV1 + DV1],
                                                start=(j == 0), stop=(j == t))
            pe_done.by(last)

        @block.scalar
        def _(act):
            after_all(act)
            for t in range(TT):
                for hh in range(H1):
                    link(act, act_done, nc.scalar.activation(
                        oo[:, t, hh * DV1:hh * DV1 + DV1],
                        ps[:, 2 * t + hh // 2, (hh % 2) * DV1:(hh % 2) * DV1 + DV1], ACT.Square,
                        accum_out=small[:, 8 + 4 * t + hh:9 + 4 * t + hh]))

        def rstd_of(cols, n):
            a, b_ = cols

            @block.vector
            def _(dve):
                after_all(dve)
                link(dve, dve_done, nc.vector.tensor_scalar(small[:, a:b_], small[:, a:b_], 1.0 / n, EPS,
                                                            ALU.mult, ALU.add))

            @block.gpsimd
            def _(pool):
                after_all(pool)
                inverse_root(pool, small[:, a + 16:b_ + 16], small[:, a:b_])

        rstd_of((8, 16), DV1)

        @block.vector
        def _(dve):
            after_all(dve)
            for t in range(TT):
                for hh in range(H1):
                    last = nc.vector.tensor_scalar(oo[:, t, hh * DV1:hh * DV1 + DV1],
                                                   ps[:, 2 * t + hh // 2, (hh % 2) * DV1:(hh % 2) * DV1 + DV1],
                                                   small[:, 24 + 4 * t + hh:25 + 4 * t + hh], None, ALU.mult)
            dve_done.by(last)

        yT = hT

        def transpose_rows(src, ntt, evac):
            for t in range(ntt):
                for q in range(2):
                    b = 4 + (2 * t + q) % 4

                    @block.tensor
                    def _(pe):
                        after_all(pe) if t == q == 0 else None
                        claim(pe, b)
                        for j in range(4):
                            last = nc.tensor.transpose(ps[:, b, j * P:j * P + P],
                                                       src[:, t, (4 * q + j) * P:(4 * q + j + 1) * P], ident)
                        pe_done.by(last)

                    @block.vector
                    def _(dve):
                        dve.wait_ge(pe_done.sem, pe_done.n)
                        for j in range(4):
                            last = evac(ps[:, b, j * P:j * P + P], 4 * q + j, t)
                        dve_done.by(last)
                        freed[b] = [(dve_done, dve_done.n)]

        transpose_rows(oo, TT, lambda part, k, t: nc.vector.scalar_tensor_tensor(
            yT[:, k, t * P:t * P + P], part, c("gla_head")[:, k % 2:k % 2 + 1], rT[:, k, t * P:t * P + P],
            ALU.mult, ALU.mult))

        def settle():
            @block.tensor
            def _(pe):
                after_all(pe)

        settle()
        for n in range(2):
            token_rows([2 * n, 2 * n + 1], yT, 0, KT)
            add_rows([2 * n, 2 * n + 1], lambda t: h[:, t, :], n)

        ffn_silu = sem("ffn_silu")
        ffn_act = sem("ffn_act")
        ffn_out = sem("ffn_out")
        ffn_gate = sem("ffn_gate")
        counts = {"silu": 0, "act": RING, "out": 0, "gate": 0, "conv": 0, "tap": 0, "scaled": 0}

        def feed_forward(nf, experts, gates, hid, sg, gcol, scr):
            t0 = tile_used.n
            kd = -(-nf // 4)
            per = nf + 2 * kd
            looped = nf // RING
            s0, a0, o0, g0 = counts["silu"], counts["act"], counts["out"], counts["gate"]
            slot = lambda k: (t0 + k) % RING
            many = experts > 1
            assert not many or per % RING == 0

            def loop(eng, n, body):
                if n == 1:
                    body(0)
                else:
                    with eng.Fori(0, n) as i:
                        body(i)

            def turns(eng, tile):
                def turn(g):
                    for s in range(RING):
                        tile(g, s)
                loop(eng, looped, turn)
                for s in range(nf - looped * RING):
                    tile(looped, s)

            @block.tensor
            def _(pe):
                after_all(pe)

                def expert(e):
                    def up(g, s):
                        w = ring[:, slot(s), :].rearrange("p (k n) -> p k n", k=KT)
                        pe.wait_ge(landed[slot(s)], (e * (per // RING) + g) * 16 + 16 * ((t0 + s) // RING + 1))
                        b = BANKS_PLAIN[s]
                        back = since(BANKS_PLAIN, s)
                        pe.wait_ge(ffn_act, e * nf + g * RING + (a0 + s - back + 1))
                        for half in range(2):
                            for k in range(KT):
                                last = nc.tensor.matmul(ps[:, b, half * SEQ:half * SEQ + SEQ],
                                                        w[:, k, half * P:half * P + P], hT[:, k, 0:SEQ],
                                                        start=(k == 0), stop=(k == KT - 1))
                        last.then_inc(tile_used.sem, 1)

                    turns(pe, up)
                    pe.wait_ge(ffn_act, e * nf + a0 + nf)
                    for half in range(2):
                        if many:
                            pe.wait_ge(ffn_out, e * 4 + o0)
                        for d in range(kd):
                            k = nf + half * kd + d
                            s = slot(k)
                            pe.wait_ge(landed[s], e * (per // RING) * 16 + 16 * ((t0 + k) // RING + 1))
                            w = ring[:, s, :].rearrange("p (k n) -> p k n", k=4)
                            for t in range(TT):
                                for j in range(min(4, nf - 4 * d)):
                                    last = nc.tensor.matmul(ps[:, 4 + 2 * half + t, :],
                                                            hid[:, 4 * d + j, t * P:t * P + P], w[:, j, :],
                                                            start=(d == j == 0), stop=(4 * d + j == nf - 1))
                            last.then_inc(tile_used.sem, 1)
                loop(pe, experts, expert)

            @block.scalar
            def _(act):
                after_all(act)

                def expert(e):
                    def gate(g, s):
                        f = g * RING + s
                        act.wait_ge(tile_used.sem, e * per + g * RING + (t0 + s + 1))
                        act.wait_ge(ffn_act, e * nf + g * RING + (a0 + s - RING + 1))
                        nc.scalar.activation(sg[:, s, :], ps[:, BANKS_PLAIN[s], 0:SEQ],
                                             ACT.Silu).then_inc(ffn_silu, 1)
                    turns(act, gate)
                loop(act, experts, expert)

            @block.vector
            def _(dve):
                after_all(dve)

                def expert(e):
                    def hidden(g, s):
                        dve.wait_ge(ffn_silu, e * nf + g * RING + (s0 + s + 1))
                        nc.vector.tensor_tensor(hid[:, g * RING + s, :], sg[:, s, :],
                                                ps[:, BANKS_PLAIN[s], SEQ:2 * SEQ], ALU.mult).then_inc(ffn_act, 1)
                    turns(dve, hidden)
                    if gates is not None:
                        dve.wait_ge(ffn_out, e * 4 + o0)
                        nc.vector.tensor_copy(gcol, gates[:, :, bass.ds(e, 1)]).then_inc(ffn_gate, 1)
                        dve.wait_ge(ffn_gate, e + (g0 + 1))
                    for half in range(2):
                        dve.wait_ge(tile_used.sem, e * per + (t0 + nf + (half + 1) * kd))
                        for t in range(TT):
                            hs = h[:, t, half * 512:half * 512 + 512]
                            o = ps[:, 4 + 2 * half + t, :]
                            if gates is None:
                                nc.vector.tensor_tensor(hs, hs, o, ALU.add).then_inc(ffn_out, 1)
                            else:
                                nc.vector.scalar_tensor_tensor(hs, o, gcol[:, t, :], hs, ALU.mult,
                                                               ALU.add).then_inc(ffn_out, 1)
                loop(dve, experts, expert)

            counts["silu"] += experts * nf
            counts["act"] += experts * nf
            counts["out"] += experts * 4
            counts["gate"] += experts if gates is not None else 0
            tile_used.n += experts * per

            @block.vector
            def _(dve):
                dve.wait_ge(ffn_out, counts["out"])
                dve_done.by(nc.vector.tensor_copy(small[:, 480:481], small[:, 481:482]))
            for b in range(8):
                freed[b] = [(dve_done, dve_done.n)]

        @block.vector
        def _(dve):
            dve_done.by(nc.vector.memset(small[:, 480:496], 0.0))
            dve.sem_inc(ffn_act, RING)

        reset()
        xs = take(TT, D)
        norm_T(h, [(hT, c("ffn0"), None)], 0, xs)
        reset()
        hid = take(F_MOE, SEQ)
        sg = take(RING, SEQ)
        feed_forward(F_FFN, 1, None, hid, sg, None, None)

        reset()
        xs = take(TT, D)
        hT2 = take(KT, SEQ)
        norm_T(h, [(hT, c("kvn"), None), (hT2, c("attn1"), None)], 0, xs)
        reset()
        xs = take(TT, D)
        hT2 = take(KT, SEQ)
        kT, qT = take(SBH, SEQ), take(SBH, SEQ)
        v = take(TT, D)
        zs, sp_, uu, wt = take(TT, SEQ), take(TT, SEQ), take(TT, SEQ), take(TT, SEQ)
        settle()
        for n in range(4):
            feature_tile([n, n], hT, 0, SEQ)
            copy_bank(n, kT[:, 2 * n:2 * n + 2, :].rearrange("p h t -> p (h t)"))
        for n in range(2):
            token_rows([4, 5], hT, 0, KT)
            for t in range(TT):
                copy_bank(4 + t, v[:, t, n * 512:n * 512 + 512])
        for n in range(4):
            feature_tile([n, n], hT2, 0, SEQ)
            copy_bank(n, qT[:, 2 * n:2 * n + 2, :].rearrange("p h t -> p (h t)"))
        for hh in range(SBH):
            @block.tensor
            def _(pe):
                after_all(pe)
                for j in range(TT):
                    last = nc.tensor.matmul(ps[:, 0, j * SEQ:j * SEQ + SEQ], kT[:, hh, j * P:j * P + P],
                                            qT[:, hh, :], start=True, stop=True)
                pe_done.by(last)

            @block.scalar
            def _(act):
                after_all(act)
                link(act, act_done, nc.scalar.activation(zs, ps[:, 0, :], ACT.Copy, scale=float(P) ** -0.5))
                link(act, act_done, nc.scalar.activation(uu, zs, ACT.Abs))
                link(act, act_done, nc.scalar.activation(uu, uu, ACT.Exp, scale=-1.0))
                link(act, act_done, nc.scalar.activation(uu, uu, ACT.Ln, bias=1.0))

            @block.vector
            def _(dve):
                after_all(dve)
                link(dve, dve_done, nc.vector.scalar_tensor_tensor(uu, zs, 0.0, uu, ALU.max, ALU.add))
                nc.vector.tensor_tensor(sp_.rearrange("p a b -> p (a b)"), uu.rearrange("p a b -> p (a b)"),
                                        c("sb_mask"), ALU.mult)
                dve_done.by(nc.vector.tensor_tensor(uu, zs, uu, ALU.subtract))

            @block.tensor
            def _(pe):
                after_all(pe)
                nc.tensor.matmul(ps[:, 1, 0:SEQ], c("sb_later"), sp_[:, 0, :], start=True, stop=False)
                nc.tensor.matmul(ps[:, 1, 0:SEQ], c("minus"), sp_[:, 1, :], start=False, stop=True)
                pe_done.by(nc.tensor.matmul(ps[:, 1, SEQ:2 * SEQ], c("sb_later"), sp_[:, 1, :],
                                            start=True, stop=True))

            @block.vector
            def _(dve):
                after_all(dve)
                dve_done.by(nc.vector.tensor_tensor(uu.rearrange("p a b -> p (a b)"),
                                                    uu.rearrange("p a b -> p (a b)"), ps[:, 1, :], ALU.add))

            @block.scalar
            def _(act):
                after_all(act)
                act_done.by(nc.scalar.activation(uu, uu, ACT.Exp))

            @block.vector
            def _(dve):
                after_all(dve)
                dve_done.by(nc.vector.tensor_tensor(wt.rearrange("p a b -> p (a b)"),
                                                    uu.rearrange("p a b -> p (a b)"), c("sb_mask"), ALU.mult))

            @block.tensor
            def _(pe):
                after_all(pe)
                for j in range(TT):
                    last = nc.tensor.matmul(ps[:, 2, 0:SEQ], v[:, j, hh * P:hh * P + P], wt[:, j, :],
                                            start=(j == 0), stop=(j == TT - 1))
                pe_done.by(last)
            copy_bank(2, hT[:, hh, 0:SEQ], slice(0, SEQ))

        settle()
        for n in range(2):
            token_rows([2 * n, 2 * n + 1], hT, 0, KT)
            add_rows([2 * n, 2 * n + 1], lambda t: h[:, t, :], n)

        reset()
        xs = take(TT, D)
        norm_T(h, [(hT, c("ffn1"), None)], 0, xs)
        reset()
        hid = take(F_MOE, SEQ)
        sg = take(RING, SEQ)
        lg = take(TT, EXPERTS)
        top = take(TT, 8)
        idx = arena[:, cur[0]:cur[0] + 16].bitcast(U32).rearrange("p (t n) -> p t n", t=TT)
        cur[0] += 16
        idf = take(TT, 8)
        wsel = take(TT, 4)
        sel = take(TT, EXPERTS)
        gates = take(TT, EXPERTS)
        gcol = take(TT, 1)

        @block.tensor
        def _(pe):
            after_all(pe)
            wr = c("router").rearrange("p (k n) -> p k n", k=KT)
            for t in range(TT):
                for k in range(KT):
                    last = nc.tensor.matmul(ps[:, 0, t * EXPERTS:(t + 1) * EXPERTS], hT[:, k, t * P:t * P + P],
                                            wr[:, k, :], start=(k == 0), stop=(k == KT - 1))
            pe_done.by(last)

        @block.vector
        def _(dve):
            after_all(dve)
            link(dve, dve_done, nc.vector.tensor_copy(lg.rearrange("p t n -> p (t n)"), ps[:, 0, 0:TT * EXPERTS]))
            for t in range(TT):
                link(dve, dve_done, nc.vector.max(top[:, t, :], lg[:, t, :]))
                link(dve, dve_done, nc.vector.max_index(idx[:, t, :], top[:, t, :], lg[:, t, :]))
            link(dve, dve_done, nc.vector.tensor_copy(idf, idx))
            link(dve, dve_done, nc.vector.tensor_tensor(wsel[:, :, 0], top[:, :, 1], top[:, :, 0], ALU.subtract))

        @block.scalar
        def _(act):
            after_all(act)
            act_done.by(nc.scalar.activation(wsel[:, :, 1], wsel[:, :, 0], ACT.Exp))

        @block.vector
        def _(dve):
            after_all(dve)
            link(dve, dve_done, nc.vector.tensor_scalar(wsel[:, :, 2], wsel[:, :, 1], 1.0, None, ALU.add))
            link(dve, dve_done, nc.vector.reciprocal(wsel[:, :, 2], wsel[:, :, 2]))
            link(dve, dve_done, nc.vector.tensor_tensor(wsel[:, :, 3], wsel[:, :, 1], wsel[:, :, 2], ALU.mult))
            for t in range(TT):
                link(dve, dve_done, nc.vector.tensor_scalar(gates[:, t, :], c("iota8"), idf[:, t, 0:1],
                                                            wsel[:, t, 2:3], ALU.is_equal, ALU.mult))
                link(dve, dve_done, nc.vector.tensor_scalar(sel[:, t, :], c("iota8"), idf[:, t, 1:2],
                                                            wsel[:, t, 3:4], ALU.is_equal, ALU.mult))
            link(dve, dve_done, nc.vector.tensor_tensor(gates, gates, sel, ALU.add))

        feed_forward(F_MOE, EXPERTS, gates, hid, sg, gcol, None)

        def final_norm(gain_row):
            @block.scalar
            def _(act):
                after_all(act)
                for t in range(TT):
                    link(act, act_done, nc.scalar.activation(arena[:, 0:D], h[:, t, :], ACT.Square,
                                                             accum_out=small[:, 8 + t:9 + t]))
            rstd_of((8, 10), D)

            @block.vector
            def _(dve):
                after_all(dve)
                for t in range(TT):
                    dve_done.by(nc.vector.scalar_tensor_tensor(h[:, t, :], h[:, t, :], small[:, 24 + t:25 + t],
                                                               gain_row, ALU.mult, ALU.mult))

        final_norm(c("final1"))

        mod = small[:, 64:64 + 64].rearrange("p (a k) -> p a k", k=KT)

        def modulation(layer, which, gain, streams=2):
            out_ = []

            @block.vector
            def _(dve):
                after_all(dve)
                for s in range(2):
                    shift = ada[:, layer, 24 * which:24 * which + 8, s]
                    scale = ada[:, layer, 24 * which + 8:24 * which + 16, s]
                    dst = mod[:, s, :]
                    link(dve, dve_done, nc.vector.tensor_copy(mod[:, 2 + s, :], shift))
                    link(dve, dve_done, nc.vector.scalar_tensor_tensor(dst, scale, 1.0, gain, ALU.add, ALU.mult))
                    out_.append((dst, mod[:, 2 + s, :]))
            return out_

        def gate_rows(layer, which, dst, streams=(0, 1)):
            diag = take(P)
            for s in streams:
                for k in range(KT):
                    @block.vector
                    def _(dve):
                        after_all(dve)
                        dve_done.by(nc.vector.tensor_scalar(
                            diag, ident, ada[:, layer, 24 * which + 16 + k:24 * which + 17 + k, s], None, ALU.mult))

                    @block.tensor
                    def _(pe):
                        after_all(pe)
                        pe_done.by(nc.tensor.matmul(ps[:, s, 0:P], ones, diag, start=True, stop=True))

                    @block.vector
                    def _(dve):
                        after_all(dve)
                        dve_done.by(nc.vector.tensor_copy(dst[:, s, k * P:k * P + P], ps[:, s, 0:P]))

        reset()
        xs = take(TT, D)
        (sc_l, sh_l), (sc_c, sh_c) = modulation(0, 0, c("norm1_0"))
        norm_T(cx, [(hT, sc_c, sh_c)], 0, xs)
        norm_T(h, [(hT, sc_l, sh_l)], SEQ, xs)

        reset()
        T4 = 4
        uT = take(4, 512)
        vn = take(T4, 512)
        qT, kT = take(GH, 512), take(GH, 512)
        kt, vt = take(T4, GH * P), take(T4, GH * P)
        gT = take(GH, 512)
        mark_gdn = cur[0]
        settle()
        for n in range(2):
            feature_tile([2 * n, 2 * n + 1], hT, 0, 512)
            for i in range(2):
                @block.scalar
                def _(act):
                    act.wait_ge(tile_used.sem, tile_used.n)
                    act_done.by(nc.scalar.activation(uT[:, 2 * n + i, :], ps[:, 2 * n + i, :], ACT.Gelu))
                    freed[2 * n + i] = [(act_done, act_done.n)]
        token_rows([4, 5, 6, 7], hT, 0, KT)
        for t in range(T4):
            @block.scalar
            def _(act):
                act.wait_ge(tile_used.sem, tile_used.n)
                act_done.by(nc.scalar.activation(vn[:, t, :], ps[:, 4 + t, :], ACT.Gelu,
                                                 accum_out=small[:, 8 + t:9 + t]))
                freed[4 + t] = [(act_done, act_done.n)]

        @block.vector
        def _(dve):
            after_all(dve)
            link(dve, dve_done, nc.vector.tensor_scalar(small[:, 12:16], small[:, 8:12], 1.0 / 512, None, ALU.mult))
            for t in range(T4):
                link(dve, dve_done, nc.vector.tensor_scalar(vn[:, t, :], vn[:, t, :], small[:, 12 + t:13 + t],
                                                            None, ALU.subtract))

        scratch512 = take(512)

        @block.scalar
        def _(act):
            after_all(act)
            for t in range(T4):
                link(act, act_done, nc.scalar.activation(scratch512, vn[:, t, :], ACT.Square,
                                                         accum_out=small[:, 8 + t:9 + t]))
        rstd_of((8, 12), 512)

        @block.vector
        def _(dve):
            after_all(dve)
            for t in range(T4):
                link(dve, dve_done, nc.vector.scalar_tensor_tensor(vn[:, t, :], vn[:, t, :], small[:, 24 + t:25 + t],
                                                                   c("ln_g"), ALU.mult, ALU.mult))
                link(dve, dve_done, nc.vector.tensor_tensor(vn[:, t, :], vn[:, t, :], c("ln_b"), ALU.add))

        reset(mark_gdn)
        cb = take(2, 512)
        for n in range(6):
            feature_tile([0, 1], hT, 0, 512)
            for i in range(2):
                ft = 2 * n + i
                tap = lambda j: c("conv_qkv")[:, j * 12 + ft:j * 12 + ft + 1]
                seg = lambda x, a, b_: x.rearrange("p (s t) -> p s t", s=2)[:, :, a:b_]
                src, dst = ps[:, i, :], cb[:, i, :]

                @block.scalar
                def _(act):
                    after_all(act)
                    act_done.by(nc.scalar.activation(dst, src, ACT.Copy, scale=tap(1)))

                @block.vector
                def _(dve):
                    after_all(dve)
                    link(dve, dve_done, nc.vector.scalar_tensor_tensor(
                        seg(dst, 1, SEQ), seg(src, 0, SEQ - 1), tap(0), seg(dst, 1, SEQ), ALU.mult, ALU.add))
                    dve_done.by(nc.vector.scalar_tensor_tensor(
                        seg(dst, 0, SEQ - 1), seg(src, 1, SEQ), tap(2), seg(dst, 0, SEQ - 1), ALU.mult, ALU.add))
                    freed[i] = [(dve_done, dve_done.n)]
                kind, hh = ft // 4, ft % 4
                full = (qT, kT, cb)[kind]
                fv = full[:, hh, :] if kind < 2 else dst

                @block.scalar
                def _(act):
                    after_all(act)
                    link(act, act_done, nc.scalar.activation(fv, dst, ACT.Silu))
                if kind < 2:
                    @block.scalar
                    def _(act):
                        after_all(act)
                        link(act, act_done, nc.scalar.activation(dst, fv, ACT.Square))

                    @block.tensor
                    def _(pe):
                        after_all(pe)
                        pe_done.by(nc.tensor.matmul(ps[:, 2, :], ones, dst, start=True, stop=True))

                    @block.vector
                    def _(dve):
                        after_all(dve)
                        link(dve, dve_done, nc.vector.tensor_scalar(dst, ps[:, 2, :], EPS, None, ALU.add))
                        link(dve, dve_done, nc.vector.reciprocal(dst, dst))

                    @block.scalar
                    def _(act):
                        after_all(act)
                        act_done.by(nc.scalar.activation(dst, dst, ACT.Sqrt))

                    @block.vector
                    def _(dve):
                        after_all(dve)
                        dve_done.by(nc.vector.scalar_tensor_tensor(
                            fv, fv, float(P) ** -0.5 if kind == 0 else 1.0, dst, ALU.mult, ALU.mult))
                if kind > 0:
                    row = (kt, vt)[kind - 1]

                    @block.tensor
                    def _(pe):
                        after_all(pe)
                        for t in range(T4):
                            last = nc.tensor.transpose(ps[:, 3, t * P:t * P + P], fv[:, t * P:t * P + P], ident)
                        pe_done.by(last)

                    @block.vector
                    def _(dve):
                        after_all(dve)
                        dve_done.by(nc.vector.tensor_copy(row[:, :, hh * P:hh * P + P],
                                                          ps[:, 3, :].rearrange("p (t n) -> p t n", t=T4)))
        for n in range(2):
            feature_tile([4 + 2 * n, 5 + 2 * n], hT, 0, 512)
            for i in range(2):
                @block.scalar
                def _(act):
                    act.wait_ge(tile_used.sem, tile_used.n)
                    act_done.by(nc.scalar.activation(gT[:, 2 * n + i, :], ps[:, 4 + 2 * n + i, :], ACT.Silu))
                    freed[4 + 2 * n + i] = [(act_done, act_done.n)]
        reset(mark_gdn)
        abv = take(T4, 16)
        lal, beta, t8 = take(T4, 8), take(T4, 8), take(T4, 8)

        @block.tensor
        def _(pe):
            after_all(pe)
            wab = c("w_ab").rearrange("p (k n) -> p k n", k=KT)
            for t in range(T4):
                for k in range(KT):
                    last = nc.tensor.matmul(ps[:, 0, t * 16:t * 16 + 16], hT[:, k, t * P:t * P + P], wab[:, k, :],
                                            start=(k == 0), stop=(k == KT - 1))
            pe_done.by(last)

        bc8 = lambda x: x.unsqueeze(1).to_broadcast([P, T4, 8])

        @block.vector
        def _(dve):
            after_all(dve)
            link(dve, dve_done, nc.vector.tensor_copy(abv.rearrange("p t n -> p (t n)"), ps[:, 0, 0:64]))
            link(dve, dve_done, nc.vector.tensor_tensor(lal, abv[:, :, 0:8], bc8(c("dt_bias")), ALU.add))

        @block.scalar
        def _(act):
            after_all(act)
            link(act, act_done, nc.scalar.activation(t8, lal, ACT.Abs))
            link(act, act_done, nc.scalar.activation(t8, t8, ACT.Exp, scale=-1.0))
            link(act, act_done, nc.scalar.activation(t8, t8, ACT.Ln, bias=1.0))
            link(act, act_done, nc.scalar.activation(c("a_log"), c("a_log"), ACT.Exp))
            link(act, act_done, nc.scalar.activation(beta, abv[:, :, 8:16], ACT.Exp, scale=-1.0))

        @block.vector
        def _(dve):
            after_all(dve)
            link(dve, dve_done, nc.vector.scalar_tensor_tensor(lal, lal, 0.0, t8, ALU.max, ALU.add))
            link(dve, dve_done, nc.vector.tensor_tensor(lal, lal, bc8(c("a_log")), ALU.mult))
            link(dve, dve_done, nc.vector.tensor_scalar(lal, lal, -1.0, None, ALU.mult))
            link(dve, dve_done, nc.vector.tensor_scalar(beta, beta, 1.0, None, ALU.add))
            link(dve, dve_done, nc.vector.reciprocal(beta, beta))

        yT = hT
        for g in range(4):
            @block.tensor
            def _(pe):
                after_all(pe)
                for t in range(T4):
                    last = nc.tensor.matmul(ps[:, 1, t * P:t * P + P], vn[:, t, g * P:g * P + P],
                                            c("ws", g * P, g * P + P), start=True, stop=True)
                pe_done.by(last)

            @block.vector
            def _(dve):
                after_all(dve)
                bsr = c("bs", g * P, g * P + P).unsqueeze(1).to_broadcast([P, T4, P])
                yg = yT[:, g, :].rearrange("p (t n) -> p t n", t=T4)
                link(dve, dve_done, nc.vector.tensor_tensor(yg, ps[:, 1, :].rearrange("p (t n) -> p t n", t=T4),
                                                            bsr, ALU.add))
                link(dve, dve_done, nc.vector.tensor_tensor(yT[:, g, :], yT[:, g, :], uT[:, g, :], ALU.mult))

        osum = vn
        W = GH * P
        vec4 = lambda x: x.unsqueeze(2).to_broadcast([P, GH, P])
        as4 = lambda x: x.rearrange("p (h n) -> p h n", h=GH)
        At, X, TM, UM, attn, qg, r_, kdec, beb = (take(W) for _ in range(9))
        S, lab, DT, eg = (hT[:, 4 + n, :] for n in range(4))
        vnew = beb
        gc, bg, ed, ge = take(GH), take(GH), take(GH), take(GH)
        for d in range(2):
            tri = c(f"tri{d}")
            strict = c(f"strict{d}")
            end = P - 1 if d == 0 else 0

            @block.vector
            def _(dve):
                after_all(dve)
                dve_done.by(nc.vector.memset(S, 0.0))
            for T in ((0, 1, 2, 3), (1, 0, 3, 2))[d]:
                tok = slice(T * P, T * P + P)
                la4 = lal[:, T, 4 * d:4 * d + 4]
                be4 = beta[:, T, 4 * d:4 * d + 4]

                @block.vector
                def _(dve):
                    after_all(dve)
                    nc.vector.tensor_copy(as4(lab), vec4(la4))
                    dve_done.by(nc.vector.tensor_copy(as4(beb), vec4(be4)))

                @block.tensor
                def _(pe):
                    after_all(pe)
                    for hh in range(GH):
                        hs = slice(hh * P, hh * P + P)
                        nc.tensor.matmul(ps[:, 0, hs], lab[:, hs], tri, start=True, stop=True)
                        nc.tensor.matmul(ps[:, 1, hs], beb[:, hs], ident, start=True, stop=True)
                        nc.tensor.matmul(ps[:, 2, hs], kT[:, hh, tok], kT[:, hh, tok], start=True, stop=True)
                        nc.tensor.matmul(ps[:, 3, hs], kT[:, hh, tok], qT[:, hh, tok], start=True, stop=True)
                    pe_done.by(nc.tensor.matmul(ps[:, 4, 0:GH], tri, la4, start=True, stop=True))

                @block.vector
                def _(dve):
                    after_all(dve)
                    link(dve, dve_done, nc.vector.tensor_copy(gc, ps[:, 4, 0:GH]))
                    for hh in range(GH):
                        hs = slice(hh * P, hh * P + P)
                        nc.vector.tensor_scalar(DT[:, hs], ps[:, 0, hs], gc[:, hh:hh + 1], 0.0,
                                                ALU.subtract, ALU.min)
                    dve_done.by(nc.vector.tensor_tensor(ed, as4(ps[:, 0, :])[:, :, end], gc, ALU.subtract))

                @block.scalar
                def _(act):
                    after_all(act)
                    link(act, act_done, nc.scalar.activation(DT, DT, ACT.Exp))
                    link(act, act_done, nc.scalar.activation(eg, ps[:, 0, :], ACT.Exp))
                    link(act, act_done, nc.scalar.activation(bg, gc, ACT.Exp))
                    link(act, act_done, nc.scalar.activation(ed, ed, ACT.Exp))
                    link(act, act_done, nc.scalar.activation(ge, as4(ps[:, 0, :])[:, :, end], ACT.Exp))

                b4 = lambda m: m.unsqueeze(1).to_broadcast([P, GH, P])

                @block.vector
                def _(dve):
                    after_all(dve)
                    link(dve, dve_done, nc.vector.tensor_tensor(as4(DT), as4(DT), b4(tri), ALU.mult))
                    link(dve, dve_done, nc.vector.tensor_tensor(attn, ps[:, 3, :], DT, ALU.mult))
                    link(dve, dve_done, nc.vector.tensor_tensor(At, ps[:, 2, :], DT, ALU.mult))
                    link(dve, dve_done, nc.vector.tensor_tensor(At, At, ps[:, 1, :], ALU.mult))
                    link(dve, dve_done, nc.vector.tensor_tensor(as4(At), as4(At), b4(strict), ALU.mult))
                    link(dve, dve_done, nc.vector.tensor_tensor(as4(qg), qT[:, :, tok], as4(eg), ALU.mult))
                    link(dve, dve_done, nc.vector.tensor_tensor(bg, bg, be4, ALU.mult))
                    link(dve, dve_done, nc.vector.tensor_tensor(as4(kdec), as4(kt[:, T, :]), vec4(ed), ALU.mult))
                    link(dve, dve_done, nc.vector.tensor_tensor(as4(X), as4(At), b4(c(f"lev{d}_0")), ALU.mult))
                    link(dve, dve_done, nc.vector.tensor_tensor(as4(UM), b4(ident), as4(X), ALU.subtract))

                @block.tensor
                def _(pe):
                    after_all(pe)
                    for hh in range(GH):
                        hs = slice(hh * P, hh * P + P)
                        last = nc.tensor.matmul(ps[:, 5, hs], X[:, hs], ident, start=True, stop=True)
                    pe_done.by(last)

                @block.vector
                def _(dve):
                    after_all(dve)
                    dve_done.by(nc.vector.tensor_tensor(as4(TM), b4(ident), as4(ps[:, 5, :]), ALU.subtract))

                for lev in range(1, 7):
                    @block.vector
                    def _(dve):
                        after_all(dve)
                        dve_done.by(nc.vector.tensor_tensor(as4(X), as4(At), b4(c(f"lev{d}_{lev}")), ALU.mult))

                    @block.tensor
                    def _(pe):
                        after_all(pe)
                        for hh in range(GH):
                            hs = slice(hh * P, hh * P + P)
                            last = nc.tensor.matmul(ps[:, 5, hs], X[:, hs], TM[:, hs], start=True, stop=True)
                        pe_done.by(last)

                    @block.scalar
                    def _(act):
                        after_all(act)
                        act_done.by(nc.scalar.activation(X, ps[:, 5, :], ACT.Copy))

                    @block.tensor
                    def _(pe):
                        after_all(pe)
                        for hh in range(GH):
                            hs = slice(hh * P, hh * P + P)
                            last = nc.tensor.matmul(ps[:, 6, hs], X[:, hs], UM[:, hs], start=True, stop=True)
                            if lev < 6:
                                last = nc.tensor.matmul(ps[:, 7, hs], UM[:, hs], X[:, hs], start=True, stop=True)
                        pe_done.by(last)

                    @block.vector
                    def _(dve):
                        after_all(dve)
                        dve_done.by(nc.vector.tensor_tensor(UM, UM, ps[:, 6, :], ALU.subtract))
                        if lev < 6:
                            dve_done.by(nc.vector.tensor_tensor(TM, TM, ps[:, 7, :], ALU.subtract))

                @block.tensor
                def _(pe):
                    after_all(pe)
                    for hh in range(GH):
                        hs = slice(hh * P, hh * P + P)
                        last = nc.tensor.matmul(ps[:, 0, hs], kT[:, hh, tok], S[:, hs], start=True, stop=True)
                    pe_done.by(last)

                @block.vector
                def _(dve):
                    after_all(dve)
                    link(dve, dve_done, nc.vector.tensor_tensor(as4(lab), as4(ps[:, 0, :]), vec4(bg), ALU.mult))
                    link(dve, dve_done, nc.vector.tensor_tensor(as4(r_), as4(vt[:, T, :]), vec4(be4), ALU.mult))
                    link(dve, dve_done, nc.vector.tensor_tensor(r_, r_, lab, ALU.subtract))

                @block.tensor
                def _(pe):
                    after_all(pe)
                    for hh in range(GH):
                        hs = slice(hh * P, hh * P + P)
                        last = nc.tensor.matmul(ps[:, 1, hs], UM[:, hs], r_[:, hs], start=True, stop=True)
                    pe_done.by(last)

                @block.scalar
                def _(act):
                    after_all(act)
                    act_done.by(nc.scalar.activation(vnew, ps[:, 1, :], ACT.Copy))

                @block.tensor
                def _(pe):
                    after_all(pe)
                    for hh in range(GH):
                        hs = slice(hh * P, hh * P + P)
                        nc.tensor.matmul(ps[:, 2, hs], qg[:, hs], S[:, hs], start=True, stop=False)
                        nc.tensor.matmul(ps[:, 2, hs], attn[:, hs], vnew[:, hs], start=False, stop=True)
                        last = nc.tensor.matmul(ps[:, 3, hs], kdec[:, hs], vnew[:, hs], start=True, stop=True)
                    pe_done.by(last)

                @block.vector
                def _(dve):
                    after_all(dve)
                    if d == 0:
                        dve_done.by(nc.vector.tensor_copy(osum[:, T, :], ps[:, 2, :]))
                    else:
                        dve_done.by(nc.vector.tensor_tensor(osum[:, T, :], osum[:, T, :], ps[:, 2, :], ALU.add))
                    link(dve, dve_done, nc.vector.tensor_tensor(as4(S), as4(S), vec4(ge), ALU.mult))
                    link(dve, dve_done, nc.vector.tensor_tensor(S, S, ps[:, 3, :], ALU.add))

        @block.scalar
        def _(act):
            after_all(act)
            for t in range(T4):
                for hh in range(GH):
                    link(act, act_done, nc.scalar.activation(X[:, 0:P], osum[:, t, hh * P:hh * P + P], ACT.Square,
                                                             accum_out=small[:, 8 + 4 * t + hh:9 + 4 * t + hh]))

        @block.vector
        def _(dve):
            after_all(dve)
            link(dve, dve_done, nc.vector.tensor_scalar(small[:, 24:40], small[:, 8:24], 1.0 / P, EPS,
                                                        ALU.mult, ALU.add))

        @block.gpsimd
        def _(pool):
            after_all(pool)
            inverse_root(pool, small[:, 8:24], small[:, 24:40])

        @block.vector
        def _(dve):
            after_all(dve)
            for t in range(T4):
                ins = nc.vector.tensor_tensor(as4(osum[:, t, :]), as4(osum[:, t, :]),
                                              vec4(small[:, 8 + 4 * t:12 + 4 * t]), ALU.mult)
            dve_done.by(ins)
        for hh in range(GH):
            @block.tensor
            def _(pe):
                after_all(pe)
                for t in range(T4):
                    last = nc.tensor.transpose(ps[:, hh, t * P:t * P + P], osum[:, t, hh * P:hh * P + P], ident)
                pe_done.by(last)

            @block.vector
            def _(dve):
                after_all(dve)
                dve_done.by(nc.vector.scalar_tensor_tensor(yT[:, 4 + hh, :], ps[:, hh, :], c("b_norm"),
                                                           gT[:, hh, :], ALU.mult, ALU.mult))

        def gated_out(layer, which, src, ntt, kt_):
            rows = take(2, D)
            scr = take(4, 512)
            gate_rows(layer, which, rows, (0, 1) if ntt == 4 else (0,))
            settle()
            strm = (lambda t: (cx if t < 2 else h)[:, t % 2, :]) if ntt == 4 else (lambda t: h[:, t, :])
            gt = (lambda t: rows[:, 1 if t < 2 else 0, :]) if ntt == 4 else (lambda t: rows[:, 0, :])
            for n in range(2):
                banks = [(4 * n + i) for i in range(ntt)]
                token_rows(banks, src, 0, kt_)
                add_rows(banks, strm, n, gt, scr)

        reset()
        gated_out(0, 0, yT, 4, KT)

        conv_centre = sem("conv_centre")
        conv_side = sem("conv_side")
        conv_silu = sem("conv_silu")
        conv_hid = sem("conv_hid")
        conv_left = sem("conv_left")
        cc = {"n": 0}

        @block.vector
        def _(dve):
            dve.sem_inc(conv_side, 2 * RING)
            dve.sem_inc(conv_hid, RING)

        def conv_feed_forward(layer, ntok):
            nf = F_FFN
            segs = ntok // SEQ
            hid = take(nf, ntok)
            cg, cu = take(3, ntok), take(3, ntok)
            t0, c0 = tile_used.n, cc["n"]
            slot = lambda k: (t0 + k) % RING
            looped = nf // RING
            wofs = where["conv_ffn"][0] + layer * 3 * 2 * nf
            tap = lambda j, half, g, s: par[:, bass.ds(g * RING + (wofs + (j * 2 + half) * nf + s), 1)]
            seg = lambda x, a, b_: x.rearrange("p (s t) -> p s t", s=segs)[:, :, a:b_]

            def turns(eng, tile):
                with eng.Fori(0, looped) as g:
                    for s in range(RING):
                        tile(g, s)
                for s in range(nf - looped * RING):
                    tile(looped, s)

            @block.tensor
            def _(pe):
                after_all(pe)

                def up(g, s):
                    pe.wait_ge(landed[slot(s)], g * 16 + 16 * ((t0 + s) // RING + 1))
                    w = ring[:, slot(s), :].rearrange("p (k n) -> p k n", k=KT)
                    pe.wait_ge(conv_side, g * (2 * RING) + 2 * (RING + c0 + s - since(BANKS_CONV, s) + 1))
                    for half in range(2):
                        for k in range(KT):
                            last = nc.tensor.matmul(ps[:, 2 * BANKS_CONV[s] + half, 0:ntok],
                                                    w[:, k, half * P:half * P + P], hT[:, k, 0:ntok],
                                                    start=(k == 0), stop=(k == KT - 1))
                    last.then_inc(tile_used.sem, 1)
                turns(pe, up)

            @block.scalar
            def _(act):
                after_all(act)

                def gate(g, s):
                    b = BANKS_CONV[s]
                    act.wait_ge(tile_used.sem, g * RING + (t0 + s + 1))
                    act.wait_ge(conv_hid, g * RING + (RING + c0 + s - since(BANKS_CONV, s) + 1))
                    for half, buf in enumerate((cg, cu)):
                        nc.scalar.activation(buf[:, b, :], ps[:, 2 * b + half, 0:ntok], ACT.Copy,
                                             scale=tap(1, half, g, s)).then_inc(conv_centre, 1)
                    act.wait_ge(conv_side, g * (2 * RING) + 2 * (RING + c0 + s + 1))
                    nc.scalar.activation(cg[:, b, :], cg[:, b, :], ACT.Silu).then_inc(conv_silu, 1)
                turns(act, gate)

            @block.vector
            def _(dve):
                after_all(dve)

                def hidden(g, s):
                    b = BANKS_CONV[s]
                    dve.wait_ge(conv_centre, g * (2 * RING) + 2 * (c0 + s + 1))
                    for half, buf in enumerate((cg, cu)):
                        x, o = ps[:, 2 * b + half, 0:ntok], buf[:, b, :]
                        nc.vector.scalar_tensor_tensor(seg(o, 1, SEQ), seg(x, 0, SEQ - 1), tap(0, half, g, s),
                                                       seg(o, 1, SEQ), ALU.mult, ALU.add).then_inc(conv_left, 1)
                    dve.wait_ge(conv_left, g * (2 * RING) + 2 * (c0 + s + 1))
                    for half, buf in enumerate((cg, cu)):
                        x, o = ps[:, 2 * b + half, 0:ntok], buf[:, b, :]
                        nc.vector.scalar_tensor_tensor(seg(o, 0, SEQ - 1), seg(x, 1, SEQ), tap(2, half, g, s),
                                                       seg(o, 0, SEQ - 1), ALU.mult, ALU.add).then_inc(conv_side, 1)
                    dve.wait_ge(conv_side, g * (2 * RING) + 2 * (RING + c0 + s + 1))
                    dve.wait_ge(conv_silu, g * RING + (c0 + s + 1))
                    nc.vector.tensor_tensor(hid[:, g * RING + s, :], cg[:, b, :], cu[:, b, :],
                                            ALU.mult).then_inc(conv_hid, 1)
                turns(dve, hidden)
                dve.wait_ge(conv_hid, RING + c0 + nf)
                dve_done.by(nc.vector.tensor_copy(small[:, 480:481], small[:, 481:482]))
            tile_used.n += nf
            cc["n"] += nf
            for b in range(8):
                freed[b] = [(dve_done, dve_done.n)]
            return hid

        def second_ffn(layer, both):
            nonlocal hT
            reset()
            xs = take(TT, D)
            (sc_l, sh_l), (sc_c, sh_c) = modulation(layer, 1, c(f"norm2_{layer}"))
            if both:
                norm_T(cx, [(hT, sc_c, sh_c)], 0, xs)
            norm_T(h, [(hT, sc_l, sh_l)], SEQ if both else 0, xs)
            reset()
            hid = conv_feed_forward(layer, 512 if both else 256)
            gated_out(layer, 1, hid, 4 if both else 2, F_FFN)

        second_ffn(0, True)

        reset()
        xs = take(TT, D)
        (sc_l, sh_l), (sc_c, sh_c) = modulation(1, 0, c("norm1_1"))
        norm_T(cx, [(hT, sc_c, sh_c)], 0, xs)
        norm_T(h, [(hT, sc_l, sh_l)], SEQ, xs)
        reset()
        zkv = take(T4, 320)
        zq = take(TT, 384)
        kr2 = take(T4, P)
        ckvT = take(2, 512)
        krT = take(512)
        cqT = take(3, SEQ)
        settle()
        token_rows([0, 1, 2, 3], hT, 0, KT, cols=320)
        for t in range(T4):
            copy_bank(t, zkv[:, t, :], slice(0, 320))
        token_rows([4, 5], hT, SEQ, KT, cols=384)
        for t in range(TT):
            copy_bank(4 + t, zq[:, t, :], slice(0, 384))

        mark = cur[0]
        sq = take(384)

        @block.scalar
        def _(act):
            after_all(act)
            for t in range(T4):
                link(act, act_done, nc.scalar.activation(sq[:, 0:256], zkv[:, t, 0:256], ACT.Square,
                                                         accum_out=small[:, 8 + t:9 + t]))
            for t in range(TT):
                link(act, act_done, nc.scalar.activation(sq, zq[:, t, :], ACT.Square,
                                                         accum_out=small[:, 12 + t:13 + t]))
        rstd_of((8, 12), 256)
        rstd_of((12, 14), 384)

        def rotate(dve, dst, src, t, n, a_, b_):
            cos = c("cos", 32 * t, 32 * t + 32).unsqueeze(1).to_broadcast([P, n, 32])
            sin = c("sin", 32 * t, 32 * t + 32).unsqueeze(1).to_broadcast([P, n, 32])
            x1, x2 = src[:, :, 0:32], src[:, :, 32:64]
            nc.vector.tensor_tensor(a_, x1, cos, ALU.mult)
            link(dve, dve_done, nc.vector.tensor_tensor(b_, x2, sin, ALU.mult))
            link(dve, dve_done, nc.vector.tensor_tensor(dst[:, :, 0:32], a_, b_, ALU.subtract))
            nc.vector.tensor_tensor(a_, x2, cos, ALU.mult)
            link(dve, dve_done, nc.vector.tensor_tensor(b_, x1, sin, ALU.mult))
            link(dve, dve_done, nc.vector.tensor_tensor(dst[:, :, 32:64], a_, b_, ALU.add))

        ra, rb = take(8, 32), take(8, 32)

        @block.vector
        def _(dve):
            after_all(dve)
            for t in range(T4):
                link(dve, dve_done, nc.vector.tensor_scalar(zkv[:, t, 0:256], zkv[:, t, 0:256],
                                                            small[:, 24 + t:25 + t], None, ALU.mult))
                kr = zkv[:, t, 256:320].unsqueeze(1)
                if t < 2:
                    link(dve, dve_done, nc.vector.tensor_copy(kr2[:, t, 0:64], zkv[:, t, 256:320]))
                else:
                    rotate(dve, kr2[:, t, 0:64].unsqueeze(1), kr, t - 2, 1, ra[:, 0:1, :], rb[:, 0:1, :])
                link(dve, dve_done, nc.vector.tensor_copy(kr2[:, t, 64:128], kr2[:, t, 0:64]))
            for t in range(TT):
                link(dve, dve_done, nc.vector.tensor_scalar(zq[:, t, :], zq[:, t, :],
                                                            small[:, 28 + t:29 + t], None, ALU.mult))

        @block.tensor
        def _(pe):
            after_all(pe)
            for t in range(T4):
                for k in range(2):
                    nc.tensor.transpose(ps[:, k, t * P:t * P + P], zkv[:, t, k * P:k * P + P], ident)
                last = nc.tensor.transpose(ps[:, 2, t * P:t * P + P], kr2[:, t, :], ident)
            for t in range(TT):
                for k in range(3):
                    last = nc.tensor.transpose(ps[:, 3 + k, t * P:t * P + P], zq[:, t, k * P:k * P + P], ident)
            pe_done.by(last)

        @block.vector
        def _(dve):
            after_all(dve)
            for k in range(2):
                nc.vector.tensor_scalar(ckvT[:, k, :], ps[:, k, :], c("kv_n")[:, k:k + 1], None, ALU.mult)
            nc.vector.tensor_copy(krT, ps[:, 2, :])
            for k in range(3):
                last = nc.vector.tensor_scalar(cqT[:, k, :], ps[:, 3 + k, 0:SEQ], c("q_n")[:, k:k + 1], None,
                                               ALU.mult)
            dve_done.by(last)

        reset(mark)
        qnT = take(MH, SEQ)
        qr = take(TT, 512)
        qrT = take(4, SEQ)
        ra, rb = take(8, 32), take(8, 32)
        knT = hT.rearrange("p k t -> p (k t)").rearrange("p (h t) -> p h t", h=MH)
        v = take(T4, D)
        pp = take(512)
        pT = take(4, SEQ)
        oT = take(MH, SEQ)
        settle()
        for n in range(2):
            @block.tensor
            def _(pe):
                w = weights(pe).rearrange("p (k n) -> p k n", k=4)
                claim(pe, 6, 7)
                for i in range(4):
                    for k in range(3):
                        last = nc.tensor.matmul(ps[:, 6 + i // 2, (i % 2) * SEQ:(i % 2) * SEQ + SEQ],
                                                w[:, k, i * P:i * P + P], cqT[:, k, :],
                                                start=(k == 0), stop=(k == 2))
                tile_used.by(last)
            for i in range(2):
                copy_bank(6 + i, qnT[:, 4 * n + 2 * i:4 * n + 2 * i + 2, :].rearrange("p h t -> p (h t)"))
        token_rows([0, 1], cqT, 0, 3)

        @block.vector
        def _(dve):
            after_all(dve)
            for t in range(TT):
                rotate(dve, qr[:, t, :].rearrange("p (h n) -> p h n", h=8),
                       ps[:, t, :].rearrange("p (h n) -> p h n", h=8), t, 8, ra, rb)

        @block.tensor
        def _(pe):
            after_all(pe)
            for k in range(4):
                for t in range(TT):
                    last = nc.tensor.transpose(ps[:, 2 + k // 2, (k % 2) * SEQ + t * P:(k % 2) * SEQ + t * P + P],
                                               qr[:, t, k * P:k * P + P], ident)
            pe_done.by(last)

        @block.vector
        def _(dve):
            after_all(dve)
            dve_done.by(nc.vector.tensor_copy(qrT.rearrange("p k t -> p (k t)"), ps[:, 2:4, :]))
        settle()

        @block.tensor
        def _(pe):
            w = weights(pe).rearrange("p (k n) -> p k n", k=2)
            for i in range(MH):
                for k in range(2):
                    last = nc.tensor.matmul(ps[:, i, :], w[:, k, i * P:i * P + P], ckvT[:, k, :],
                                            start=(k == 0), stop=(k == 1))
            tile_used.by(last)
        for i in range(MH):
            copy_bank(i, knT[:, i, :])

        @block.tensor
        def _(pe):
            w = weights(pe).rearrange("p (k n) -> p k n", k=2)
            claim(pe, *range(8))
            for t in range(T4):
                for n in range(2):
                    for k in range(2):
                        last = nc.tensor.matmul(ps[:, 2 * t + n, :], ckvT[:, k, t * P:t * P + P],
                                                w[:, k, n * 512:n * 512 + 512], start=(k == 0), stop=(k == 1))
            tile_used.by(last)
        for t in range(T4):
            for n in range(2):
                copy_bank(2 * t + n, v[:, t, n * 512:n * 512 + 512])
        scale = float(128 + 64) ** -0.5
        for hh in range(MH):
            ro = 64 * (hh % 2)
            for t in range(TT):
                @block.tensor
                def _(pe):
                    after_all(pe)
                    nc.tensor.matmul(ps[:, t, :], qnT[:, hh, t * P:t * P + P], knT[:, hh, :], start=True, stop=False)
                    pe_done.by(nc.tensor.matmul(ps[:, t, :], qrT[ro:ro + 64, hh // 2, t * P:t * P + P],
                                                krT[ro:ro + 64, :], start=False, stop=True))

                @block.vector
                def _(dve):
                    after_all(dve)
                    link(dve, dve_done, nc.vector.reduce_max(small[:, 40:41], ps[:, t, :], AXX))
                    link(dve, dve_done, nc.vector.tensor_scalar(small[:, 41:42], small[:, 40:41], -scale, None,
                                                                ALU.mult))

                @block.scalar
                def _(act):
                    after_all(act)
                    act_done.by(nc.scalar.activation(pp, ps[:, t, :], ACT.Exp, bias=small[:, 41:42], scale=scale,
                                                     accum_out=small[:, 42:43]))

                @block.vector
                def _(dve):
                    after_all(dve)
                    link(dve, dve_done, nc.vector.reciprocal(small[:, 43:44], small[:, 42:43]))
                    link(dve, dve_done, nc.vector.tensor_scalar(pp, pp, small[:, 43:44], None, ALU.mult))

                @block.tensor
                def _(pe):
                    after_all(pe)
                    for j in range(T4):
                        last = nc.tensor.transpose(ps[:, 2, j * P:j * P + P], pp[:, j * P:j * P + P], ident)
                    pe_done.by(last)

                @block.vector
                def _(dve):
                    after_all(dve)
                    dve_done.by(nc.vector.tensor_copy(pT[:, :, t * P:t * P + P],
                                                      ps[:, 2, :].rearrange("p (j n) -> p j n", j=T4)))

            @block.tensor
            def _(pe):
                after_all(pe)
                for j in range(T4):
                    last = nc.tensor.matmul(ps[:, 3, 0:SEQ], v[:, j, hh * P:hh * P + P], pT[:, j, :],
                                            start=(j == 0), stop=(j == T4 - 1))
                pe_done.by(last)

            @block.vector
            def _(dve):
                after_all(dve)
                dve_done.by(nc.vector.tensor_copy(oT[:, hh, :], ps[:, 3, 0:SEQ]))

        @block.vector
        def _(dve):
            after_all(dve)
            dve_done.by(nc.vector.tensor_copy(hT[:, :, 0:SEQ], oT))
        reset()
        for eng in (block.vector, block.tensor):
            @eng
            def _(e):
                after_all(e)
        gated_out(1, 0, hT, 2, KT)
        second_ffn(1, False)
        final_norm(c("final2"))
        assert tile_used.n == n_tiles, (tile_used.n, n_tiles)

        @block.sync
        def _(sp):
            sp.wait_ge(dve_done.sem, dve_done.n)
            for t in range(TT):
                sp.dma_start(out["out"][t * P:t * P + P, :], h[:, t, :]).then_inc(stored, 16)
            sp.wait_ge(stored, 16 * TT)




def weight_stream(i):
    tiles = []

    def features(w, *firsts):
        w8 = w.reshape(KT, P, -1)
        t = np.stack([w8[:, :, f:f + P] for f in firsts], axis=2)
        tiles.append(t.transpose(1, 0, 2, 3).reshape(P, TILE))

    def rows(w, col, cols=512, kper=4):
        k = w.shape[0] // P
        wide = TILE // kper
        wk = w.reshape(k, P, -1)[:, :, col:col + cols]
        for k0 in range(0, k, kper):
            t = np.zeros((kper, P, wide), np.float32)
            part = wk[k0:k0 + kper]
            t[:part.shape[0], :, :part.shape[2]] = part
            tiles.append(t.transpose(1, 0, 2).reshape(P, TILE))

    def span(w, a, b):
        for n in range(a, b, 2 * P):
            features(w, n, n + P)

    def both_halves(w):
        rows(w, 0)
        rows(w, 512)

    for layer in range(2):
        span(i["ada_w_2"][layer], 0, 6 * D)
    w = i["gla_w_in"][0]
    span(w, 0, 1024)
    rows(w, 1024), rows(w, 1536)
    span(w, 2064, 3088)
    both_halves(i["gla_w_out"][0])
    g, u = i["ffn_w_gate"][0], i["ffn_w_up"][0]
    gu = np.concatenate([g, u], axis=1)
    for f in range(F_FFN):
        features(gu, f * P, FF + f * P)
    both_halves(i["ffn_w_down"][0])
    span(i["sb_w_kv"], 0, 1024)
    rows(i["sb_w_kv"], 1024), rows(i["sb_w_kv"], 1536)
    span(i["sb_w_q"][0], 0, 1024)
    both_halves(i["sb_w_out"][0])
    for e in range(EXPERTS):
        gu = np.concatenate([i["moe_w_gate"][0, e], i["moe_w_up"][0, e]], axis=1)
        for f in range(F_MOE):
            features(gu, f * P, F_MOE * P + f * P)
        both_halves(i["moe_w_down"][0, e])
    w = i["ab_w_in_2"][0]
    span(w, 0, 512)
    rows(w, 512)
    span(w, 1024, 2560)
    span(w, 2560, 3072)
    both_halves(i["ab_w_out_2"][0])

    def conv_ffn(layer):
        for f in range(F_FFN):
            features(i["ffn_w_up_2"][layer], f * P, FF + f * P)
        both_halves(i["ffn_w_down_2"][layer])

    conv_ffn(0)
    w = i["mla_w_in_2"][0]
    rows(w, 384, 320)
    rows(w, 0, 384)
    uq = i["mla_w_uq_2"][0].reshape(384, MH, 192)
    nope = uq[:, :, 0:128].reshape(384, MH * 128)
    rows(nope, 0), rows(nope, 512)
    rows(uq[:, :, 128:192].reshape(384, MH * 64), 0)
    ukv = i["mla_w_ukv_2"][0].reshape(256, MH, 256)
    rows(ukv[:, :, 0:128].reshape(256, D), 0, D, 2)
    rows(ukv[:, :, 128:256].reshape(256, D), 0, D, 2)
    both_halves(i["mla_w_out_2"][0])
    conv_ffn(1)
    return np.stack(tiles)


def parameters(i):
    out = {}
    f32 = np.float32

    def col(v):
        return v.reshape(-1, P).T

    def rep(v):
        return np.broadcast_to(v.reshape(1, -1), (P, v.size))

    def padded(a):
        z = np.zeros((P, a.shape[1]), f32)
        z[:a.shape[0]] = a
        return z

    def ktiles(w):
        return w.reshape(KT, P, -1).transpose(1, 0, 2).reshape(P, -1)

    r = np.arange(P)
    out["ident"] = np.eye(P, dtype=f32)
    out["ones"] = np.ones((P, P), f32)
    out["minus"] = -np.ones((P, P), f32)
    out["attn0"], out["attn1"] = col(i["attn_norm"][0]), col(i["attn_norm"][1])
    out["ffn0"], out["ffn1"] = col(i["ffn_norm"][0]), col(i["ffn_norm"][1])
    out["kvn"] = col(i["kv_norm"])
    for layer in range(2):
        out[f"norm1_{layer}"] = col(i["norm1_g_2"][layer])
        out[f"norm2_{layer}"] = col(i["norm2_g_2"][layer])
    out["gla_head"] = col(i["gla_head_norm"][0])
    out["b_norm"] = col(i["b_norm_g_2"][0])
    out["q_n"], out["kv_n"] = col(i["mla_q_norm_g_2"][0]), col(i["mla_kv_norm_g_2"][0])
    b = i["ada_b_2"].reshape(2 * 48, P).T
    out["ada_b"] = np.repeat(b, 2, axis=1)
    out["cond"] = np.stack([i["c_2"][0], i["c_ctx_2"]], axis=1).reshape(KT, P, 2).transpose(1, 0, 2).reshape(P, -1)
    out["w_glr"] = ktiles(i["gla_w_in"][0][:, 2048:2064])
    out["gate_up"] = padded(i["gla_w_gate_up"][0])
    out["gate_b"] = padded(i["gla_b_gate"])
    same = (r[:, None] // CHUNK) == (r[None, :] // CHUNK)
    out["gla_mask"] = (same & (r[:, None] <= r[None, :])).astype(f32)
    out["gla_sum"] = out["gla_mask"] / f32(16)
    out["router"] = ktiles(i["moe_w_router"][0])
    out["iota8"] = rep(np.arange(8, dtype=f32))
    t = np.arange(SEQ)
    out["sb_mask"] = np.concatenate([(r[:, None] + P * j < t[None, :]) for j in range(TT)], axis=1).astype(f32)
    out["sb_later"] = -(r[:, None] > r[None, :]).astype(f32)
    out["w_ab"] = ktiles(i["ab_w_in_2"][0][:, 3072:3088])
    out["ln_g"], out["ln_b"] = rep(i["a_ln_g_2"][0]), rep(i["a_ln_b_2"][0])
    out["ws"] = i["a_ws_2"][0].transpose(2, 0, 1).reshape(P, -1)
    out["bs"] = rep(i["a_bs_2"][0])
    out["conv_qkv"] = i["b_conv_w_2"][0].reshape(3 * 12, P).T
    out["conv_ffn"] = i["ffn_conv_w_2"].reshape(2 * 3 * 2 * F_FFN, P).T
    out["a_log"], out["dt_bias"] = rep(i["b_a_log_2"][0]), rep(i["b_dt_bias_2"][0])
    out["final1"], out["final2"] = rep(i["final_norm"]), rep(i["final_g_2"])
    j, k = r[:, None], r[None, :]
    for d in range(2):
        before = (j < k) if d == 0 else (j > k)
        out[f"tri{d}"] = (before | (j == k)).astype(f32)
        out[f"strict{d}"] = before.astype(f32)
        for lev in range(7):
            s = 1 << lev
            out[f"lev{d}_{lev}"] = (before & (j // (2 * s) == k // (2 * s)) & (j // s != k // s)).astype(f32)
    rows_, grid = SEQ // 64, 64
    row = np.repeat(np.arange(rows_, dtype=f32), grid)
    colv = np.tile(np.arange(grid, dtype=f32), rows_)
    inv = (f32(10000.0) ** (-np.arange(16, dtype=f32) / f32(16))).astype(f32)
    ang = np.concatenate([row[:, None] * inv, colv[:, None] * inv], axis=-1)
    out["cos"] = np.cos(ang).astype(f32).reshape(TT, P, 32).transpose(1, 0, 2).reshape(P, -1)
    out["sin"] = np.sin(ang).astype(f32).reshape(TT, P, 32).transpose(1, 0, 2).reshape(P, -1)
    where, at = {}, 0
    for name, a in out.items():
        where[name] = (at, a.shape[1])
        at += a.shape[1]
    return np.concatenate(list(out.values()), axis=1).astype(f32), where


def kernel(**inputs):
    import concourse.bacc as _bacc
    from concourse.bass_utils import run_bass_kernel_spmd as _run

    i = {k: np.asarray(v) for k, v in inputs.items()}
    par, where = parameters(i)
    arrays = {
        "in_stream": weight_stream(i),
        "in_params": np.ascontiguousarray(par),
        "in_x": np.ascontiguousarray(i["x"][0]),
        "in_ctx": np.ascontiguousarray(i["ctx_2"][0]),
    }
    nc = _bacc.Bacc("TRN2", target_bir_lowering=False, num_devices=1)
    aps = {n: nc.dram_tensor(n, a.shape, F32, kind="ExternalInput").ap() for n, a in arrays.items()}
    out = nc.dram_tensor("out_0", (SEQ, D), F32, kind="ExternalOutput").ap()
    build(nc, aps["in_stream"], aps["in_params"], where,
          {"x": aps["in_x"], "ctx": aps["in_ctx"], "out": out})
    r = _run(nc, [arrays], core_ids=[0])
    return r.results[0]["out_0"].reshape(1, SEQ, D)
```

```python
from contextlib import ExitStack

import numpy as np

import concourse.bass as bass
from concourse import mybir

F32 = mybir.dt.float32
U32 = mybir.dt.uint32
ALU = mybir.AluOpType
ACT = mybir.ActivationFunctionType
AXX = mybir.AxisListType.X

P = 128
D = 1024
KT = D // P
SEQ = 256
TT = SEQ // P
TILE = 2048
RING = 7
CHUNK = 64
H1, DV1 = 4, 256
SBH = 8
EXPERTS = 8
F_MOE = 3584 // P
F_FFN = 2816 // P
FF = 2816
EPS = 1e-6
CAP = P
GH = 4
MH = 8
BANKS_PLAIN = [0, 1, 2, 3, 0, 1, 2]
BANKS_CONV = [0, 1, 2, 0, 1, 2, 1]


def since(pattern, s):
    n = len(pattern)
    return next(d for d in range(1, n + 1) if pattern[(s - d) % n] == pattern[s])


class Done:

    def __init__(self, sem):
        self.sem, self.n = sem, 0

    def by(self, ins):
        ins.then_inc(self.sem, 1)
        self.n += 1
        return self.n


def build(nc, stream, params, where, out):
    n_tiles = stream.shape[0]
    width = params.shape[1]
    with ExitStack() as ctx:
        def sb(name, shape, dt=F32):
            return ctx.enter_context(nc.sbuf_tensor(name, shape, dt))

        def sem(name):
            return ctx.enter_context(nc.semaphore(name))

        ring = sb("ring", [P, RING, TILE])
        par = sb("par", [P, width])
        h = sb("h", [P, TT, D])
        cx = sb("cx", [P, TT, D])
        hT = sb("hT", [P, KT, 2 * SEQ])
        ARENA = 19968
        arena = sb("arena", [P, ARENA])
        ada = sb("ada", [P, 2, 48, 2])
        small = sb("small", [P, 512])
        ps = ctx.enter_context(nc.psum_tensor("ps", [P, 8, 512], F32))

        landed = [sem(f"landed{i}") for i in range(RING)]
        params_in = sem("params_in")
        x_in = sem("x_in")
        stored = sem("stored")
        tile_used = Done(sem("tile_used"))
        pe_done = Done(sem("pe_done"))
        act_done = Done(sem("act_done"))
        dve_done = Done(sem("dve_done"))
        pool_done = Done(sem("pool_done"))
        everyone = (tile_used, pe_done, act_done, dve_done, pool_done)

        def after_all(eng):
            for d in everyone:
                if d.n:
                    eng.wait_ge(d.sem, d.n)

        def link(eng, done, ins):
            eng.wait_ge(done.sem, done.by(ins))

        def c(name, a=0, b=None):
            off, n = where[name]
            return par[:, off + a:off + (n if b is None else b)]

        cur = [0]

        def reset(at=0):
            cur[0] = at

        def take(*shape):
            n = int(np.prod(shape))
            assert cur[0] + n <= ARENA, (cur[0], n)
            v = arena[:, cur[0]:cur[0] + n]
            cur[0] += n
            if len(shape) == 2:
                v = v.rearrange("p (a b) -> p a b", a=shape[0])
            if len(shape) == 3:
                v = v.rearrange("p (a b c) -> p a b c", a=shape[0], b=shape[1])
            return v

        ident, ones = c("ident"), c("ones")
        block = ctx.enter_context(nc.Block())

        @block.sync
        def _(sp):
            sp.dma_start(par[:, :], params).then_inc(params_in, 16)
            for t in range(RING):
                sp.dma_start(ring[:, t, :], stream[t]).then_inc(landed[t], 16)

        def load_turns(sp, first, end):
            with sp.Fori(first, end) as turn:
                for s in range(RING):
                    sp.wait_ge(tile_used.sem, turn * RING + (s - RING + 1))
                    sp.dma_start(ring[:, s, :], stream[turn * RING + s]).then_inc(landed[s], 16)

        def weights(pe, ahead=0):
            t = tile_used.n + ahead
            pe.wait_ge(landed[t % RING], 16 * (t // RING + 1))
            return ring[:, t % RING, :]

        freed = [[] for _ in range(8)]

        def claim(pe, *banks):
            for b in banks:
                for d, n in freed[b]:
                    pe.wait_ge(d.sem, n)
                freed[b] = []

        def feature_tile(banks, src, tok0, ntok):
            @block.tensor
            def _(pe):
                w = weights(pe).rearrange("p (k n) -> p k n", k=KT)
                claim(pe, *set(banks))
                for half in range(2):
                    o = ps[:, banks[half], :]
                    if banks[0] == banks[1]:
                        o = ps[:, banks[0], half * 256:half * 256 + 256]
                    for k in range(KT):
                        last = nc.tensor.matmul(o[:, 0:ntok], w[:, k, half * P:half * P + P],
                                                src[:, k, tok0:tok0 + ntok],
                                                start=(k == 0), stop=(k == KT - 1))
                tile_used.by(last)
            return tile_used.n

        def token_rows(banks, src, tok0, ktiles, cols=512, kper=4):
            @block.tensor
            def _(pe):
                claim(pe, *banks)
                for t0 in range(0, ktiles, kper):
                    w = weights(pe).rearrange("p (k n) -> p k n", k=kper)
                    for n, b in enumerate(banks):
                        for k in range(t0, min(t0 + kper, ktiles)):
                            last = nc.tensor.matmul(ps[:, b, 0:cols],
                                                    src[:, k, tok0 + n * P:tok0 + n * P + P],
                                                    w[:, k - t0, 0:cols],
                                                    start=(k == 0), stop=(k == ktiles - 1))
                    tile_used.by(last)
            return tile_used.n

        def inverse_root(pool, out_, in_):
            link(pool, pool_done, nc.gpsimd.tensor_tensor(out_, in_, half_pow[:, 0:in_.shape[1]], ALU.pow))

        def norm_T(x, outs, tok0, scratch):
            for t in range(TT):
                @block.scalar
                def _(act):
                    after_all(act)
                    link(act, act_done, nc.scalar.activation(scratch[:, t, :], x[:, t, :], ACT.Square,
                                                             accum_out=small[:, t:t + 1]))

            @block.vector
            def _(dve):
                dve.wait_ge(act_done.sem, act_done.n)
                link(dve, dve_done, nc.vector.tensor_scalar(small[:, 2:4], small[:, 0:2], 1.0 / D, EPS,
                                                            ALU.mult, ALU.add))

            @block.gpsimd
            def _(pool):
                pool.wait_ge(dve_done.sem, dve_done.n)
                inverse_root(pool, small[:, 4:6], small[:, 2:4])

            for t in range(TT):
                @block.vector
                def _(dve):
                    dve.wait_ge(pool_done.sem, pool_done.n)
                    link(dve, dve_done, nc.vector.tensor_scalar(scratch[:, t, :], x[:, t, :],
                                                                small[:, 4 + t:5 + t], None, ALU.mult))
                for q in range(2):
                    b = (2 * t + q) % 4

                    @block.tensor
                    def _(pe):
                        claim(pe, b)
                        pe.wait_ge(dve_done.sem, dve_done.n)
                        for j in range(4):
                            last = nc.tensor.transpose(ps[:, b, j * P:j * P + P],
                                                       scratch[:, t, (4 * q + j) * P:(4 * q + j + 1) * P], ident)
                        pe_done.by(last)

                for q in range(2):
                    b = (2 * t + q) % 4

                    @block.vector
                    def _(dve):
                        dve.wait_ge(pe_done.sem, pe_done.n - 1 + q)
                        for dst, gain, shift in outs:
                            for j in range(4):
                                k = 4 * q + j
                                o = dst[:, k, tok0 + t * P:tok0 + t * P + P]
                                if shift is None:
                                    ins = nc.vector.tensor_scalar(o, ps[:, b, j * P:j * P + P], gain[:, k:k + 1],
                                                                  None, ALU.mult)
                                else:
                                    ins = nc.vector.tensor_scalar(o, ps[:, b, j * P:j * P + P], gain[:, k:k + 1],
                                                                  shift[:, k:k + 1], ALU.mult, ALU.add)
                        dve_done.by(ins)
                        freed[b] = [(dve_done, dve_done.n)]

        def copy_bank(b, dst, cols=slice(0, 512)):
            @block.vector
            def _(dve):
                dve.wait_ge(tile_used.sem, tile_used.n)
                dve.wait_ge(pe_done.sem, pe_done.n) if pe_done.n else None
                dve_done.by(nc.vector.tensor_copy(dst, ps[:, b, cols]))
                freed[b] = [(dve_done, dve_done.n)]

        def add_rows(banks, x, half, gate=None, scratch=None):
            @block.vector
            def _(dve):
                dve.wait_ge(tile_used.sem, tile_used.n)
                for n, b in enumerate(banks):
                    xs = x(n)[:, half * 512:half * 512 + 512]
                    if gate is None:
                        dve_done.by(nc.vector.tensor_tensor(xs, xs, ps[:, b, :], ALU.add))
                    else:
                        link(dve, dve_done, nc.vector.tensor_tensor(scratch[:, n, :], ps[:, b, :],
                                                                    gate(n)[:, half * 512:half * 512 + 512], ALU.mult))
                        dve_done.by(nc.vector.tensor_tensor(xs, xs, scratch[:, n, :], ALU.add))
                    freed[b] = [(dve_done, dve_done.n)]

        def settle():
            @block.tensor
            def _(pe):
                after_all(pe)

        half_pow = small[:, 496:512]

        @block.scalar
        def _(act):
            for t in range(TT):
                act.dma_start(h[:, t, :], out["x"][t * P:t * P + P, :]).then_inc(x_in, 16)
                act.dma_start(cx[:, t, :], out["ctx"][t * P:t * P + P, :]).then_inc(x_in, 16)

        @block.gpsimd
        def _(pool):
            pool_done.by(nc.gpsimd.memset(half_pow, -0.5))

        for eng in (block.tensor, block.scalar, block.vector, block.gpsimd):
            @eng
            def _(e):
                e.wait_ge(params_in, 16)
                e.wait_ge(x_in, 16 * 2 * TT)

        @block.scalar
        def _(act):
            link(act, act_done, nc.scalar.activation(c("cond"), c("cond"), ACT.Silu))
        cond = c("cond").rearrange("p (k n) -> p k n", k=KT)

        reset()
        arow = take(6 * D)

        def ada_layer(layer):
            for n in range(12):
                b = n % 4

                @block.tensor
                def _(pe):
                    pe.wait_ge(act_done.sem, act_done.n) if n == 0 else None
                    claim(pe, b)
                    for half in range(2):
                        w = weights(pe).rearrange("p (k n) -> p k n", k=KT)
                        for k in range(KT):
                            last = nc.tensor.matmul(ps[0:2, b, half * 256:half * 256 + 256], cond[:, k, :],
                                                    w[:, k, :], start=(k == 0), stop=(k == KT - 1))
                        tile_used.by(last)

                @block.vector
                def _(dve):
                    if n == 0:
                        after_all(dve)
                    dve.wait_ge(tile_used.sem, tile_used.n)
                    dve_done.by(nc.vector.tensor_copy(arow[0:2, n * 512:n * 512 + 512], ps[0:2, b, :]))
                    freed[b] = [(dve_done, dve_done.n)]

            @block.tensor
            def _(pe):
                after_all(pe)
                for n in range(48):
                    last = nc.tensor.matmul(ps[:, 4, 2 * n:2 * n + 2], arow[0:2, n * P:n * P + P],
                                            ident[0:2, 0:2], start=True, stop=True)
                pe_done.by(last)

            @block.vector
            def _(dve):
                after_all(dve)
                dve_done.by(nc.vector.tensor_tensor(ada[:, layer, :, :].rearrange("p n c -> p (n c)"),
                                                    ps[:, 4, 0:96], c("ada_b", 96 * layer, 96 * layer + 96),
                                                    ALU.add))

        ada_layer(0)
        ada_layer(1)

        reset()
        xs = take(TT, D)
        norm_T(h, [(hT, c("attn0"), None)], 0, xs)
        reset()
        qdec, kinv, kend = take(H1, SEQ), take(H1, SEQ), take(H1, SEQ)
        q31, q30, q20 = take(H1, CHUNK), take(H1, CHUNK), take(H1, CHUNK)
        expb, expnb, expe = take(H1, SEQ), take(H1, SEQ), take(H1, SEQ)
        v = take(TT, D)
        rT = take(KT, SEQ)
        la = take(TT, 512)
        tmp = take(TT, 512)
        glr = take(SEQ)
        bend, de = take(16).rearrange("p (h n) -> p h n", h=H1), take(16).rearrange("p (h n) -> p h n", h=H1)
        e12 = take(H1)
        aT = take(H1, TT, SEQ)
        oo = take(TT, D)

        @block.tensor
        def _(pe):
            after_all(pe)
            wl = c("w_glr").rearrange("p (k n) -> p k n", k=KT)
            for k in range(KT):
                last = nc.tensor.matmul(ps[0:16, 0, 0:SEQ], wl[:, k, :], hT[:, k, 0:SEQ],
                                        start=(k == 0), stop=(k == KT - 1))
            pe_done.by(last)

        @block.vector
        def _(dve):
            after_all(dve)
            dve_done.by(nc.vector.tensor_copy(glr[0:16, :], ps[0:16, 0, 0:SEQ]))

        @block.tensor
        def _(pe):
            after_all(pe)
            for t in range(TT):
                nc.tensor.matmul(ps[:, 1 + t, :], glr[0:16, t * P:t * P + P], c("gate_up")[0:16, :],
                                 start=True, stop=False)
                last = nc.tensor.matmul(ps[:, 1 + t, :], ones[0:1, :], c("gate_b")[0:1, :],
                                        start=False, stop=True)
            pe_done.by(last)

        @block.scalar
        def _(act):
            after_all(act)
            link(act, act_done, nc.scalar.activation(tmp, ps[:, 1:3, :], ACT.Abs))
            link(act, act_done, nc.scalar.activation(tmp, tmp, ACT.Exp, scale=-1.0))
            link(act, act_done, nc.scalar.activation(tmp, tmp, ACT.Ln, bias=1.0))

        @block.vector
        def _(dve):
            after_all(dve)
            dve_done.by(nc.vector.scalar_tensor_tensor(la, ps[:, 1:3, :], 0.0, tmp, ALU.min, ALU.subtract))

        @block.tensor
        def _(pe):
            after_all(pe)
            for hh in range(H1):
                for t in range(TT):
                    last = nc.tensor.matmul(ps[:, hh // 2, (hh % 2) * SEQ + t * P:(hh % 2) * SEQ + t * P + P],
                                            la[:, t, hh * P:hh * P + P], c("gla_sum"), start=True, stop=True)
            pe_done.by(last)

        pb = ps[:, 0:2, :].rearrange("p b (h n c) -> p (b h) n c", h=2, c=CHUNK)

        @block.scalar
        def _(act):
            after_all(act)
            link(act, act_done, nc.scalar.activation(expb.rearrange("p h t -> p (h t)"), ps[:, 0:2, :], ACT.Exp))
            link(act, act_done, nc.scalar.activation(expnb.rearrange("p h t -> p (h t)"), ps[:, 0:2, :], ACT.Exp,
                                                     scale=-1.0))

        @block.vector
        def _(dve):
            after_all(dve)
            link(dve, dve_done, nc.vector.tensor_copy(bend, pb[:, :, :, CHUNK - 1]))
            for hh in range(H1):
                ins = nc.vector.tensor_tensor(
                    expe[:, hh, :].rearrange("p (n c) -> p n c", c=CHUNK),
                    bend[:, hh, :].unsqueeze(2).to_broadcast([P, 4, CHUNK]), pb[:, hh, :, :], ALU.subtract)
            dve_done.by(ins)

        @block.scalar
        def _(act):
            after_all(act)
            link(act, act_done, nc.scalar.activation(expe, expe, ACT.Exp))
            link(act, act_done, nc.scalar.activation(de, bend, ACT.Exp))

        for n in range(2):
            feature_tile([2 + n, 2 + n], hT, 0, SEQ)

            @block.vector
            def _(dve):
                after_all(dve)
                dve_done.by(nc.vector.scalar_tensor_tensor(
                    qdec[:, 2 * n:2 * n + 2, :].rearrange("p h t -> p (h t)"), ps[:, 2 + n, :], float(P) ** -0.5,
                    expb[:, 2 * n:2 * n + 2, :].rearrange("p h t -> p (h t)"), ALU.mult, ALU.mult))
                freed[2 + n] = [(dve_done, dve_done.n)]
        for n in range(2):
            feature_tile([4 + n, 4 + n], hT, 0, SEQ)

            @block.vector
            def _(dve):
                after_all(dve)
                kp = ps[:, 4 + n, :]
                nc.vector.tensor_tensor(kinv[:, 2 * n:2 * n + 2, :].rearrange("p h t -> p (h t)"), kp,
                                        expnb[:, 2 * n:2 * n + 2, :].rearrange("p h t -> p (h t)"), ALU.mult)
                dve_done.by(nc.vector.tensor_tensor(
                    kend[:, 2 * n:2 * n + 2, :].rearrange("p h t -> p (h t)"), kp,
                    expe[:, 2 * n:2 * n + 2, :].rearrange("p h t -> p (h t)"), ALU.mult))
                freed[4 + n] = [(dve_done, dve_done.n)]
        for n in range(2):
            token_rows([6, 7], hT, 0, KT)
            for t in range(TT):
                copy_bank(6 + t, v[:, t, n * 512:n * 512 + 512])
        for n in range(4):
            b = n % 4
            feature_tile([b, b], hT, 0, SEQ)

            @block.scalar
            def _(act):
                act.wait_ge(tile_used.sem, tile_used.n)
                act_done.by(nc.scalar.activation(rT[:, 2 * n:2 * n + 2, :].rearrange("p h t -> p (h t)"),
                                                 ps[:, b, :], ACT.Silu))
                freed[b] = [(act_done, act_done.n)]

        @block.vector
        def _(dve):
            after_all(dve)
            def spread(e):
                return e.unsqueeze(2).to_broadcast([P, H1, CHUNK])
            link(dve, dve_done, nc.vector.tensor_tensor(e12, de[:, :, 1], de[:, :, 2], ALU.mult))
            nc.vector.tensor_tensor(q20, qdec[:, :, 128:192], spread(de[:, :, 1]), ALU.mult)
            nc.vector.tensor_tensor(q31, qdec[:, :, 192:256], spread(de[:, :, 2]), ALU.mult)
            nc.vector.tensor_tensor(q30, qdec[:, :, 192:256], spread(e12), ALU.mult)
            dve_done.by(nc.vector.memset(aT, 0.0))

        for hh in range(H1):
            b = 4 + hh

            @block.tensor
            def _(pe):
                after_all(pe) if hh == 0 else None
                for t in range(TT):
                    nc.tensor.matmul(ps[:, b, t * P:t * P + P], kinv[:, hh, t * P:t * P + P],
                                     qdec[:, hh, t * P:t * P + P], start=True, stop=True)
                ch = lambda x, n: x[:, hh, n * CHUNK:n * CHUNK + CHUNK]
                pairs = [(0, 256, ch(kend, 0), ch(qdec, 1)), (0, 320, ch(kend, 0), q20[:, hh, :]),
                         (0, 384, ch(kend, 0), q30[:, hh, :]), (64, 320, ch(kend, 1), ch(qdec, 2)),
                         (64, 384, ch(kend, 1), q31[:, hh, :]), (0, 448, ch(kend, 2), ch(qdec, 3))]
                for row, col, lhs, rhs in pairs:
                    last = nc.tensor.matmul(ps[row:row + 64, b, col:col + 64], lhs, rhs, start=True, stop=True)
                pe_done.by(last)

            @block.vector
            def _(dve):
                after_all(dve)
                for t in range(TT):
                    last = nc.vector.tensor_tensor(aT[:, hh, t, t * P:t * P + P], ps[:, b, t * P:t * P + P],
                                                   c("gla_mask"), ALU.mult)
                link(dve, dve_done, last)
                nc.vector.tensor_copy(aT[0:64, hh, 0, 64:256], ps[0:64, b, 256:448])
                nc.vector.tensor_copy(aT[64:128, hh, 0, 128:256], ps[64:128, b, 320:448])
                dve_done.by(nc.vector.tensor_copy(aT[0:64, hh, 1, 192:256], ps[0:64, b, 448:512]))

        @block.tensor
        def _(pe):
            after_all(pe)
            for hh in range(H1):
                for t in range(TT):
                    for j in range(t + 1):
                        last = nc.tensor.matmul(ps[:, 2 * t + hh // 2, (hh % 2) * DV1:(hh % 2) * DV1 + DV1],
                                                aT[:, hh, j, t * P:t * P + P], v[:, j, hh * DV1:hh * DV1 + DV1],
                                                start=(j == 0), stop=(j == t))
            pe_done.by(last)

        @block.scalar
        def _(act):
            after_all(act)
            for t in range(TT):
                for hh in range(H1):
                    link(act, act_done, nc.scalar.activation(
                        oo[:, t, hh * DV1:hh * DV1 + DV1],
                        ps[:, 2 * t + hh // 2, (hh % 2) * DV1:(hh % 2) * DV1 + DV1], ACT.Square,
                        accum_out=small[:, 8 + 4 * t + hh:9 + 4 * t + hh]))

        def rstd_of(cols, n):
            a, b_ = cols

            @block.vector
            def _(dve):
                after_all(dve)
                link(dve, dve_done, nc.vector.tensor_scalar(small[:, a:b_], small[:, a:b_], 1.0 / n, EPS,
                                                            ALU.mult, ALU.add))

            @block.gpsimd
            def _(pool):
                after_all(pool)
                inverse_root(pool, small[:, a + 16:b_ + 16], small[:, a:b_])

        rstd_of((8, 16), DV1)

        @block.vector
        def _(dve):
            after_all(dve)
            for t in range(TT):
                for hh in range(H1):
                    last = nc.vector.tensor_scalar(oo[:, t, hh * DV1:hh * DV1 + DV1],
                                                   ps[:, 2 * t + hh // 2, (hh % 2) * DV1:(hh % 2) * DV1 + DV1],
                                                   small[:, 24 + 4 * t + hh:25 + 4 * t + hh], None, ALU.mult)
            dve_done.by(last)

        yT = hT

        def transpose_rows(src, ntt, evac):
            for t in range(ntt):
                for q in range(2):
                    b = 4 + (2 * t + q) % 4

                    @block.tensor
                    def _(pe):
                        after_all(pe) if t == q == 0 else None
                        claim(pe, b)
                        for j in range(4):
                            last = nc.tensor.transpose(ps[:, b, j * P:j * P + P],
                                                       src[:, t, (4 * q + j) * P:(4 * q + j + 1) * P], ident)
                        pe_done.by(last)

                    @block.vector
                    def _(dve):
                        dve.wait_ge(pe_done.sem, pe_done.n)
                        for j in range(4):
                            last = evac(ps[:, b, j * P:j * P + P], 4 * q + j, t)
                        dve_done.by(last)
                        freed[b] = [(dve_done, dve_done.n)]

        transpose_rows(oo, TT, lambda part, k, t: nc.vector.scalar_tensor_tensor(
            yT[:, k, t * P:t * P + P], part, c("gla_head")[:, k % 2:k % 2 + 1], rT[:, k, t * P:t * P + P],
            ALU.mult, ALU.mult))

        settle()
        for n in range(2):
            token_rows([2 * n, 2 * n + 1], yT, 0, KT)
            add_rows([2 * n, 2 * n + 1], lambda t: h[:, t, :], n)

        ffn_silu = sem("ffn_silu")
        ffn_act = sem("ffn_act")

        def turns(eng, n, looped, tile, size=RING):
            with eng.Fori(0, looped) as g:
                for s in range(size):
                    tile(g, s)
            for s in range(n - looped * size):
                tile(looped, s)

        def feed_forward(nf, hid, sg):
            t0 = tile_used.n
            slot = lambda k: (t0 + k) % RING
            looped = nf // RING

            @block.tensor
            def _(pe):
                after_all(pe)

                def up(g, s):
                    w = ring[:, slot(s), :].rearrange("p (k n) -> p k n", k=KT)
                    pe.wait_ge(landed[slot(s)], g * 16 + 16 * ((t0 + s) // RING + 1))
                    b = BANKS_PLAIN[s]
                    pe.wait_ge(ffn_act, g * RING + (RING + s - since(BANKS_PLAIN, s) + 1))
                    for half in range(2):
                        for k in range(KT):
                            last = nc.tensor.matmul(ps[:, b, half * SEQ:half * SEQ + SEQ],
                                                    w[:, k, half * P:half * P + P], hT[:, k, 0:SEQ],
                                                    start=(k == 0), stop=(k == KT - 1))
                    last.then_inc(tile_used.sem, 1)
                turns(pe, nf, looped, up)

            @block.scalar
            def _(act):
                after_all(act)

                def gate(g, s):
                    act.wait_ge(tile_used.sem, g * RING + (t0 + s + 1))
                    act.wait_ge(ffn_act, g * RING + (s + 1))
                    nc.scalar.activation(sg[:, s, :], ps[:, BANKS_PLAIN[s], 0:SEQ],
                                         ACT.Silu).then_inc(ffn_silu, 1)
                turns(act, nf, looped, gate)

            @block.vector
            def _(dve):
                after_all(dve)

                def hidden(g, s):
                    dve.wait_ge(ffn_silu, g * RING + (s + 1))
                    nc.vector.tensor_tensor(hid[:, g * RING + s, :], sg[:, s, :],
                                            ps[:, BANKS_PLAIN[s], SEQ:2 * SEQ], ALU.mult).then_inc(ffn_act, 1)
                turns(dve, nf, looped, hidden)
                dve.wait_ge(ffn_act, RING + nf)
                dve_done.by(nc.vector.tensor_copy(small[:, 480:481], small[:, 481:482]))
            tile_used.n += nf
            for b in range(4):
                freed[b] = [(dve_done, dve_done.n)]

        @block.vector
        def _(dve):
            dve_done.by(nc.vector.memset(small[:, 480:496], 0.0))
            dve.sem_inc(ffn_act, RING)

        reset()
        xs = take(TT, D)
        norm_T(h, [(hT, c("ffn0"), None)], 0, xs)
        reset()
        hid = take(F_FFN, SEQ)
        sg = take(RING, SEQ)
        feed_forward(F_FFN, hid, sg)
        for n in range(2):
            settle() if n == 0 else None
            token_rows([4 + 2 * n, 5 + 2 * n], hid, 0, F_FFN)
            add_rows([4 + 2 * n, 5 + 2 * n], lambda t: h[:, t, :], n)

        reset()
        xs = take(TT, D)
        hT2 = take(KT, SEQ)
        norm_T(h, [(hT, c("kvn"), None), (hT2, c("attn1"), None)], 0, xs)
        reset()
        xs = take(TT, D)
        hT2 = take(KT, SEQ)
        kT, qT = take(SBH, SEQ), take(SBH, SEQ)
        v = take(TT, D)
        zs, sp_, uu, wt = take(TT, SEQ), take(TT, SEQ), take(TT, SEQ), take(TT, SEQ)
        settle()
        for n in range(4):
            feature_tile([n, n], hT, 0, SEQ)
            copy_bank(n, kT[:, 2 * n:2 * n + 2, :].rearrange("p h t -> p (h t)"))
        for n in range(2):
            token_rows([4, 5], hT, 0, KT)
            for t in range(TT):
                copy_bank(4 + t, v[:, t, n * 512:n * 512 + 512])
        for n in range(4):
            feature_tile([n, n], hT2, 0, SEQ)
            copy_bank(n, qT[:, 2 * n:2 * n + 2, :].rearrange("p h t -> p (h t)"))
        for hh in range(SBH):
            @block.tensor
            def _(pe):
                after_all(pe)
                for j in range(TT):
                    last = nc.tensor.matmul(ps[:, 0, j * SEQ:j * SEQ + SEQ], kT[:, hh, j * P:j * P + P],
                                            qT[:, hh, :], start=True, stop=True)
                pe_done.by(last)

            @block.scalar
            def _(act):
                after_all(act)
                link(act, act_done, nc.scalar.activation(zs, ps[:, 0, :], ACT.Copy, scale=float(P) ** -0.5))
                link(act, act_done, nc.scalar.activation(uu, zs, ACT.Abs))
                link(act, act_done, nc.scalar.activation(uu, uu, ACT.Exp, scale=-1.0))
                link(act, act_done, nc.scalar.activation(uu, uu, ACT.Ln, bias=1.0))

            @block.vector
            def _(dve):
                after_all(dve)
                link(dve, dve_done, nc.vector.scalar_tensor_tensor(uu, zs, 0.0, uu, ALU.max, ALU.add))
                nc.vector.tensor_tensor(sp_.rearrange("p a b -> p (a b)"), uu.rearrange("p a b -> p (a b)"),
                                        c("sb_mask"), ALU.mult)
                dve_done.by(nc.vector.tensor_tensor(uu, zs, uu, ALU.subtract))

            @block.tensor
            def _(pe):
                after_all(pe)
                nc.tensor.matmul(ps[:, 1, 0:SEQ], c("sb_later"), sp_[:, 0, :], start=True, stop=False)
                nc.tensor.matmul(ps[:, 1, 0:SEQ], c("minus"), sp_[:, 1, :], start=False, stop=True)
                pe_done.by(nc.tensor.matmul(ps[:, 1, SEQ:2 * SEQ], c("sb_later"), sp_[:, 1, :],
                                            start=True, stop=True))

            @block.vector
            def _(dve):
                after_all(dve)
                dve_done.by(nc.vector.tensor_tensor(uu.rearrange("p a b -> p (a b)"),
                                                    uu.rearrange("p a b -> p (a b)"), ps[:, 1, :], ALU.add))

            @block.scalar
            def _(act):
                after_all(act)
                act_done.by(nc.scalar.activation(uu, uu, ACT.Exp))

            @block.vector
            def _(dve):
                after_all(dve)
                dve_done.by(nc.vector.tensor_tensor(wt.rearrange("p a b -> p (a b)"),
                                                    uu.rearrange("p a b -> p (a b)"), c("sb_mask"), ALU.mult))

            @block.tensor
            def _(pe):
                after_all(pe)
                for j in range(TT):
                    last = nc.tensor.matmul(ps[:, 2, 0:SEQ], v[:, j, hh * P:hh * P + P], wt[:, j, :],
                                            start=(j == 0), stop=(j == TT - 1))
                pe_done.by(last)
            copy_bank(2, hT[:, hh, 0:SEQ], slice(0, SEQ))

        settle()
        for n in range(2):
            token_rows([2 * n, 2 * n + 1], hT, 0, KT)
            add_rows([2 * n, 2 * n + 1], lambda t: h[:, t, :], n)

        moe_gathered = sem("moe_gathered")
        moe_tokens = sem("moe_tokens")
        moe_silu = sem("moe_silu")
        moe_hid = sem("moe_hid")
        moe_y = sem("moe_y")
        moe_spread = sem("moe_spread")
        moe_place = sem("moe_place")
        reset()
        xn = take(TT, D)
        norm_T(h, [(hT, c("ffn1"), None)], 0, xn)
        hid = take(F_MOE, P)
        sg = take(2, P)
        hTe = take(KT, P)
        pick = take(TT, EXPERTS + 1, P)
        place = take(EXPERTS, SEQ)
        placed = take(SEQ)
        y = take(D)
        tmp = take(P)
        mark = cur[0]
        lg = take(TT, EXPERTS)
        top = take(TT, 8)
        idx = arena[:, cur[0]:cur[0] + 16].bitcast(U32).rearrange("p (t n) -> p t n", t=TT)
        cur[0] += 16
        idf = take(TT, 8)
        wsel = take(TT, 4)
        sel = take(TT, EXPERTS)
        chosen = take(TT, EXPERTS)
        gates = take(TT, EXPERTS)
        rank = take(TT, EXPERTS)
        rest = small[:, 256:272].rearrange("p (t n) -> p t n", t=TT)
        over = small[:, 272:274]
        flag = small[:, 274:275].bitcast(U32)

        @block.tensor
        def _(pe):
            after_all(pe)
            wr = c("router").rearrange("p (k n) -> p k n", k=KT)
            for t in range(TT):
                for k in range(KT):
                    last = nc.tensor.matmul(ps[:, 4, t * EXPERTS:(t + 1) * EXPERTS], hT[:, k, t * P:t * P + P],
                                            wr[:, k, :], start=(k == 0), stop=(k == KT - 1))
            pe_done.by(last)

        @block.vector
        def _(dve):
            after_all(dve)
            link(dve, dve_done, nc.vector.tensor_copy(lg.rearrange("p t n -> p (t n)"), ps[:, 4, 0:TT * EXPERTS]))
            for t in range(TT):
                link(dve, dve_done, nc.vector.max(top[:, t, :], lg[:, t, :]))
                link(dve, dve_done, nc.vector.max_index(idx[:, t, :], top[:, t, :], lg[:, t, :]))
            link(dve, dve_done, nc.vector.tensor_copy(idf, idx))
            link(dve, dve_done, nc.vector.tensor_tensor(wsel[:, :, 0], top[:, :, 1], top[:, :, 0], ALU.subtract))

        @block.scalar
        def _(act):
            after_all(act)
            act_done.by(nc.scalar.activation(wsel[:, :, 1], wsel[:, :, 0], ACT.Exp))

        @block.vector
        def _(dve):
            after_all(dve)
            link(dve, dve_done, nc.vector.tensor_scalar(wsel[:, :, 2], wsel[:, :, 1], 1.0, None, ALU.add))
            link(dve, dve_done, nc.vector.reciprocal(wsel[:, :, 2], wsel[:, :, 2]))
            link(dve, dve_done, nc.vector.tensor_tensor(wsel[:, :, 3], wsel[:, :, 1], wsel[:, :, 2], ALU.mult))
            for t in range(TT):
                nc.vector.tensor_scalar(gates[:, t, :], c("iota8"), idf[:, t, 0:1],
                                        wsel[:, t, 2:3], ALU.is_equal, ALU.mult)
                link(dve, dve_done, nc.vector.tensor_scalar(sel[:, t, :], c("iota8"), idf[:, t, 1:2],
                                                            wsel[:, t, 3:4], ALU.is_equal, ALU.mult))
            link(dve, dve_done, nc.vector.tensor_tensor(gates, gates, sel, ALU.add))
            for t in range(TT):
                nc.vector.tensor_scalar(sel[:, t, :], c("iota8"), idf[:, t, 1:2], None, ALU.is_equal)
                ins = nc.vector.tensor_scalar(chosen[:, t, :], c("iota8"), idf[:, t, 0:1], None, ALU.is_equal)
            link(dve, dve_done, ins)
            link(dve, dve_done, nc.vector.tensor_tensor(chosen, chosen, sel, ALU.add))

        @block.tensor
        def _(pe):
            after_all(pe)
            nc.tensor.matmul(ps[:, 4, 0:8], c("strict0"), chosen[:, 0, :], start=True, stop=True)
            nc.tensor.matmul(ps[:, 4, 8:16], ones, chosen[:, 0, :], start=True, stop=False)
            nc.tensor.matmul(ps[:, 4, 8:16], c("strict0"), chosen[:, 1, :], start=False, stop=True)
            nc.tensor.matmul(ps[:, 4, 16:24], ones, chosen[:, 0, :], start=True, stop=False)
            pe_done.by(nc.tensor.matmul(ps[:, 4, 16:24], ones, chosen[:, 1, :], start=False, stop=True))

        @block.vector
        def _(dve):
            after_all(dve)
            nc.vector.tensor_reduce(over[:, 0:1], ps[:, 4, 16:24], AXX, ALU.max)
            link(dve, dve_done, nc.vector.tensor_copy(rank.rearrange("p t n -> p (t n)"), ps[:, 4, 0:16]))
            link(dve, dve_done, nc.vector.tensor_scalar(flag, over[:, 0:1], float(CAP), None, ALU.is_gt))
            link(dve, dve_done, nc.vector.tensor_scalar(rest, rank, float(CAP), None, ALU.is_ge))
            link(dve, dve_done, nc.vector.tensor_tensor(rest, rest, gates, ALU.mult))
            nc.vector.memset(pick[:, :, EXPERTS, :], 0.0)
            for e in range(EXPERTS):
                for t in range(TT):
                    ins = nc.vector.tensor_scalar(pick[:, t, e, :], c("slots"), rank[:, t, e:e + 1],
                                                  chosen[:, t, e:e + 1], ALU.is_equal, ALU.mult)
            link(dve, dve_done, ins)
        flag_known = dve_done.n

        @block.tensor
        def _(pe):
            after_all(pe)
            for t in range(TT):
                for half in range(2):
                    nc.tensor.matmul(ps[:, 2 * t + half, :], ident, h[:, t, half * 512:half * 512 + 512],
                                     start=True, stop=False, skip_group_check=True)
            for e in range(EXPERTS):
                for t in range(TT):
                    last = nc.tensor.transpose(ps[:, 4 + e // 2, (e % 2) * SEQ + t * P:(e % 2) * SEQ + t * P + P],
                                               pick[:, t, e, :], ident)
            pe_done.by(last)

        @block.vector
        def _(dve):
            after_all(dve)
            dve_done.by(nc.vector.tensor_copy(place.rearrange("p e t -> p (e t)"),
                                              ps[:, 4:8, :].rearrange("p b n -> p (b n)")))
        for e in range(EXPERTS):
            @block.vector
            def _(dve):
                after_all(dve)
                nc.vector.tensor_copy(sg[:, 0, :], gates[:, 0, e:e + 1].to_broadcast([P, P]))
                dve_done.by(nc.vector.tensor_copy(sg[:, 1, :], gates[:, 1, e:e + 1].to_broadcast([P, P])))

            @block.tensor
            def _(pe):
                after_all(pe)
                for t in range(TT):
                    last = nc.tensor.matmul(ps[:, 4, t * P:t * P + P], sg[:, t, :], ident, start=True, stop=True)
                pe_done.by(last)

            @block.vector
            def _(dve):
                after_all(dve)
                dve_done.by(nc.vector.tensor_tensor(place[:, e, :], place[:, e, :], ps[:, 4, 0:SEQ], ALU.mult))

        nf = F_MOE
        kd = nf // 4
        per = nf + 2 * kd
        turns_per = per // RING
        BODY = 2 * RING
        assert per % RING == 0 and nf % BODY == 0
        moe_t0 = tile_used.n
        slot = lambda k: (moe_t0 + k) % RING
        wait_of = lambda k: 16 * ((moe_t0 + k) // RING + 1)

        def gather(pe, e):
            for k in range(KT):
                for t in range(TT):
                    last = nc.tensor.matmul(ps[:, 4 + k // 4, (k % 4) * P:(k % 4) * P + P],
                                            xn[:, t, k * P:k * P + P],
                                            pick[:, t, bass.ds(e, 1), :].rearrange("p a n -> p (a n)"),
                                            start=(t == 0), stop=(t == TT - 1), skip_group_check=True)
            last.then_inc(moe_gathered, 1)

        def copy_tokens(dve):
            for k in range(KT):
                last = nc.vector.tensor_scalar(hTe[:, k, :], ps[:, 4 + k // 4, (k % 4) * P:(k % 4) * P + P],
                                               c("ffn1")[:, k:k + 1], None, ALU.mult)
            last.then_inc(moe_tokens, 1)

        @block.tensor
        def _(pe):
            after_all(pe)
            gather(pe, 0)
            with pe.Fori(0, EXPERTS) as e:
                with pe.Fori(0, nf // BODY) as g:
                    pe.wait_ge(moe_tokens, e + 1)
                    for s in range(BODY):
                        pe.wait_ge(landed[slot(s)], e * (16 * turns_per) + g * (16 * BODY // RING) + wait_of(s))
                        w = ring[:, slot(s), :].rearrange("p (k n) -> p k n", k=KT)
                        pe.wait_ge(moe_hid, e * nf + g * BODY + (s + 1))
                        for half in range(2):
                            for k in range(KT):
                                last = nc.tensor.matmul(ps[:, 4 + s % 2, half * P:half * P + P],
                                                        w[:, k, half * P:half * P + P], hTe[:, k, :],
                                                        start=(k == 0), stop=(k == KT - 1), skip_group_check=True)
                        last.then_inc(tile_used.sem, 1)
                pe.wait_ge(moe_hid, e * nf + (nf + 2))
                gather(pe, e + 1)
                for half in range(2):
                    for d in range(kd):
                        k0 = nf + half * kd + d
                        pe.wait_ge(landed[slot(k0)], e * (16 * turns_per) + wait_of(k0))
                        w = ring[:, slot(k0), :].rearrange("p (k n) -> p k n", k=4)
                        for j in range(4):
                            last = nc.tensor.matmul(ps[:, 6 + half, :], hid[:, 4 * d + j, :], w[:, j, :],
                                                    start=(d == j == 0), stop=(d == kd - 1 and j == 3),
                                                    skip_group_check=True)
                        last.then_inc(tile_used.sem, 1)
                pe.wait_ge(moe_y, e * 2 + 2)
                pe.wait_ge(moe_place, e + 1)
                for half in range(2):
                    for t in range(TT):
                        last = nc.tensor.matmul(ps[:, 2 * t + half, :], placed[:, t * P:t * P + P],
                                                y[:, half * 512:half * 512 + 512], start=False, stop=False,
                                                skip_group_check=True)
                last.then_inc(moe_spread, 1)

        @block.scalar
        def _(act):
            after_all(act)
            with act.Fori(0, EXPERTS) as e:
                with act.Fori(0, nf // BODY) as g:
                    for s in range(BODY):
                        act.wait_ge(tile_used.sem, e * per + g * BODY + (moe_t0 + s + 1))
                        act.wait_ge(moe_hid, e * nf + g * BODY + (s + 1))
                        nc.scalar.activation(sg[:, s % 2, :], ps[:, 4 + s % 2, 0:P], ACT.Silu).then_inc(moe_silu, 1)
                for half in range(2):
                    act.wait_ge(tile_used.sem, e * per + (moe_t0 + nf + (half + 1) * kd))
                    nc.scalar.activation(y[:, half * 512:half * 512 + 512], ps[:, 6 + half, :],
                                         ACT.Copy).then_inc(moe_y, 1)

        @block.vector
        def _(dve):
            after_all(dve)
            dve.sem_inc(moe_hid, 2)
            dve.wait_ge(moe_gathered, 1)
            copy_tokens(dve)
            with dve.Fori(0, EXPERTS) as e:
                with dve.Fori(0, nf // BODY) as g:
                    for s in range(BODY):
                        dve.wait_ge(moe_silu, e * nf + g * BODY + (s + 1))
                        nc.vector.tensor_tensor(hid[:, g * BODY + s, :], sg[:, s % 2, :],
                                                ps[:, 4 + s % 2, P:2 * P], ALU.mult).then_inc(moe_hid, 1)
                dve.wait_ge(moe_gathered, e + 2)
                copy_tokens(dve)

        @block.gpsimd
        def _(pool):
            after_all(pool)
            pool.sem_inc(moe_spread, 1)
            with pool.Fori(0, EXPERTS) as e:
                pool.wait_ge(moe_spread, e + 1)
                nc.gpsimd.tensor_copy(placed, place[:, bass.ds(e, 1), :].rearrange("p a t -> p (a t)"))\
                    .then_inc(moe_place, 1)
        tile_used.n += EXPERTS * per

        @block.vector
        def _(dve):
            dve.wait_ge(moe_spread, EXPERTS + 1)
            for t in range(TT):
                ins = nc.vector.tensor_copy(h[:, t, :], ps[:, 2 * t:2 * t + 2, :].rearrange("p b n -> p (b n)"))
            dve.wait_ge(moe_tokens, EXPERTS + 1)
            dve_done.by(ins)
        for b in range(8):
            freed[b] = [(dve_done, dve_done.n)]

        over_landed = [sem(f"over_landed{n}") for n in range(2)]
        over_used = sem("over_used")
        over_silu = sem("over_silu")
        over_hid = sem("over_hid")
        over_gate = sem("over_gate")
        over_out = sem("over_out")
        main_end = {d: d.n for d in everyone}
        reset()
        oring = take(2, TILE)
        ohid = take(nf, SEQ)
        osg = take(2, SEQ)
        ogate = take(TT, 1)
        moe_turn = -(-tile_used.n // RING)

        def flag_set(eng):
            eng.wait_ge(dve_done.sem, flag_known)
            return eng.value_load(flag[0:1, 0:1], min_val=0, max_val=1) > 0

        @block.sync
        def _(sp):
            load_turns(sp, 1, moe_turn)
            with sp.If(flag_set(sp)):
                for d in everyone:
                    if main_end[d]:
                        sp.wait_ge(d.sem, main_end[d])
                with sp.Fori(0, EXPERTS * per // 2) as i:
                    for s in range(2):
                        sp.wait_ge(over_used, i * 2 + (s + 1))
                        sp.dma_start(oring[:, s, :], stream[i * 2 + (moe_t0 + s)]).then_inc(over_landed[s], 16)

        @block.tensor
        def _(pe):
            after_all(pe)
            with pe.If(flag_set(pe)):
                pe.sem_inc(over_used, 2)
                with pe.Fori(0, EXPERTS) as e:
                    with pe.Fori(0, nf // 2) as g:
                        for s in range(2):
                            pe.wait_ge(over_landed[s], e * (8 * per) + g * 16 + 16)
                            w = oring[:, s, :].rearrange("p (k n) -> p k n", k=KT)
                            pe.wait_ge(over_hid, e * nf + g * 2 + (s + 1))
                            for half in range(2):
                                for k in range(KT):
                                    last = nc.tensor.matmul(ps[:, 4 + s, half * SEQ:half * SEQ + SEQ],
                                                            w[:, k, half * P:half * P + P], hT[:, k, 0:SEQ],
                                                            start=(k == 0), stop=(k == KT - 1))
                            last.then_inc(over_used, 1)
                    pe.wait_ge(over_hid, e * nf + (nf + 2))
                    pe.wait_ge(over_out, e * 4 + 4)
                    for half in range(2):
                        for d in range(kd):
                            k0 = nf + half * kd + d
                            pe.wait_ge(over_landed[k0 % 2], e * (8 * per) + 16 * (k0 // 2 + 1))
                            w = oring[:, k0 % 2, :].rearrange("p (k n) -> p k n", k=4)
                            for t in range(TT):
                                for j in range(4):
                                    last = nc.tensor.matmul(ps[:, 2 * half + t, :],
                                                            ohid[:, 4 * d + j, t * P:t * P + P], w[:, j, :],
                                                            start=(d == j == 0), stop=(d == kd - 1 and j == 3))
                            last.then_inc(over_used, 1)

        @block.scalar
        def _(act):
            after_all(act)
            with act.If(flag_set(act)):
                with act.Fori(0, EXPERTS) as e:
                    with act.Fori(0, nf // 2) as g:
                        for s in range(2):
                            act.wait_ge(over_used, e * per + g * 2 + (s + 3))
                            act.wait_ge(over_hid, e * nf + g * 2 + (s + 1))
                            nc.scalar.activation(osg[:, s, :], ps[:, 4 + s, 0:SEQ], ACT.Silu).then_inc(over_silu, 1)

        @block.vector
        def _(dve):
            after_all(dve)
            with dve.If(flag_set(dve)):
                dve.sem_inc(over_hid, 2)
                dve.sem_inc(over_out, 4)
                with dve.Fori(0, EXPERTS) as e:
                    with dve.Fori(0, nf // 2) as g:
                        for s in range(2):
                            dve.wait_ge(over_silu, e * nf + g * 2 + (s + 1))
                            nc.vector.tensor_tensor(ohid[:, g * 2 + s, :], osg[:, s, :],
                                                    ps[:, 4 + s, SEQ:2 * SEQ], ALU.mult).then_inc(over_hid, 1)
                    dve.wait_ge(over_out, e * 4 + 4)
                    nc.vector.tensor_copy(ogate, rest[:, :, bass.ds(e, 1)]).then_inc(over_gate, 1)
                    dve.wait_ge(over_gate, e + 1)
                    for half in range(2):
                        dve.wait_ge(over_used, e * per + (2 + nf + (half + 1) * kd))
                        for t in range(TT):
                            hs = h[:, t, half * 512:half * 512 + 512]
                            nc.vector.scalar_tensor_tensor(hs, ps[:, 2 * half + t, :], ogate[:, t, :], hs,
                                                           ALU.mult, ALU.add).then_inc(over_out, 1)
                dve.wait_ge(over_out, EXPERTS * 4 + 4)

        @block.vector
        def _(dve):
            dve_done.by(nc.vector.tensor_copy(small[:, 480:481], small[:, 481:482]))

        def final_norm(gain_row):
            @block.scalar
            def _(act):
                after_all(act)
                for t in range(TT):
                    link(act, act_done, nc.scalar.activation(arena[:, 0:D], h[:, t, :], ACT.Square,
                                                             accum_out=small[:, 8 + t:9 + t]))
            rstd_of((8, 10), D)

            @block.vector
            def _(dve):
                after_all(dve)
                for t in range(TT):
                    dve_done.by(nc.vector.scalar_tensor_tensor(h[:, t, :], h[:, t, :], small[:, 24 + t:25 + t],
                                                               gain_row, ALU.mult, ALU.mult))

        final_norm(c("final1"))

        mod = small[:, 64:64 + 64].rearrange("p (a k) -> p a k", k=KT)

        def modulation(layer, which, gain, streams=2):
            out_ = []

            @block.vector
            def _(dve):
                after_all(dve)
                for s in range(2):
                    shift = ada[:, layer, 24 * which:24 * which + 8, s]
                    scale = ada[:, layer, 24 * which + 8:24 * which + 16, s]
                    dst = mod[:, s, :]
                    link(dve, dve_done, nc.vector.tensor_copy(mod[:, 2 + s, :], shift))
                    link(dve, dve_done, nc.vector.scalar_tensor_tensor(dst, scale, 1.0, gain, ALU.add, ALU.mult))
                    out_.append((dst, mod[:, 2 + s, :]))
            return out_

        def gate_rows(layer, which, dst, streams=(0, 1)):
            diag = take(P)
            for s in streams:
                for k in range(KT):
                    @block.vector
                    def _(dve):
                        after_all(dve)
                        dve_done.by(nc.vector.tensor_scalar(
                            diag, ident, ada[:, layer, 24 * which + 16 + k:24 * which + 17 + k, s], None, ALU.mult))

                    @block.tensor
                    def _(pe):
                        after_all(pe)
                        pe_done.by(nc.tensor.matmul(ps[:, s, 0:P], ones, diag, start=True, stop=True))

                    @block.vector
                    def _(dve):
                        after_all(dve)
                        dve_done.by(nc.vector.tensor_copy(dst[:, s, k * P:k * P + P], ps[:, s, 0:P]))

        reset()
        xs = take(TT, D)
        (sc_l, sh_l), (sc_c, sh_c) = modulation(0, 0, c("norm1_0"))
        norm_T(cx, [(hT, sc_c, sh_c)], 0, xs)
        norm_T(h, [(hT, sc_l, sh_l)], SEQ, xs)

        reset()
        T4 = 4
        uT = take(4, 512)
        vn = take(T4, 512)
        qT, kT = take(GH, 512), take(GH, 512)
        kt, vt = take(T4, GH * P), take(T4, GH * P)
        gT = take(GH, 512)
        mark_gdn = cur[0]
        settle()
        for n in range(2):
            feature_tile([2 * n, 2 * n + 1], hT, 0, 512)
            for i in range(2):
                @block.scalar
                def _(act):
                    act.wait_ge(tile_used.sem, tile_used.n)
                    act_done.by(nc.scalar.activation(uT[:, 2 * n + i, :], ps[:, 2 * n + i, :], ACT.Gelu))
                    freed[2 * n + i] = [(act_done, act_done.n)]
        token_rows([4, 5, 6, 7], hT, 0, KT)
        for t in range(T4):
            @block.scalar
            def _(act):
                act.wait_ge(tile_used.sem, tile_used.n)
                act_done.by(nc.scalar.activation(vn[:, t, :], ps[:, 4 + t, :], ACT.Gelu,
                                                 accum_out=small[:, 8 + t:9 + t]))
                freed[4 + t] = [(act_done, act_done.n)]

        @block.vector
        def _(dve):
            after_all(dve)
            link(dve, dve_done, nc.vector.tensor_scalar(small[:, 12:16], small[:, 8:12], 1.0 / 512, None, ALU.mult))
            for t in range(T4):
                link(dve, dve_done, nc.vector.tensor_scalar(vn[:, t, :], vn[:, t, :], small[:, 12 + t:13 + t],
                                                            None, ALU.subtract))

        scratch512 = take(512)

        @block.scalar
        def _(act):
            after_all(act)
            for t in range(T4):
                link(act, act_done, nc.scalar.activation(scratch512, vn[:, t, :], ACT.Square,
                                                         accum_out=small[:, 8 + t:9 + t]))
        rstd_of((8, 12), 512)

        @block.vector
        def _(dve):
            after_all(dve)
            for t in range(T4):
                link(dve, dve_done, nc.vector.scalar_tensor_tensor(vn[:, t, :], vn[:, t, :], small[:, 24 + t:25 + t],
                                                                   c("ln_g"), ALU.mult, ALU.mult))
                link(dve, dve_done, nc.vector.tensor_tensor(vn[:, t, :], vn[:, t, :], c("ln_b"), ALU.add))

        reset(mark_gdn)
        cb = take(2, 512)
        for n in range(6):
            feature_tile([0, 1], hT, 0, 512)
            for i in range(2):
                ft = 2 * n + i
                tap = lambda j: c("conv_qkv")[:, j * 12 + ft:j * 12 + ft + 1]
                seg = lambda x, a, b_: x.rearrange("p (s t) -> p s t", s=2)[:, :, a:b_]
                src, dst = ps[:, i, :], cb[:, i, :]

                @block.scalar
                def _(act):
                    after_all(act)
                    act_done.by(nc.scalar.activation(dst, src, ACT.Copy, scale=tap(1)))

                @block.vector
                def _(dve):
                    after_all(dve)
                    link(dve, dve_done, nc.vector.scalar_tensor_tensor(
                        seg(dst, 1, SEQ), seg(src, 0, SEQ - 1), tap(0), seg(dst, 1, SEQ), ALU.mult, ALU.add))
                    dve_done.by(nc.vector.scalar_tensor_tensor(
                        seg(dst, 0, SEQ - 1), seg(src, 1, SEQ), tap(2), seg(dst, 0, SEQ - 1), ALU.mult, ALU.add))
                    freed[i] = [(dve_done, dve_done.n)]
                kind, hh = ft // 4, ft % 4
                full = (qT, kT, cb)[kind]
                fv = full[:, hh, :] if kind < 2 else dst

                @block.scalar
                def _(act):
                    after_all(act)
                    link(act, act_done, nc.scalar.activation(fv, dst, ACT.Silu))
                if kind < 2:
                    @block.scalar
                    def _(act):
                        after_all(act)
                        link(act, act_done, nc.scalar.activation(dst, fv, ACT.Square))

                    @block.tensor
                    def _(pe):
                        after_all(pe)
                        pe_done.by(nc.tensor.matmul(ps[:, 2, :], ones, dst, start=True, stop=True))

                    @block.vector
                    def _(dve):
                        after_all(dve)
                        link(dve, dve_done, nc.vector.tensor_scalar(dst, ps[:, 2, :], EPS, None, ALU.add))
                        link(dve, dve_done, nc.vector.reciprocal(dst, dst))

                    @block.scalar
                    def _(act):
                        after_all(act)
                        act_done.by(nc.scalar.activation(dst, dst, ACT.Sqrt))

                    @block.vector
                    def _(dve):
                        after_all(dve)
                        dve_done.by(nc.vector.scalar_tensor_tensor(
                            fv, fv, float(P) ** -0.5 if kind == 0 else 1.0, dst, ALU.mult, ALU.mult))
                if kind > 0:
                    row = (kt, vt)[kind - 1]

                    @block.tensor
                    def _(pe):
                        after_all(pe)
                        for t in range(T4):
                            last = nc.tensor.transpose(ps[:, 3, t * P:t * P + P], fv[:, t * P:t * P + P], ident)
                        pe_done.by(last)

                    @block.vector
                    def _(dve):
                        after_all(dve)
                        dve_done.by(nc.vector.tensor_copy(row[:, :, hh * P:hh * P + P],
                                                          ps[:, 3, :].rearrange("p (t n) -> p t n", t=T4)))
        for n in range(2):
            feature_tile([4 + 2 * n, 5 + 2 * n], hT, 0, 512)
            for i in range(2):
                @block.scalar
                def _(act):
                    act.wait_ge(tile_used.sem, tile_used.n)
                    act_done.by(nc.scalar.activation(gT[:, 2 * n + i, :], ps[:, 4 + 2 * n + i, :], ACT.Silu))
                    freed[4 + 2 * n + i] = [(act_done, act_done.n)]
        reset(mark_gdn)
        abv = take(T4, 16)
        lal, beta, t8 = take(T4, 8), take(T4, 8), take(T4, 8)

        @block.tensor
        def _(pe):
            after_all(pe)
            wab = c("w_ab").rearrange("p (k n) -> p k n", k=KT)
            for t in range(T4):
                for k in range(KT):
                    last = nc.tensor.matmul(ps[:, 0, t * 16:t * 16 + 16], hT[:, k, t * P:t * P + P], wab[:, k, :],
                                            start=(k == 0), stop=(k == KT - 1))
            pe_done.by(last)

        bc8 = lambda x: x.unsqueeze(1).to_broadcast([P, T4, 8])

        @block.vector
        def _(dve):
            after_all(dve)
            link(dve, dve_done, nc.vector.tensor_copy(abv.rearrange("p t n -> p (t n)"), ps[:, 0, 0:64]))
            link(dve, dve_done, nc.vector.tensor_tensor(lal, abv[:, :, 0:8], bc8(c("dt_bias")), ALU.add))

        @block.scalar
        def _(act):
            after_all(act)
            link(act, act_done, nc.scalar.activation(t8, lal, ACT.Abs))
            link(act, act_done, nc.scalar.activation(t8, t8, ACT.Exp, scale=-1.0))
            link(act, act_done, nc.scalar.activation(t8, t8, ACT.Ln, bias=1.0))
            link(act, act_done, nc.scalar.activation(c("a_log"), c("a_log"), ACT.Exp))
            link(act, act_done, nc.scalar.activation(beta, abv[:, :, 8:16], ACT.Exp, scale=-1.0))

        @block.vector
        def _(dve):
            after_all(dve)
            link(dve, dve_done, nc.vector.scalar_tensor_tensor(lal, lal, 0.0, t8, ALU.max, ALU.add))
            link(dve, dve_done, nc.vector.tensor_tensor(lal, lal, bc8(c("a_log")), ALU.mult))
            link(dve, dve_done, nc.vector.tensor_scalar(lal, lal, -1.0, None, ALU.mult))
            link(dve, dve_done, nc.vector.tensor_scalar(beta, beta, 1.0, None, ALU.add))
            link(dve, dve_done, nc.vector.reciprocal(beta, beta))

        yT = hT
        for g in range(4):
            @block.tensor
            def _(pe):
                after_all(pe)
                for t in range(T4):
                    last = nc.tensor.matmul(ps[:, 1, t * P:t * P + P], vn[:, t, g * P:g * P + P],
                                            c("ws", g * P, g * P + P), start=True, stop=True)
                pe_done.by(last)

            @block.vector
            def _(dve):
                after_all(dve)
                bsr = c("bs", g * P, g * P + P).unsqueeze(1).to_broadcast([P, T4, P])
                yg = yT[:, g, :].rearrange("p (t n) -> p t n", t=T4)
                link(dve, dve_done, nc.vector.tensor_tensor(yg, ps[:, 1, :].rearrange("p (t n) -> p t n", t=T4),
                                                            bsr, ALU.add))
                link(dve, dve_done, nc.vector.tensor_tensor(yT[:, g, :], yT[:, g, :], uT[:, g, :], ALU.mult))

        osum = vn
        W = GH * P
        vec4 = lambda x: x.unsqueeze(2).to_broadcast([P, GH, P])
        as4 = lambda x: x.rearrange("p (h n) -> p h n", h=GH)
        At, X, TM, UM, attn, qg, r_, kdec, beb = (take(W) for _ in range(9))
        S, lab, DT, eg = (hT[:, 4 + n, :] for n in range(4))
        vnew = beb
        gc, bg, ed, ge = take(GH), take(GH), take(GH), take(GH)
        for d in range(2):
            tri = c(f"tri{d}")
            strict = c(f"strict{d}")
            end = P - 1 if d == 0 else 0

            @block.vector
            def _(dve):
                after_all(dve)
                dve_done.by(nc.vector.memset(S, 0.0))
            for T in ((0, 1, 2, 3), (1, 0, 3, 2))[d]:
                tok = slice(T * P, T * P + P)
                la4 = lal[:, T, 4 * d:4 * d + 4]
                be4 = beta[:, T, 4 * d:4 * d + 4]

                @block.vector
                def _(dve):
                    after_all(dve)
                    nc.vector.tensor_copy(as4(lab), vec4(la4))
                    dve_done.by(nc.vector.tensor_copy(as4(beb), vec4(be4)))

                @block.tensor
                def _(pe):
                    after_all(pe)
                    for hh in range(GH):
                        hs = slice(hh * P, hh * P + P)
                        nc.tensor.matmul(ps[:, 0, hs], lab[:, hs], tri, start=True, stop=True)
                        nc.tensor.matmul(ps[:, 1, hs], beb[:, hs], ident, start=True, stop=True)
                        nc.tensor.matmul(ps[:, 2, hs], kT[:, hh, tok], kT[:, hh, tok], start=True, stop=True)
                        nc.tensor.matmul(ps[:, 3, hs], kT[:, hh, tok], qT[:, hh, tok], start=True, stop=True)
                    pe_done.by(nc.tensor.matmul(ps[:, 4, 0:GH], tri, la4, start=True, stop=True))

                @block.vector
                def _(dve):
                    after_all(dve)
                    link(dve, dve_done, nc.vector.tensor_copy(gc, ps[:, 4, 0:GH]))
                    for hh in range(GH):
                        hs = slice(hh * P, hh * P + P)
                        nc.vector.tensor_scalar(DT[:, hs], ps[:, 0, hs], gc[:, hh:hh + 1], 0.0,
                                                ALU.subtract, ALU.min)
                    dve_done.by(nc.vector.tensor_tensor(ed, as4(ps[:, 0, :])[:, :, end], gc, ALU.subtract))

                @block.scalar
                def _(act):
                    after_all(act)
                    link(act, act_done, nc.scalar.activation(DT, DT, ACT.Exp))
                    link(act, act_done, nc.scalar.activation(eg, ps[:, 0, :], ACT.Exp))
                    link(act, act_done, nc.scalar.activation(bg, gc, ACT.Exp))
                    link(act, act_done, nc.scalar.activation(ed, ed, ACT.Exp))
                    link(act, act_done, nc.scalar.activation(ge, as4(ps[:, 0, :])[:, :, end], ACT.Exp))

                b4 = lambda m: m.unsqueeze(1).to_broadcast([P, GH, P])

                @block.vector
                def _(dve):
                    after_all(dve)
                    link(dve, dve_done, nc.vector.tensor_tensor(as4(DT), as4(DT), b4(tri), ALU.mult))
                    link(dve, dve_done, nc.vector.tensor_tensor(attn, ps[:, 3, :], DT, ALU.mult))
                    link(dve, dve_done, nc.vector.tensor_tensor(At, ps[:, 2, :], DT, ALU.mult))
                    link(dve, dve_done, nc.vector.tensor_tensor(At, At, ps[:, 1, :], ALU.mult))
                    link(dve, dve_done, nc.vector.tensor_tensor(as4(At), as4(At), b4(strict), ALU.mult))
                    link(dve, dve_done, nc.vector.tensor_tensor(as4(qg), qT[:, :, tok], as4(eg), ALU.mult))
                    link(dve, dve_done, nc.vector.tensor_tensor(bg, bg, be4, ALU.mult))
                    link(dve, dve_done, nc.vector.tensor_tensor(as4(kdec), as4(kt[:, T, :]), vec4(ed), ALU.mult))
                    link(dve, dve_done, nc.vector.tensor_tensor(as4(X), as4(At), b4(c(f"lev{d}_0")), ALU.mult))
                    link(dve, dve_done, nc.vector.tensor_tensor(as4(UM), b4(ident), as4(X), ALU.subtract))

                @block.tensor
                def _(pe):
                    after_all(pe)
                    for hh in range(GH):
                        hs = slice(hh * P, hh * P + P)
                        last = nc.tensor.matmul(ps[:, 5, hs], X[:, hs], ident, start=True, stop=True)
                    pe_done.by(last)

                @block.vector
                def _(dve):
                    after_all(dve)
                    dve_done.by(nc.vector.tensor_tensor(as4(TM), b4(ident), as4(ps[:, 5, :]), ALU.subtract))

                for lev in range(1, 7):
                    @block.vector
                    def _(dve):
                        after_all(dve)
                        dve_done.by(nc.vector.tensor_tensor(as4(X), as4(At), b4(c(f"lev{d}_{lev}")), ALU.mult))

                    @block.tensor
                    def _(pe):
                        after_all(pe)
                        for hh in range(GH):
                            hs = slice(hh * P, hh * P + P)
                            last = nc.tensor.matmul(ps[:, 5, hs], X[:, hs], TM[:, hs], start=True, stop=True)
                        pe_done.by(last)

                    @block.scalar
                    def _(act):
                        after_all(act)
                        act_done.by(nc.scalar.activation(X, ps[:, 5, :], ACT.Copy))

                    @block.tensor
                    def _(pe):
                        after_all(pe)
                        for hh in range(GH):
                            hs = slice(hh * P, hh * P + P)
                            last = nc.tensor.matmul(ps[:, 6, hs], X[:, hs], UM[:, hs], start=True, stop=True)
                            if lev < 6:
                                last = nc.tensor.matmul(ps[:, 7, hs], UM[:, hs], X[:, hs], start=True, stop=True)
                        pe_done.by(last)

                    @block.vector
                    def _(dve):
                        after_all(dve)
                        dve_done.by(nc.vector.tensor_tensor(UM, UM, ps[:, 6, :], ALU.subtract))
                        if lev < 6:
                            dve_done.by(nc.vector.tensor_tensor(TM, TM, ps[:, 7, :], ALU.subtract))

                @block.tensor
                def _(pe):
                    after_all(pe)
                    for hh in range(GH):
                        hs = slice(hh * P, hh * P + P)
                        last = nc.tensor.matmul(ps[:, 0, hs], kT[:, hh, tok], S[:, hs], start=True, stop=True)
                    pe_done.by(last)

                @block.vector
                def _(dve):
                    after_all(dve)
                    link(dve, dve_done, nc.vector.tensor_tensor(as4(lab), as4(ps[:, 0, :]), vec4(bg), ALU.mult))
                    link(dve, dve_done, nc.vector.tensor_tensor(as4(r_), as4(vt[:, T, :]), vec4(be4), ALU.mult))
                    link(dve, dve_done, nc.vector.tensor_tensor(r_, r_, lab, ALU.subtract))

                @block.tensor
                def _(pe):
                    after_all(pe)
                    for hh in range(GH):
                        hs = slice(hh * P, hh * P + P)
                        last = nc.tensor.matmul(ps[:, 1, hs], UM[:, hs], r_[:, hs], start=True, stop=True)
                    pe_done.by(last)

                @block.scalar
                def _(act):
                    after_all(act)
                    act_done.by(nc.scalar.activation(vnew, ps[:, 1, :], ACT.Copy))

                @block.tensor
                def _(pe):
                    after_all(pe)
                    for hh in range(GH):
                        hs = slice(hh * P, hh * P + P)
                        nc.tensor.matmul(ps[:, 2, hs], qg[:, hs], S[:, hs], start=True, stop=False)
                        nc.tensor.matmul(ps[:, 2, hs], attn[:, hs], vnew[:, hs], start=False, stop=True)
                        last = nc.tensor.matmul(ps[:, 3, hs], kdec[:, hs], vnew[:, hs], start=True, stop=True)
                    pe_done.by(last)

                @block.vector
                def _(dve):
                    after_all(dve)
                    if d == 0:
                        dve_done.by(nc.vector.tensor_copy(osum[:, T, :], ps[:, 2, :]))
                    else:
                        dve_done.by(nc.vector.tensor_tensor(osum[:, T, :], osum[:, T, :], ps[:, 2, :], ALU.add))
                    link(dve, dve_done, nc.vector.tensor_tensor(as4(S), as4(S), vec4(ge), ALU.mult))
                    link(dve, dve_done, nc.vector.tensor_tensor(S, S, ps[:, 3, :], ALU.add))

        @block.scalar
        def _(act):
            after_all(act)
            for t in range(T4):
                for hh in range(GH):
                    link(act, act_done, nc.scalar.activation(X[:, 0:P], osum[:, t, hh * P:hh * P + P], ACT.Square,
                                                             accum_out=small[:, 8 + 4 * t + hh:9 + 4 * t + hh]))

        @block.vector
        def _(dve):
            after_all(dve)
            link(dve, dve_done, nc.vector.tensor_scalar(small[:, 24:40], small[:, 8:24], 1.0 / P, EPS,
                                                        ALU.mult, ALU.add))

        @block.gpsimd
        def _(pool):
            after_all(pool)
            inverse_root(pool, small[:, 8:24], small[:, 24:40])

        @block.vector
        def _(dve):
            after_all(dve)
            for t in range(T4):
                ins = nc.vector.tensor_tensor(as4(osum[:, t, :]), as4(osum[:, t, :]),
                                              vec4(small[:, 8 + 4 * t:12 + 4 * t]), ALU.mult)
            dve_done.by(ins)
        for hh in range(GH):
            @block.tensor
            def _(pe):
                after_all(pe)
                for t in range(T4):
                    last = nc.tensor.transpose(ps[:, hh, t * P:t * P + P], osum[:, t, hh * P:hh * P + P], ident)
                pe_done.by(last)

            @block.vector
            def _(dve):
                after_all(dve)
                dve_done.by(nc.vector.scalar_tensor_tensor(yT[:, 4 + hh, :], ps[:, hh, :], c("b_norm"),
                                                           gT[:, hh, :], ALU.mult, ALU.mult))

        def gated_out(layer, which, src, ntt, kt_):
            rows = take(2, D)
            scr = take(4, 512)
            gate_rows(layer, which, rows, (0, 1) if ntt == 4 else (0,))
            settle()
            strm = (lambda t: (cx if t < 2 else h)[:, t % 2, :]) if ntt == 4 else (lambda t: h[:, t, :])
            gt = (lambda t: rows[:, 1 if t < 2 else 0, :]) if ntt == 4 else (lambda t: rows[:, 0, :])
            for n in range(2):
                banks = [(4 * n + i) for i in range(ntt)]
                token_rows(banks, src, 0, kt_)
                add_rows(banks, strm, n, gt, scr)

        reset()
        gated_out(0, 0, yT, 4, KT)

        conv_centre = sem("conv_centre")
        conv_side = sem("conv_side")
        conv_silu = sem("conv_silu")
        conv_hid = sem("conv_hid")
        conv_left = sem("conv_left")
        cc = {"n": 0}

        @block.vector
        def _(dve):
            dve.sem_inc(conv_side, 2 * RING)
            dve.sem_inc(conv_hid, RING)

        def conv_feed_forward(layer, ntok):
            nf = F_FFN
            segs = ntok // SEQ
            hid = take(nf, ntok)
            cg, cu = take(3, ntok), take(3, ntok)
            t0, c0 = tile_used.n, cc["n"]
            slot = lambda k: (t0 + k) % RING
            looped = nf // RING
            wofs = where["conv_ffn"][0] + layer * 3 * 2 * nf
            tap = lambda j, half, g, s: par[:, bass.ds(g * RING + (wofs + (j * 2 + half) * nf + s), 1)]
            seg = lambda x, a, b_: x.rearrange("p (s t) -> p s t", s=segs)[:, :, a:b_]

            @block.tensor
            def _(pe):
                after_all(pe)

                def up(g, s):
                    pe.wait_ge(landed[slot(s)], g * 16 + 16 * ((t0 + s) // RING + 1))
                    w = ring[:, slot(s), :].rearrange("p (k n) -> p k n", k=KT)
                    pe.wait_ge(conv_side, g * (2 * RING) + 2 * (RING + c0 + s - since(BANKS_CONV, s) + 1))
                    for half in range(2):
                        for k in range(KT):
                            last = nc.tensor.matmul(ps[:, 2 * BANKS_CONV[s] + half, 0:ntok],
                                                    w[:, k, half * P:half * P + P], hT[:, k, 0:ntok],
                                                    start=(k == 0), stop=(k == KT - 1))
                    last.then_inc(tile_used.sem, 1)
                turns(pe, nf, looped, up)

            @block.scalar
            def _(act):
                after_all(act)

                def gate(g, s):
                    b = BANKS_CONV[s]
                    act.wait_ge(tile_used.sem, g * RING + (t0 + s + 1))
                    act.wait_ge(conv_hid, g * RING + (RING + c0 + s - since(BANKS_CONV, s) + 1))
                    for half, buf in enumerate((cg, cu)):
                        nc.scalar.activation(buf[:, b, :], ps[:, 2 * b + half, 0:ntok], ACT.Copy,
                                             scale=tap(1, half, g, s)).then_inc(conv_centre, 1)
                    act.wait_ge(conv_side, g * (2 * RING) + 2 * (RING + c0 + s + 1))
                    nc.scalar.activation(cg[:, b, :], cg[:, b, :], ACT.Silu).then_inc(conv_silu, 1)
                turns(act, nf, looped, gate)

            @block.vector
            def _(dve):
                after_all(dve)

                def hidden(g, s):
                    b = BANKS_CONV[s]
                    dve.wait_ge(conv_centre, g * (2 * RING) + 2 * (c0 + s + 1))
                    for half, buf in enumerate((cg, cu)):
                        x, o = ps[:, 2 * b + half, 0:ntok], buf[:, b, :]
                        nc.vector.scalar_tensor_tensor(seg(o, 1, SEQ), seg(x, 0, SEQ - 1), tap(0, half, g, s),
                                                       seg(o, 1, SEQ), ALU.mult, ALU.add).then_inc(conv_left, 1)
                    dve.wait_ge(conv_left, g * (2 * RING) + 2 * (c0 + s + 1))
                    for half, buf in enumerate((cg, cu)):
                        x, o = ps[:, 2 * b + half, 0:ntok], buf[:, b, :]
                        nc.vector.scalar_tensor_tensor(seg(o, 0, SEQ - 1), seg(x, 1, SEQ), tap(2, half, g, s),
                                                       seg(o, 0, SEQ - 1), ALU.mult, ALU.add).then_inc(conv_side, 1)
                    dve.wait_ge(conv_side, g * (2 * RING) + 2 * (RING + c0 + s + 1))
                    dve.wait_ge(conv_silu, g * RING + (c0 + s + 1))
                    nc.vector.tensor_tensor(hid[:, g * RING + s, :], cg[:, b, :], cu[:, b, :],
                                            ALU.mult).then_inc(conv_hid, 1)
                turns(dve, nf, looped, hidden)
                dve.wait_ge(conv_hid, RING + c0 + nf)
                dve_done.by(nc.vector.tensor_copy(small[:, 480:481], small[:, 481:482]))
            tile_used.n += nf
            cc["n"] += nf
            for b in range(8):
                freed[b] = [(dve_done, dve_done.n)]
            return hid

        def second_ffn(layer, both):
            nonlocal hT
            reset()
            xs = take(TT, D)
            (sc_l, sh_l), (sc_c, sh_c) = modulation(layer, 1, c(f"norm2_{layer}"))
            if both:
                norm_T(cx, [(hT, sc_c, sh_c)], 0, xs)
            norm_T(h, [(hT, sc_l, sh_l)], SEQ if both else 0, xs)
            reset()
            hid = conv_feed_forward(layer, 512 if both else 256)
            gated_out(layer, 1, hid, 4 if both else 2, F_FFN)

        second_ffn(0, True)

        reset()
        xs = take(TT, D)
        (sc_l, sh_l), (sc_c, sh_c) = modulation(1, 0, c("norm1_1"))
        norm_T(cx, [(hT, sc_c, sh_c)], 0, xs)
        norm_T(h, [(hT, sc_l, sh_l)], SEQ, xs)
        reset()
        zkv = take(T4, 320)
        zq = take(TT, 384)
        kr2 = take(T4, P)
        ckvT = take(2, 512)
        krT = take(512)
        cqT = take(3, SEQ)
        settle()
        token_rows([0, 1, 2, 3], hT, 0, KT, cols=320)
        for t in range(T4):
            copy_bank(t, zkv[:, t, :], slice(0, 320))
        token_rows([4, 5], hT, SEQ, KT, cols=384)
        for t in range(TT):
            copy_bank(4 + t, zq[:, t, :], slice(0, 384))

        mark = cur[0]
        sq = take(384)

        @block.scalar
        def _(act):
            after_all(act)
            for t in range(T4):
                link(act, act_done, nc.scalar.activation(sq[:, 0:256], zkv[:, t, 0:256], ACT.Square,
                                                         accum_out=small[:, 8 + t:9 + t]))
            for t in range(TT):
                link(act, act_done, nc.scalar.activation(sq, zq[:, t, :], ACT.Square,
                                                         accum_out=small[:, 12 + t:13 + t]))
        rstd_of((8, 12), 256)
        rstd_of((12, 14), 384)

        def rotate(dve, dst, src, t, n, a_, b_):
            cos = c("cos", 32 * t, 32 * t + 32).unsqueeze(1).to_broadcast([P, n, 32])
            sin = c("sin", 32 * t, 32 * t + 32).unsqueeze(1).to_broadcast([P, n, 32])
            x1, x2 = src[:, :, 0:32], src[:, :, 32:64]
            nc.vector.tensor_tensor(a_, x1, cos, ALU.mult)
            link(dve, dve_done, nc.vector.tensor_tensor(b_, x2, sin, ALU.mult))
            link(dve, dve_done, nc.vector.tensor_tensor(dst[:, :, 0:32], a_, b_, ALU.subtract))
            nc.vector.tensor_tensor(a_, x2, cos, ALU.mult)
            link(dve, dve_done, nc.vector.tensor_tensor(b_, x1, sin, ALU.mult))
            link(dve, dve_done, nc.vector.tensor_tensor(dst[:, :, 32:64], a_, b_, ALU.add))

        ra, rb = take(8, 32), take(8, 32)

        @block.vector
        def _(dve):
            after_all(dve)
            for t in range(T4):
                link(dve, dve_done, nc.vector.tensor_scalar(zkv[:, t, 0:256], zkv[:, t, 0:256],
                                                            small[:, 24 + t:25 + t], None, ALU.mult))
                kr = zkv[:, t, 256:320].unsqueeze(1)
                if t < 2:
                    link(dve, dve_done, nc.vector.tensor_copy(kr2[:, t, 0:64], zkv[:, t, 256:320]))
                else:
                    rotate(dve, kr2[:, t, 0:64].unsqueeze(1), kr, t - 2, 1, ra[:, 0:1, :], rb[:, 0:1, :])
                link(dve, dve_done, nc.vector.tensor_copy(kr2[:, t, 64:128], kr2[:, t, 0:64]))
            for t in range(TT):
                link(dve, dve_done, nc.vector.tensor_scalar(zq[:, t, :], zq[:, t, :],
                                                            small[:, 28 + t:29 + t], None, ALU.mult))

        @block.tensor
        def _(pe):
            after_all(pe)
            for t in range(T4):
                for k in range(2):
                    nc.tensor.transpose(ps[:, k, t * P:t * P + P], zkv[:, t, k * P:k * P + P], ident)
                last = nc.tensor.transpose(ps[:, 2, t * P:t * P + P], kr2[:, t, :], ident)
            for t in range(TT):
                for k in range(3):
                    last = nc.tensor.transpose(ps[:, 3 + k, t * P:t * P + P], zq[:, t, k * P:k * P + P], ident)
            pe_done.by(last)

        @block.vector
        def _(dve):
            after_all(dve)
            for k in range(2):
                nc.vector.tensor_scalar(ckvT[:, k, :], ps[:, k, :], c("kv_n")[:, k:k + 1], None, ALU.mult)
            nc.vector.tensor_copy(krT, ps[:, 2, :])
            for k in range(3):
                last = nc.vector.tensor_scalar(cqT[:, k, :], ps[:, 3 + k, 0:SEQ], c("q_n")[:, k:k + 1], None,
                                               ALU.mult)
            dve_done.by(last)

        reset(mark)
        qnT = take(MH, SEQ)
        qr = take(TT, 512)
        qrT = take(4, SEQ)
        ra, rb = take(8, 32), take(8, 32)
        knT = hT.rearrange("p k t -> p (k t)").rearrange("p (h t) -> p h t", h=MH)
        v = take(T4, D)
        pp = take(512)
        pT = take(4, SEQ)
        oT = take(MH, SEQ)
        settle()
        for n in range(2):
            @block.tensor
            def _(pe):
                w = weights(pe).rearrange("p (k n) -> p k n", k=4)
                claim(pe, 6, 7)
                for i in range(4):
                    for k in range(3):
                        last = nc.tensor.matmul(ps[:, 6 + i // 2, (i % 2) * SEQ:(i % 2) * SEQ + SEQ],
                                                w[:, k, i * P:i * P + P], cqT[:, k, :],
                                                start=(k == 0), stop=(k == 2))
                tile_used.by(last)
            for i in range(2):
                copy_bank(6 + i, qnT[:, 4 * n + 2 * i:4 * n + 2 * i + 2, :].rearrange("p h t -> p (h t)"))
        token_rows([0, 1], cqT, 0, 3)

        @block.vector
        def _(dve):
            after_all(dve)
            for t in range(TT):
                rotate(dve, qr[:, t, :].rearrange("p (h n) -> p h n", h=8),
                       ps[:, t, :].rearrange("p (h n) -> p h n", h=8), t, 8, ra, rb)

        @block.tensor
        def _(pe):
            after_all(pe)
            for k in range(4):
                for t in range(TT):
                    last = nc.tensor.transpose(ps[:, 2 + k // 2, (k % 2) * SEQ + t * P:(k % 2) * SEQ + t * P + P],
                                               qr[:, t, k * P:k * P + P], ident)
            pe_done.by(last)

        @block.vector
        def _(dve):
            after_all(dve)
            dve_done.by(nc.vector.tensor_copy(qrT.rearrange("p k t -> p (k t)"), ps[:, 2:4, :]))
        settle()

        @block.tensor
        def _(pe):
            w = weights(pe).rearrange("p (k n) -> p k n", k=2)
            for i in range(MH):
                for k in range(2):
                    last = nc.tensor.matmul(ps[:, i, :], w[:, k, i * P:i * P + P], ckvT[:, k, :],
                                            start=(k == 0), stop=(k == 1))
            tile_used.by(last)
        for i in range(MH):
            copy_bank(i, knT[:, i, :])

        @block.tensor
        def _(pe):
            w = weights(pe).rearrange("p (k n) -> p k n", k=2)
            claim(pe, *range(8))
            for t in range(T4):
                for n in range(2):
                    for k in range(2):
                        last = nc.tensor.matmul(ps[:, 2 * t + n, :], ckvT[:, k, t * P:t * P + P],
                                                w[:, k, n * 512:n * 512 + 512], start=(k == 0), stop=(k == 1))
            tile_used.by(last)
        for t in range(T4):
            for n in range(2):
                copy_bank(2 * t + n, v[:, t, n * 512:n * 512 + 512])
        scale = float(128 + 64) ** -0.5
        for hh in range(MH):
            ro = 64 * (hh % 2)
            for t in range(TT):
                @block.tensor
                def _(pe):
                    after_all(pe)
                    nc.tensor.matmul(ps[:, t, :], qnT[:, hh, t * P:t * P + P], knT[:, hh, :], start=True, stop=False)
                    pe_done.by(nc.tensor.matmul(ps[:, t, :], qrT[ro:ro + 64, hh // 2, t * P:t * P + P],
                                                krT[ro:ro + 64, :], start=False, stop=True))

                @block.vector
                def _(dve):
                    after_all(dve)
                    link(dve, dve_done, nc.vector.reduce_max(small[:, 40:41], ps[:, t, :], AXX))
                    link(dve, dve_done, nc.vector.tensor_scalar(small[:, 41:42], small[:, 40:41], -scale, None,
                                                                ALU.mult))

                @block.scalar
                def _(act):
                    after_all(act)
                    act_done.by(nc.scalar.activation(pp, ps[:, t, :], ACT.Exp, bias=small[:, 41:42], scale=scale,
                                                     accum_out=small[:, 42:43]))

                @block.vector
                def _(dve):
                    after_all(dve)
                    link(dve, dve_done, nc.vector.reciprocal(small[:, 43:44], small[:, 42:43]))
                    link(dve, dve_done, nc.vector.tensor_scalar(pp, pp, small[:, 43:44], None, ALU.mult))

                @block.tensor
                def _(pe):
                    after_all(pe)
                    for j in range(T4):
                        last = nc.tensor.transpose(ps[:, 2, j * P:j * P + P], pp[:, j * P:j * P + P], ident)
                    pe_done.by(last)

                @block.vector
                def _(dve):
                    after_all(dve)
                    dve_done.by(nc.vector.tensor_copy(pT[:, :, t * P:t * P + P],
                                                      ps[:, 2, :].rearrange("p (j n) -> p j n", j=T4)))

            @block.tensor
            def _(pe):
                after_all(pe)
                for j in range(T4):
                    last = nc.tensor.matmul(ps[:, 3, 0:SEQ], v[:, j, hh * P:hh * P + P], pT[:, j, :],
                                            start=(j == 0), stop=(j == T4 - 1))
                pe_done.by(last)

            @block.vector
            def _(dve):
                after_all(dve)
                dve_done.by(nc.vector.tensor_copy(oT[:, hh, :], ps[:, 3, 0:SEQ]))

        @block.vector
        def _(dve):
            after_all(dve)
            dve_done.by(nc.vector.tensor_copy(hT[:, :, 0:SEQ], oT))
        reset()
        for eng in (block.vector, block.tensor):
            @eng
            def _(e):
                after_all(e)
        gated_out(1, 0, hT, 2, KT)
        second_ffn(1, False)
        final_norm(c("final2"))
        assert tile_used.n == n_tiles, (tile_used.n, n_tiles)

        @block.sync
        def _(sp):
            load_turns(sp, moe_turn, n_tiles // RING)
            for t in range(n_tiles // RING * RING, n_tiles):
                sp.wait_ge(tile_used.sem, t - RING + 1)
                sp.dma_start(ring[:, t % RING, :], stream[t]).then_inc(landed[t % RING], 16)
            sp.wait_ge(dve_done.sem, dve_done.n)
            for t in range(TT):
                sp.dma_start(out["out"][t * P:t * P + P, :], h[:, t, :]).then_inc(stored, 16)
            sp.wait_ge(stored, 16 * TT)




def weight_stream(i):
    tiles = []

    def features(w, *firsts):
        w8 = w.reshape(KT, P, -1)
        t = np.stack([w8[:, :, f:f + P] for f in firsts], axis=2)
        tiles.append(t.transpose(1, 0, 2, 3).reshape(P, TILE))

    def rows(w, col, cols=512, kper=4):
        k = w.shape[0] // P
        wide = TILE // kper
        wk = w.reshape(k, P, -1)[:, :, col:col + cols]
        for k0 in range(0, k, kper):
            t = np.zeros((kper, P, wide), np.float32)
            part = wk[k0:k0 + kper]
            t[:part.shape[0], :, :part.shape[2]] = part
            tiles.append(t.transpose(1, 0, 2).reshape(P, TILE))

    def span(w, a, b):
        for n in range(a, b, 2 * P):
            features(w, n, n + P)

    def both_halves(w):
        rows(w, 0)
        rows(w, 512)

    for layer in range(2):
        span(i["ada_w_2"][layer], 0, 6 * D)
    w = i["gla_w_in"][0]
    span(w, 0, 1024)
    rows(w, 1024), rows(w, 1536)
    span(w, 2064, 3088)
    both_halves(i["gla_w_out"][0])
    g, u = i["ffn_w_gate"][0], i["ffn_w_up"][0]
    gu = np.concatenate([g, u], axis=1)
    for f in range(F_FFN):
        features(gu, f * P, FF + f * P)
    both_halves(i["ffn_w_down"][0])
    span(i["sb_w_kv"], 0, 1024)
    rows(i["sb_w_kv"], 1024), rows(i["sb_w_kv"], 1536)
    span(i["sb_w_q"][0], 0, 1024)
    both_halves(i["sb_w_out"][0])
    for e in range(EXPERTS):
        gu = np.concatenate([i["moe_w_gate"][0, e], i["moe_w_up"][0, e]], axis=1)
        for f in range(F_MOE):
            features(gu, f * P, F_MOE * P + f * P)
        both_halves(i["moe_w_down"][0, e])
    w = i["ab_w_in_2"][0]
    span(w, 0, 512)
    rows(w, 512)
    span(w, 1024, 2560)
    span(w, 2560, 3072)
    both_halves(i["ab_w_out_2"][0])

    def conv_ffn(layer):
        for f in range(F_FFN):
            features(i["ffn_w_up_2"][layer], f * P, FF + f * P)
        both_halves(i["ffn_w_down_2"][layer])

    conv_ffn(0)
    w = i["mla_w_in_2"][0]
    rows(w, 384, 320)
    rows(w, 0, 384)
    uq = i["mla_w_uq_2"][0].reshape(384, MH, 192)
    nope = uq[:, :, 0:128].reshape(384, MH * 128)
    rows(nope, 0), rows(nope, 512)
    rows(uq[:, :, 128:192].reshape(384, MH * 64), 0)
    ukv = i["mla_w_ukv_2"][0].reshape(256, MH, 256)
    rows(ukv[:, :, 0:128].reshape(256, D), 0, D, 2)
    rows(ukv[:, :, 128:256].reshape(256, D), 0, D, 2)
    both_halves(i["mla_w_out_2"][0])
    conv_ffn(1)
    return np.stack(tiles)


def parameters(i):
    out = {}
    f32 = np.float32

    def col(v):
        return v.reshape(-1, P).T

    def rep(v):
        return np.broadcast_to(v.reshape(1, -1), (P, v.size))

    def padded(a):
        z = np.zeros((P, a.shape[1]), f32)
        z[:a.shape[0]] = a
        return z

    def ktiles(w):
        return w.reshape(KT, P, -1).transpose(1, 0, 2).reshape(P, -1)

    r = np.arange(P)
    out["ident"] = np.eye(P, dtype=f32)
    out["ones"] = np.ones((P, P), f32)
    out["minus"] = -np.ones((P, P), f32)
    out["attn0"], out["attn1"] = col(i["attn_norm"][0]), col(i["attn_norm"][1])
    out["ffn0"], out["ffn1"] = col(i["ffn_norm"][0]), col(i["ffn_norm"][1])
    out["kvn"] = col(i["kv_norm"])
    for layer in range(2):
        out[f"norm1_{layer}"] = col(i["norm1_g_2"][layer])
        out[f"norm2_{layer}"] = col(i["norm2_g_2"][layer])
    out["gla_head"] = col(i["gla_head_norm"][0])
    out["b_norm"] = col(i["b_norm_g_2"][0])
    out["q_n"], out["kv_n"] = col(i["mla_q_norm_g_2"][0]), col(i["mla_kv_norm_g_2"][0])
    b = i["ada_b_2"].reshape(2 * 48, P).T
    out["ada_b"] = np.repeat(b, 2, axis=1)
    out["cond"] = np.stack([i["c_2"][0], i["c_ctx_2"]], axis=1).reshape(KT, P, 2).transpose(1, 0, 2).reshape(P, -1)
    out["w_glr"] = ktiles(i["gla_w_in"][0][:, 2048:2064])
    out["gate_up"] = padded(i["gla_w_gate_up"][0])
    out["gate_b"] = padded(i["gla_b_gate"])
    same = (r[:, None] // CHUNK) == (r[None, :] // CHUNK)
    out["gla_mask"] = (same & (r[:, None] <= r[None, :])).astype(f32)
    out["gla_sum"] = out["gla_mask"] / f32(16)
    out["router"] = ktiles(i["moe_w_router"][0])
    slots = np.arange(P, dtype=f32)
    slots[CAP:] = -1
    out["slots"] = rep(slots)
    out["iota8"] = rep(np.arange(8, dtype=f32))
    t = np.arange(SEQ)
    out["sb_mask"] = np.concatenate([(r[:, None] + P * j < t[None, :]) for j in range(TT)], axis=1).astype(f32)
    out["sb_later"] = -(r[:, None] > r[None, :]).astype(f32)
    out["w_ab"] = ktiles(i["ab_w_in_2"][0][:, 3072:3088])
    out["ln_g"], out["ln_b"] = rep(i["a_ln_g_2"][0]), rep(i["a_ln_b_2"][0])
    out["ws"] = i["a_ws_2"][0].transpose(2, 0, 1).reshape(P, -1)
    out["bs"] = rep(i["a_bs_2"][0])
    out["conv_qkv"] = i["b_conv_w_2"][0].reshape(3 * 12, P).T
    out["conv_ffn"] = i["ffn_conv_w_2"].reshape(2 * 3 * 2 * F_FFN, P).T
    out["a_log"], out["dt_bias"] = rep(i["b_a_log_2"][0]), rep(i["b_dt_bias_2"][0])
    out["final1"], out["final2"] = rep(i["final_norm"]), rep(i["final_g_2"])
    j, k = r[:, None], r[None, :]
    for d in range(2):
        before = (j < k) if d == 0 else (j > k)
        out[f"tri{d}"] = (before | (j == k)).astype(f32)
        out[f"strict{d}"] = before.astype(f32)
        for lev in range(7):
            s = 1 << lev
            out[f"lev{d}_{lev}"] = (before & (j // (2 * s) == k // (2 * s)) & (j // s != k // s)).astype(f32)
    rows_, grid = SEQ // 64, 64
    row = np.repeat(np.arange(rows_, dtype=f32), grid)
    colv = np.tile(np.arange(grid, dtype=f32), rows_)
    inv = (f32(10000.0) ** (-np.arange(16, dtype=f32) / f32(16))).astype(f32)
    ang = np.concatenate([row[:, None] * inv, colv[:, None] * inv], axis=-1)
    out["cos"] = np.cos(ang).astype(f32).reshape(TT, P, 32).transpose(1, 0, 2).reshape(P, -1)
    out["sin"] = np.sin(ang).astype(f32).reshape(TT, P, 32).transpose(1, 0, 2).reshape(P, -1)
    where, at = {}, 0
    for name, a in out.items():
        where[name] = (at, a.shape[1])
        at += a.shape[1]
    return np.concatenate(list(out.values()), axis=1).astype(f32), where


def kernel(**inputs):
    import concourse.bacc as _bacc
    from concourse.bass_utils import run_bass_kernel_spmd as _run

    i = {k: np.asarray(v) for k, v in inputs.items()}
    par, where = parameters(i)
    arrays = {
        "in_stream": weight_stream(i),
        "in_params": np.ascontiguousarray(par),
        "in_x": np.ascontiguousarray(i["x"][0]),
        "in_ctx": np.ascontiguousarray(i["ctx_2"][0]),
    }
    nc = _bacc.Bacc("TRN2", target_bir_lowering=False, num_devices=1)
    aps = {n: nc.dram_tensor(n, a.shape, F32, kind="ExternalInput").ap() for n, a in arrays.items()}
    out = nc.dram_tensor("out_0", (SEQ, D), F32, kind="ExternalOutput").ap()
    build(nc, aps["in_stream"], aps["in_params"], where,
          {"x": aps["in_x"], "ctx": aps["in_ctx"], "out": out})
    r = _run(nc, [arrays], core_ids=[0])
    return r.results[0]["out_0"].reshape(1, SEQ, D)
```

```python
from contextlib import ExitStack

import numpy as np

import concourse.bass as bass
from concourse import mybir

F32 = mybir.dt.float32
U32 = mybir.dt.uint32
ALU = mybir.AluOpType
ACT = mybir.ActivationFunctionType
AXX = mybir.AxisListType.X

P = 128
D = 1024
KT = D // P
SEQ = 256
TT = SEQ // P
TILE = 2048
RING = 7
CHUNK = 64
H1, DV1 = 4, 256
SBH = 8
EXPERTS = 8
F_MOE = 3584 // P
TILES = 547
F_FFN = 2816 // P
FF = 2816
EPS = 1e-6
CAP = P
GH = 4
MH = 8
BANKS_PLAIN = [0, 1, 2, 3, 0, 1, 2]
BANKS_CONV = [0, 1, 2, 0, 1, 2, 1]


def since(pattern, s):
    n = len(pattern)
    return next(d for d in range(1, n + 1) if pattern[(s - d) % n] == pattern[s])


class Done:

    def __init__(self, sem, chain):
        self.sem, self.n, self.chain = sem, 0, chain

    def by(self, ins):
        ins.then_inc(self.sem, 1)
        self.n += 1
        self.chain[-1][self] = self.n
        return self.n


def build(nc, stream, params, where, out):
    order = []
    n_tiles = stream.shape[0]
    width = params.shape[1]
    with ExitStack() as ctx:
        def sb(name, shape, dt=F32):
            return ctx.enter_context(nc.sbuf_tensor(name, shape, dt))

        def sem(name):
            return ctx.enter_context(nc.semaphore(name))

        ring = sb("ring", [P, RING, TILE])
        par = sb("par", [P, width])
        h = sb("h", [P, TT, D])
        cx = sb("cx", [P, TT, D])
        hT = sb("hT", [P, KT, 2 * SEQ])
        ARENA = 19968
        arena = sb("arena", [P, ARENA])
        ada = sb("ada", [P, 2, 48, 2])
        small = sb("small", [P, 512])
        ps = ctx.enter_context(nc.psum_tensor("ps", [P, 8, 512], F32))

        landed = [sem(f"landed{i}") for i in range(RING)]
        params_in = sem("params_in")
        rest_in = sem("rest_in")
        x_in = sem("x_in")
        stored = sem("stored")
        chain = [{}]
        tile_used = Done(sem("tile_used"), chain)
        pe_done = Done(sem("pe_done"), chain)
        act_done = Done(sem("act_done"), chain)
        dve_done = Done(sem("dve_done"), chain)
        pool_done = Done(sem("pool_done"), chain)
        everyone = (tile_used, pe_done, act_done, dve_done, pool_done)

        def after_all(eng):
            for d in everyone:
                n = d.n if len(chain) == 1 else chain[-1].get(d, 0)
                if n and not (len(chain) > 1 and eng.engine == nc.tensor.engine and d in (tile_used, pe_done)):
                    eng.wait_ge(d.sem, n)

        def side_by_side(chains):
            before = {d: d.n for d in everyone}
            running = [(g, dict(before)) for g in chains]
            while running:
                for g, own in list(running):
                    chain.append(own)
                    if next(g, "end") == "end":
                        running.remove((g, own))
                    chain.pop()

        def link(eng, done, ins):
            eng.wait_ge(done.sem, done.by(ins))

        def c(name, a=0, b=None):
            off, n = where[name]
            return par[:, off + a:off + (n if b is None else b)]

        cur = [0]

        def reset(at=0):
            cur[0] = at

        def take(*shape):
            n = int(np.prod(shape))
            assert cur[0] + n <= ARENA, (cur[0], n)
            v = arena[:, cur[0]:cur[0] + n]
            cur[0] += n
            if len(shape) == 2:
                v = v.rearrange("p (a b) -> p a b", a=shape[0])
            if len(shape) == 3:
                v = v.rearrange("p (a b c) -> p a b c", a=shape[0], b=shape[1])
            return v

        ident, ones = c("ident"), c("ones")
        block = ctx.enter_context(nc.Block())

        @block.sync
        def _(sp):
            first = where["first"]
            sp.dma_start(par[:, 0:first], params[:, 0:first]).then_inc(params_in, 16)
            for t in range(RING):
                sp.dma_start(ring[:, t, :], stream[t]).then_inc(landed[t], 16)
            sp.dma_start(par[:, first:width], params[:, first:width]).then_inc(rest_in, 16)
            for t in range(TT):
                sp.dma_start(cx[:, t, :], out["ctx"][t * P:t * P + P, :]).then_inc(rest_in, 16)

        def load_turns(sp, first, end):
            with sp.Fori(first, end) as turn:
                for s in range(RING):
                    sp.wait_ge(tile_used.sem, turn * RING + (s - RING + 1))
                    sp.dma_start(ring[:, s, :], stream[turn * RING + s]).then_inc(landed[s], 16)

        def weights(pe, kind=None):
            t = tile_used.n
            if kind:
                order.append(kind)
            pe.wait_ge(landed[t % RING], 16 * (t // RING + 1))
            return ring[:, t % RING, :]

        freed = [[] for _ in range(8)]

        def claim(pe, *banks):
            for b in banks:
                for d, n in freed[b]:
                    pe.wait_ge(d.sem, n)
                freed[b] = []

        def feature_tile(banks, src, tok0, ntok, kind=None):
            @block.tensor
            def _(pe):
                w = weights(pe, kind).rearrange("p (k n) -> p k n", k=KT)
                claim(pe, *sorted(set(banks)))
                for half in range(2):
                    o = ps[:, banks[half], :]
                    if banks[0] == banks[1]:
                        o = ps[:, banks[0], half * 256:half * 256 + 256]
                    for k in range(KT):
                        last = nc.tensor.matmul(o[:, 0:ntok], w[:, k, half * P:half * P + P],
                                                src[:, k, tok0:tok0 + ntok],
                                                start=(k == 0), stop=(k == KT - 1))
                tile_used.by(last)
            return tile_used.n

        def token_rows(banks, src, tok0, ktiles, cols=512, kper=4, kind=None):
            @block.tensor
            def _(pe):
                claim(pe, *banks)
                for t0 in range(0, ktiles, kper):
                    w = weights(pe, kind).rearrange("p (k n) -> p k n", k=kper)
                    for n, b in enumerate(banks):
                        for k in range(t0, min(t0 + kper, ktiles)):
                            last = nc.tensor.matmul(ps[:, b, 0:cols],
                                                    src[:, k, tok0 + n * P:tok0 + n * P + P],
                                                    w[:, k - t0, 0:cols],
                                                    start=(k == 0), stop=(k == ktiles - 1))
                    tile_used.by(last)
            return tile_used.n

        def inverse_root(pool, out_, in_):
            link(pool, pool_done, nc.gpsimd.tensor_tensor(out_, in_, half_pow[:, 0:in_.shape[1]], ALU.pow))

        def norm_T(*args, **kw):
            for _ in norm_T_steps(*args, **kw):
                pass

        def norm_T_steps(x, outs, tok0, scratch, bank0=0, at=0, keep=False):
            for t in range(TT):
                @block.scalar
                def _(act):
                    after_all(act)
                    link(act, act_done, nc.scalar.activation(scratch[:, t, :], x[:, t, :], ACT.Square,
                                                             accum_out=small[:, at + t:at + t + 1]))

            yield

            @block.vector
            def _(dve):
                dve.wait_ge(act_done.sem, act_done.n)
                link(dve, dve_done, nc.vector.tensor_scalar(small[:, at + 2:at + 4], small[:, at:at + 2], 1.0 / D, EPS,
                                                            ALU.mult, ALU.add))

            @block.gpsimd
            def _(pool):
                pool.wait_ge(dve_done.sem, dve_done.n)
                inverse_root(pool, small[:, at + 4:at + 6], small[:, at + 2:at + 4])

            yield
            for t in range(TT):
                @block.vector
                def _(dve):
                    dve.wait_ge(pool_done.sem, pool_done.n)
                    o, i_ = (scratch[:, t, :], x[:, t, :]) if keep else (scratch[:, t, 0:P], ident)
                    link(dve, dve_done, nc.vector.tensor_scalar(o, i_, small[:, at + 4 + t:at + 5 + t], None,
                                                                ALU.mult))
                for q in range(2):
                    b = bank0 + (2 * t + q) % 3

                    @block.tensor
                    def _(pe):
                        claim(pe, b)
                        pe.wait_ge(dve_done.sem, dve_done.n)
                        for j in range(4):
                            cols = slice((4 * q + j) * P, (4 * q + j + 1) * P)
                            o = ps[:, b, j * P:j * P + P]
                            if keep:
                                last = nc.tensor.transpose(o, scratch[:, t, cols], ident)
                            else:
                                last = nc.tensor.matmul(o, x[:, t, cols], scratch[:, t, 0:P], start=True, stop=True)
                        pe_done.by(last)

                for q in range(2):
                    b = bank0 + (2 * t + q) % 3

                    @(block.vector, block.scalar)[q]
                    def _(eng):
                        eng.wait_ge(pe_done.sem, pe_done.n - 1 + q)
                        for dst, gain, shift in outs:
                            for j in range(4):
                                k = 4 * q + j
                                o, i_ = dst[:, k, tok0 + t * P:tok0 + t * P + P], ps[:, b, j * P:j * P + P]
                                g, sh = gain[:, k:k + 1], None if shift is None else shift[:, k:k + 1]
                                if q == 0:
                                    ins = nc.vector.tensor_scalar(o, i_, g, sh, ALU.mult,
                                                                  *(() if shift is None else (ALU.add,)))
                                elif shift is None:
                                    ins = nc.scalar.activation(o, i_, ACT.Copy, scale=g)
                                else:
                                    ins = nc.scalar.activation(o, i_, ACT.Identity, bias=sh, scale=g)
                        done = (dve_done, act_done)[q]
                        freed[b] = [(done, done.by(ins))]
                yield

        def copy_bank(b, dst, cols=slice(0, 512)):
            @block.vector
            def _(dve):
                dve.wait_ge(tile_used.sem, tile_used.n)
                dve.wait_ge(pe_done.sem, pe_done.n) if pe_done.n else None
                dve_done.by(nc.vector.tensor_copy(dst, ps[:, b, cols]))
                freed[b] = [(dve_done, dve_done.n)]

        def add_rows(banks, x, half, gate=None, scratch=None):
            @block.vector
            def _(dve):
                dve.wait_ge(tile_used.sem, tile_used.n)
                for n, b in enumerate(banks):
                    xs = x(n)[:, half * 512:half * 512 + 512]
                    if gate is None:
                        dve_done.by(nc.vector.tensor_tensor(xs, xs, ps[:, b, :], ALU.add))
                    else:
                        link(dve, dve_done, nc.vector.tensor_tensor(scratch[:, n, :], ps[:, b, :],
                                                                    gate(n)[:, half * 512:half * 512 + 512], ALU.mult))
                        dve_done.by(nc.vector.tensor_tensor(xs, xs, scratch[:, n, :], ALU.add))
                    freed[b] = [(dve_done, dve_done.n)]

        def settle():
            @block.tensor
            def _(pe):
                after_all(pe)

        half_pow = small[:, 496:512]

        @block.scalar
        def _(act):
            for t in range(TT):
                act.dma_start(h[:, t, :], out["x"][t * P:t * P + P, :]).then_inc(x_in, 16)

        @block.gpsimd
        def _(pool):
            pool_done.by(nc.gpsimd.memset(half_pow, -0.5))

        for eng in (block.tensor, block.scalar, block.vector, block.gpsimd):
            @eng
            def _(e):
                e.wait_ge(params_in, 16)
                e.wait_ge(x_in, 16 * TT)

        @block.scalar
        def _(act):
            link(act, act_done, nc.scalar.activation(c("cond"), c("cond"), ACT.Silu))
        cond = c("cond").rearrange("p (k n) -> p k n", k=KT)

        arow = arena[0:2, ARENA - 2 * 512:].rearrange("p (a n) -> p a n", a=2)

        def ada_lane():
            def spread(pe, n):
                for q in range(4):
                    last = nc.tensor.matmul(ps[:, 6, 8 * n + 2 * q:8 * n + 2 * q + 2],
                                            arow[:, n % 2, q * P:q * P + P], ident[0:2, 0:2],
                                            start=True, stop=True)
                pe_done.by(last)

            for n in range(24):
                @block.tensor
                def _(pe):
                    after_all(pe)
                    if n:
                        spread(pe, n - 1)
                    for half in range(2):
                        w = weights(pe, "ada").rearrange("p (k n) -> p k n", k=KT)
                        for k in range(KT):
                            last = nc.tensor.matmul(ps[0:2, 7, half * 256:half * 256 + 256], cond[:, k, :],
                                                    w[:, k, :], start=(k == 0), stop=(k == KT - 1))
                        tile_used.by(last)

                @block.vector
                def _(dve):
                    after_all(dve)
                    dve_done.by(nc.vector.tensor_copy(arow[:, n % 2, :], ps[0:2, 7, :]))
                yield

            @block.tensor
            def _(pe):
                after_all(pe)
                spread(pe, 23)

            @block.vector
            def _(dve):
                after_all(dve)
                dve_done.by(nc.vector.tensor_tensor(ada.rearrange("p l n c -> p (l n c)"), ps[:, 6, 0:192],
                                                    c("ada_b"), ALU.add))

        def rstd_of(cols, n):
            a, b_ = cols

            @block.vector
            def _(dve):
                after_all(dve)
                link(dve, dve_done, nc.vector.tensor_scalar(small[:, a:b_], small[:, a:b_], 1.0 / n, EPS,
                                                            ALU.mult, ALU.add))

            @block.gpsimd
            def _(pool):
                after_all(pool)
                inverse_root(pool, small[:, a + 16:b_ + 16], small[:, a:b_])

        def transpose_rows(src, ntt, evac):
            for t in range(ntt):
                for q in range(2):
                    b = 4 + q

                    @block.tensor
                    def _(pe):
                        after_all(pe) if t == q == 0 else None
                        claim(pe, b)
                        for j in range(4):
                            last = nc.tensor.transpose(ps[:, b, j * P:j * P + P],
                                                       src[:, t, (4 * q + j) * P:(4 * q + j + 1) * P], ident)
                        pe_done.by(last)

                    @block.vector
                    def _(dve):
                        dve.wait_ge(pe_done.sem, pe_done.n)
                        for j in range(4):
                            last = evac(ps[:, b, j * P:j * P + P], 4 * q + j, t)
                        dve_done.by(last)
                        freed[b] = [(dve_done, dve_done.n)]
                    yield

        def gla_lane():
            reset()
            xs = take(TT, D)
            yield from norm_T_steps(h, [(hT, c("attn0"), None)], 0, xs)
            reset()
            qdec, kinv, kend = take(H1, SEQ), take(H1, SEQ), take(H1, SEQ)
            q31, q30, q20 = take(H1, CHUNK), take(H1, CHUNK), take(H1, CHUNK)
            expb, expnb, expe = take(H1, SEQ), take(H1, SEQ), take(H1, SEQ)
            v = take(TT, D)
            rT = take(KT, SEQ)
            la = take(TT, 512)
            tmp = take(TT, 512)
            glr = take(SEQ)
            bend, de = take(16).rearrange("p (h n) -> p h n", h=H1), take(16).rearrange("p (h n) -> p h n", h=H1)
            e12 = take(H1)
            aT = take(H1, TT, SEQ)
            oo = take(TT, D)
            assert cur[0] <= ARENA - 2 * 512

            yield

            @block.tensor
            def _(pe):
                after_all(pe)
                wl = c("w_glr").rearrange("p (k n) -> p k n", k=KT)
                for k in range(KT):
                    last = nc.tensor.matmul(ps[0:16, 0, 0:SEQ], wl[:, k, :], hT[:, k, 0:SEQ],
                                            start=(k == 0), stop=(k == KT - 1))
                pe_done.by(last)

            yield

            @block.vector
            def _(dve):
                after_all(dve)
                dve_done.by(nc.vector.tensor_copy(glr[0:16, :], ps[0:16, 0, 0:SEQ]))

            yield

            @block.tensor
            def _(pe):
                after_all(pe)
                for t in range(TT):
                    nc.tensor.matmul(ps[:, 1 + t, :], glr[0:16, t * P:t * P + P], c("gate_up")[0:16, :],
                                     start=True, stop=False)
                    last = nc.tensor.matmul(ps[:, 1 + t, :], ones[0:1, :], c("gate_b")[0:1, :],
                                            start=False, stop=True)
                pe_done.by(last)

            yield

            @block.scalar
            def _(act):
                after_all(act)
                link(act, act_done, nc.scalar.activation(tmp, ps[:, 1:3, :], ACT.Abs))
                link(act, act_done, nc.scalar.activation(tmp, tmp, ACT.Exp, scale=-1.0))
                link(act, act_done, nc.scalar.activation(tmp, tmp, ACT.Ln, bias=1.0))

            yield

            @block.vector
            def _(dve):
                after_all(dve)
                dve_done.by(nc.vector.scalar_tensor_tensor(la, ps[:, 1:3, :], 0.0, tmp, ALU.min, ALU.subtract))

            yield

            @block.tensor
            def _(pe):
                after_all(pe)
                for hh in range(H1):
                    for t in range(TT):
                        last = nc.tensor.matmul(ps[:, hh // 2, (hh % 2) * SEQ + t * P:(hh % 2) * SEQ + t * P + P],
                                                la[:, t, hh * P:hh * P + P], c("gla_sum"), start=True, stop=True)
                pe_done.by(last)

            pb = ps[:, 0:2, :].rearrange("p b (h n c) -> p (b h) n c", h=2, c=CHUNK)

            yield

            @block.scalar
            def _(act):
                after_all(act)
                link(act, act_done, nc.scalar.activation(expb.rearrange("p h t -> p (h t)"), ps[:, 0:2, :], ACT.Exp))
                link(act, act_done, nc.scalar.activation(expnb.rearrange("p h t -> p (h t)"), ps[:, 0:2, :], ACT.Exp,
                                                         scale=-1.0))

            yield

            @block.vector
            def _(dve):
                after_all(dve)
                link(dve, dve_done, nc.vector.tensor_copy(bend, pb[:, :, :, CHUNK - 1]))
                for hh in range(H1):
                    ins = nc.vector.tensor_tensor(
                        expe[:, hh, :].rearrange("p (n c) -> p n c", c=CHUNK),
                        bend[:, hh, :].unsqueeze(2).to_broadcast([P, 4, CHUNK]), pb[:, hh, :, :], ALU.subtract)
                dve_done.by(ins)

            yield

            @block.scalar
            def _(act):
                after_all(act)
                link(act, act_done, nc.scalar.activation(expe, expe, ACT.Exp))
                link(act, act_done, nc.scalar.activation(de, bend, ACT.Exp))

            for n in range(2):
                feature_tile([2 + n, 2 + n], hT, 0, SEQ, "gla")

                @block.vector
                def _(dve):
                    after_all(dve)
                    dve_done.by(nc.vector.scalar_tensor_tensor(
                        qdec[:, 2 * n:2 * n + 2, :].rearrange("p h t -> p (h t)"), ps[:, 2 + n, :], float(P) ** -0.5,
                        expb[:, 2 * n:2 * n + 2, :].rearrange("p h t -> p (h t)"), ALU.mult, ALU.mult))
                    freed[2 + n] = [(dve_done, dve_done.n)]
            for n in range(2):
                feature_tile([4 + n, 4 + n], hT, 0, SEQ, "gla")

                @block.vector
                def _(dve):
                    after_all(dve)
                    kp = ps[:, 4 + n, :]
                    nc.vector.tensor_tensor(kinv[:, 2 * n:2 * n + 2, :].rearrange("p h t -> p (h t)"), kp,
                                            expnb[:, 2 * n:2 * n + 2, :].rearrange("p h t -> p (h t)"), ALU.mult)
                    dve_done.by(nc.vector.tensor_tensor(
                        kend[:, 2 * n:2 * n + 2, :].rearrange("p h t -> p (h t)"), kp,
                        expe[:, 2 * n:2 * n + 2, :].rearrange("p h t -> p (h t)"), ALU.mult))
                    freed[4 + n] = [(dve_done, dve_done.n)]
            for n in range(2):
                token_rows([4, 5], hT, 0, KT, kind="gla")
                for t in range(TT):
                    copy_bank(4 + t, v[:, t, n * 512:n * 512 + 512])
            for n in range(4):
                b = n % 4
                feature_tile([b, b], hT, 0, SEQ, "gla")

                @block.scalar
                def _(act):
                    act.wait_ge(tile_used.sem, tile_used.n)
                    act_done.by(nc.scalar.activation(rT[:, 2 * n:2 * n + 2, :].rearrange("p h t -> p (h t)"),
                                                     ps[:, b, :], ACT.Silu))
                    freed[b] = [(act_done, act_done.n)]

            yield

            @block.vector
            def _(dve):
                after_all(dve)
                def spread(e):
                    return e.unsqueeze(2).to_broadcast([P, H1, CHUNK])
                link(dve, dve_done, nc.vector.tensor_tensor(e12, de[:, :, 1], de[:, :, 2], ALU.mult))
                nc.vector.tensor_tensor(q20, qdec[:, :, 128:192], spread(de[:, :, 1]), ALU.mult)
                nc.vector.tensor_tensor(q31, qdec[:, :, 192:256], spread(de[:, :, 2]), ALU.mult)
                nc.vector.tensor_tensor(q30, qdec[:, :, 192:256], spread(e12), ALU.mult)
                dve_done.by(nc.vector.memset(aT, 0.0))

            for hh in range(H1):
                b = 4 + hh % 2

                yield

                @block.tensor
                def _(pe):
                    after_all(pe)
                    for t in range(TT):
                        nc.tensor.matmul(ps[:, b, t * P:t * P + P], kinv[:, hh, t * P:t * P + P],
                                         qdec[:, hh, t * P:t * P + P], start=True, stop=True)
                    ch = lambda x, n: x[:, hh, n * CHUNK:n * CHUNK + CHUNK]
                    pairs = [(0, 256, ch(kend, 0), ch(qdec, 1)), (0, 320, ch(kend, 0), q20[:, hh, :]),
                             (0, 384, ch(kend, 0), q30[:, hh, :]), (64, 320, ch(kend, 1), ch(qdec, 2)),
                             (64, 384, ch(kend, 1), q31[:, hh, :]), (0, 448, ch(kend, 2), ch(qdec, 3))]
                    for row, col, lhs, rhs in pairs:
                        last = nc.tensor.matmul(ps[row:row + 64, b, col:col + 64], lhs, rhs, start=True, stop=True)
                    pe_done.by(last)

                @block.vector
                def _(dve):
                    after_all(dve)
                    for t in range(TT):
                        last = nc.vector.tensor_tensor(aT[:, hh, t, t * P:t * P + P], ps[:, b, t * P:t * P + P],
                                                       c("gla_mask"), ALU.mult)
                    link(dve, dve_done, last)
                    nc.vector.tensor_copy(aT[0:64, hh, 0, 64:256], ps[0:64, b, 256:448])
                    nc.vector.tensor_copy(aT[64:128, hh, 0, 128:256], ps[64:128, b, 320:448])
                    dve_done.by(nc.vector.tensor_copy(aT[0:64, hh, 1, 192:256], ps[0:64, b, 448:512]))

            yield

            @block.tensor
            def _(pe):
                after_all(pe)
                for hh in range(H1):
                    for t in range(TT):
                        for j in range(t + 1):
                            last = nc.tensor.matmul(ps[:, 2 * t + hh // 2, (hh % 2) * DV1:(hh % 2) * DV1 + DV1],
                                                    aT[:, hh, j, t * P:t * P + P], v[:, j, hh * DV1:hh * DV1 + DV1],
                                                    start=(j == 0), stop=(j == t))
                pe_done.by(last)

            yield

            @block.scalar
            def _(act):
                after_all(act)
                for t in range(TT):
                    for hh in range(H1):
                        link(act, act_done, nc.scalar.activation(
                            oo[:, t, hh * DV1:hh * DV1 + DV1],
                            ps[:, 2 * t + hh // 2, (hh % 2) * DV1:(hh % 2) * DV1 + DV1], ACT.Square,
                            accum_out=small[:, 8 + 4 * t + hh:9 + 4 * t + hh]))

            rstd_of((8, 16), DV1)

            yield

            @block.vector
            def _(dve):
                after_all(dve)
                for t in range(TT):
                    for hh in range(H1):
                        last = nc.vector.tensor_scalar(oo[:, t, hh * DV1:hh * DV1 + DV1],
                                                       ps[:, 2 * t + hh // 2, (hh % 2) * DV1:(hh % 2) * DV1 + DV1],
                                                       small[:, 24 + 4 * t + hh:25 + 4 * t + hh], None, ALU.mult)
                dve_done.by(last)

            yT = hT

            yield from transpose_rows(oo, TT, lambda part, k, t: nc.vector.scalar_tensor_tensor(
                yT[:, k, t * P:t * P + P], part, c("gla_head")[:, k % 2:k % 2 + 1], rT[:, k, t * P:t * P + P],
                ALU.mult, ALU.mult))
            yield

        side_by_side([gla_lane(), ada_lane()])

        settle()
        for n in range(2):
            token_rows([2 * n, 2 * n + 1], hT, 0, KT)
            add_rows([2 * n, 2 * n + 1], lambda t: h[:, t, :], n)

        for eng in (block.tensor, block.scalar, block.vector, block.gpsimd):
            @eng
            def _(e):
                e.wait_ge(rest_in, 16 * (1 + TT))

        ffn_silu = sem("ffn_silu")
        ffn_act = sem("ffn_act")

        def turns(eng, n, looped, tile, size=RING):
            with eng.Fori(0, looped) as g:
                for s in range(size):
                    tile(g, s)
            for s in range(n - looped * size):
                tile(looped, s)

        def feed_forward(nf, hid, sg):
            t0 = tile_used.n
            slot = lambda k: (t0 + k) % RING
            looped = nf // RING

            @block.tensor
            def _(pe):
                after_all(pe)

                def up(g, s):
                    w = ring[:, slot(s), :].rearrange("p (k n) -> p k n", k=KT)
                    pe.wait_ge(landed[slot(s)], g * 16 + 16 * ((t0 + s) // RING + 1))
                    b = BANKS_PLAIN[s]
                    pe.wait_ge(ffn_act, g * RING + (RING + s - since(BANKS_PLAIN, s) + 1))
                    for half in range(2):
                        for k in range(KT):
                            last = nc.tensor.matmul(ps[:, b, half * SEQ:half * SEQ + SEQ],
                                                    w[:, k, half * P:half * P + P], hT[:, k, 0:SEQ],
                                                    start=(k == 0), stop=(k == KT - 1))
                    last.then_inc(tile_used.sem, 1)
                turns(pe, nf, looped, up)

            @block.scalar
            def _(act):
                after_all(act)

                def gate(g, s):
                    act.wait_ge(tile_used.sem, g * RING + (t0 + s + 1))
                    act.wait_ge(ffn_act, g * RING + (s + 1))
                    nc.scalar.activation(sg[:, s, :], ps[:, BANKS_PLAIN[s], 0:SEQ],
                                         ACT.Silu).then_inc(ffn_silu, 1)
                turns(act, nf, looped, gate)

            @block.vector
            def _(dve):
                after_all(dve)

                def hidden(g, s):
                    dve.wait_ge(ffn_silu, g * RING + (s + 1))
                    nc.vector.tensor_tensor(hid[:, g * RING + s, :], sg[:, s, :],
                                            ps[:, BANKS_PLAIN[s], SEQ:2 * SEQ], ALU.mult).then_inc(ffn_act, 1)
                turns(dve, nf, looped, hidden)
                dve.wait_ge(ffn_act, RING + nf)
                dve_done.by(nc.vector.tensor_copy(small[:, 480:481], small[:, 481:482]))
            tile_used.n += nf
            for b in range(4):
                freed[b] = [(dve_done, dve_done.n)]

        @block.vector
        def _(dve):
            dve_done.by(nc.vector.memset(small[:, 480:496], 0.0))
            dve.sem_inc(ffn_act, RING)

        reset()
        xs = take(TT, D)
        norm_T(h, [(hT, c("ffn0"), None)], 0, xs)
        reset()
        hid = take(F_FFN, SEQ)
        sg = take(RING, SEQ)
        feed_forward(F_FFN, hid, sg)
        for n in range(2):
            settle() if n == 0 else None
            token_rows([4 + 2 * n, 5 + 2 * n], hid, 0, F_FFN)
            add_rows([4 + 2 * n, 5 + 2 * n], lambda t: h[:, t, :], n)

        reset()
        xs = take(TT, D)
        hT2 = take(KT, SEQ)
        norm_T(h, [(hT, c("kvn"), None), (hT2, c("attn1"), None)], 0, xs)
        reset()
        xs = take(TT, D)
        hT2 = take(KT, SEQ)
        kT, qT = take(SBH, SEQ), take(SBH, SEQ)
        v = take(TT, D)
        SB_LANES = 4
        lane_buf = [[xs[:, 0, 0:512], xs[:, 0, 512:1024], xs[:, 1, 0:512]]] + \
            [[take(512) for _ in range(3)] for _ in range(SB_LANES - 1)]
        settle()
        for n in range(4):
            feature_tile([n, n], hT, 0, SEQ)
            copy_bank(n, kT[:, 2 * n:2 * n + 2, :].rearrange("p h t -> p (h t)"))
        for n in range(2):
            token_rows([4, 5], hT, 0, KT)
            for t in range(TT):
                copy_bank(4 + t, v[:, t, n * 512:n * 512 + 512])
        for n in range(4):
            feature_tile([n, n], hT2, 0, SEQ)
            copy_bank(n, qT[:, 2 * n:2 * n + 2, :].rearrange("p h t -> p (h t)"))

        def stick_head(hh, banks, bufs):
            zs, sp_, uu = bufs
            b0, b1 = banks
            halves = [slice(j * SEQ, j * SEQ + SEQ) for j in range(TT)]

            @block.tensor
            def _(pe):
                after_all(pe)
                for j in range(TT):
                    last = nc.tensor.matmul(ps[:, b0, halves[j]], kT[:, hh, j * P:j * P + P],
                                            qT[:, hh, :], start=True, stop=True)
                pe_done.by(last)
            yield

            @block.scalar
            def _(act):
                after_all(act)
                act_done.by(nc.scalar.activation(zs, ps[:, b0, :], ACT.Copy, scale=float(P) ** -0.5))
                link(act, act_done, nc.scalar.activation(uu, ps[:, b0, :], ACT.Abs, scale=float(P) ** -0.5))
                act_done.by(nc.scalar.activation(uu, uu, ACT.Exp, scale=-1.0))
            yield

            @block.scalar
            def _(act):
                after_all(act)
                act_done.by(nc.scalar.activation(uu, uu, ACT.Ln, bias=1.0))
            yield

            @block.vector
            def _(dve):
                after_all(dve)
                link(dve, dve_done, nc.vector.scalar_tensor_tensor(uu, zs, 0.0, uu, ALU.max, ALU.add))
                nc.vector.tensor_tensor(sp_, uu, c("sb_mask"), ALU.mult)
                dve_done.by(nc.vector.tensor_tensor(uu, zs, uu, ALU.subtract))
            yield

            @block.tensor
            def _(pe):
                after_all(pe)
                nc.tensor.matmul(ps[:, b1, 0:SEQ], c("sb_later"), sp_[:, halves[0]], start=True, stop=False)
                nc.tensor.matmul(ps[:, b1, 0:SEQ], c("minus"), sp_[:, halves[1]], start=False, stop=True)
                pe_done.by(nc.tensor.matmul(ps[:, b1, SEQ:2 * SEQ], c("sb_later"), sp_[:, halves[1]],
                                            start=True, stop=True))
            yield

            @block.vector
            def _(dve):
                after_all(dve)
                dve_done.by(nc.vector.tensor_tensor(uu, uu, ps[:, b1, :], ALU.add))
            yield

            @block.scalar
            def _(act):
                after_all(act)
                act_done.by(nc.scalar.activation(uu, uu, ACT.Exp))
            yield

            @block.vector
            def _(dve):
                after_all(dve)
                dve_done.by(nc.vector.tensor_tensor(zs, uu, c("sb_mask"), ALU.mult))
            yield

            @block.tensor
            def _(pe):
                after_all(pe)
                for j in range(TT):
                    last = nc.tensor.matmul(ps[:, b0, 0:SEQ], v[:, j, hh * P:hh * P + P], zs[:, halves[j]],
                                            start=(j == 0), stop=(j == TT - 1))
                pe_done.by(last)
            yield

            @block.vector
            def _(dve):
                after_all(dve)
                dve_done.by(nc.vector.tensor_copy(hT[:, hh, 0:SEQ], ps[:, b0, 0:SEQ]))
            yield

        def stick_lane(n):
            for hh in range(n, SBH, SB_LANES):
                yield from stick_head(hh, (2 * n, 2 * n + 1), lane_buf[n])

        side_by_side([stick_lane(n) for n in range(SB_LANES)])

        settle()
        for n in range(2):
            token_rows([2 * n, 2 * n + 1], hT, 0, KT)
            add_rows([2 * n, 2 * n + 1], lambda t: h[:, t, :], n)

        moe_gathered = sem("moe_gathered")
        moe_tokens = sem("moe_tokens")
        moe_silu = sem("moe_silu")
        moe_hid = sem("moe_hid")
        moe_y = sem("moe_y")
        moe_spread = sem("moe_spread")
        moe_place = sem("moe_place")
        reset()
        xn = take(TT, D)
        norm_T(h, [(hT, c("ffn1"), None)], 0, xn, keep=True)
        hid = take(F_MOE, CAP)
        sg = take(2, CAP)
        hTe = take(KT, CAP)
        pick = take(TT, EXPERTS + 1, P)
        place = take(EXPERTS, SEQ)
        placed = take(SEQ)
        y = take(D)
        tmp = take(P)
        mark = cur[0]
        lg = take(TT, EXPERTS)
        top = take(TT, 8)
        idx = arena[:, cur[0]:cur[0] + 16].bitcast(U32).rearrange("p (t n) -> p t n", t=TT)
        cur[0] += 16
        idf = take(TT, 8)
        wsel = take(TT, 4)
        sel = take(TT, EXPERTS)
        chosen = take(TT, EXPERTS)
        gates = take(TT, EXPERTS)
        rank = take(TT, EXPERTS)
        rest = small[:, 256:272].rearrange("p (t n) -> p t n", t=TT)
        over = small[:, 272:274]
        flag = small[:, 274:275].bitcast(U32)

        @block.tensor
        def _(pe):
            after_all(pe)
            wr = c("router").rearrange("p (k n) -> p k n", k=KT)
            for t in range(TT):
                for k in range(KT):
                    last = nc.tensor.matmul(ps[:, 4, t * EXPERTS:(t + 1) * EXPERTS], hT[:, k, t * P:t * P + P],
                                            wr[:, k, :], start=(k == 0), stop=(k == KT - 1))
            pe_done.by(last)

        @block.vector
        def _(dve):
            after_all(dve)
            link(dve, dve_done, nc.vector.tensor_copy(lg.rearrange("p t n -> p (t n)"), ps[:, 4, 0:TT * EXPERTS]))
            for t in range(TT):
                link(dve, dve_done, nc.vector.max(top[:, t, :], lg[:, t, :]))
                link(dve, dve_done, nc.vector.max_index(idx[:, t, :], top[:, t, :], lg[:, t, :]))
            link(dve, dve_done, nc.vector.tensor_copy(idf, idx))
            link(dve, dve_done, nc.vector.tensor_tensor(wsel[:, :, 0], top[:, :, 1], top[:, :, 0], ALU.subtract))

        @block.scalar
        def _(act):
            after_all(act)
            act_done.by(nc.scalar.activation(wsel[:, :, 1], wsel[:, :, 0], ACT.Exp))

        @block.vector
        def _(dve):
            after_all(dve)
            link(dve, dve_done, nc.vector.tensor_scalar(wsel[:, :, 2], wsel[:, :, 1], 1.0, None, ALU.add))
            link(dve, dve_done, nc.vector.reciprocal(wsel[:, :, 2], wsel[:, :, 2]))
            link(dve, dve_done, nc.vector.tensor_tensor(wsel[:, :, 3], wsel[:, :, 1], wsel[:, :, 2], ALU.mult))
            for t in range(TT):
                nc.vector.tensor_scalar(gates[:, t, :], c("iota8"), idf[:, t, 0:1],
                                        wsel[:, t, 2:3], ALU.is_equal, ALU.mult)
                link(dve, dve_done, nc.vector.tensor_scalar(sel[:, t, :], c("iota8"), idf[:, t, 1:2],
                                                            wsel[:, t, 3:4], ALU.is_equal, ALU.mult))
            link(dve, dve_done, nc.vector.tensor_tensor(gates, gates, sel, ALU.add))
            for t in range(TT):
                nc.vector.tensor_scalar(sel[:, t, :], c("iota8"), idf[:, t, 1:2], None, ALU.is_equal)
                ins = nc.vector.tensor_scalar(chosen[:, t, :], c("iota8"), idf[:, t, 0:1], None, ALU.is_equal)
            link(dve, dve_done, ins)
            link(dve, dve_done, nc.vector.tensor_tensor(chosen, chosen, sel, ALU.add))

        @block.tensor
        def _(pe):
            after_all(pe)
            nc.tensor.matmul(ps[:, 4, 0:8], c("strict0"), chosen[:, 0, :], start=True, stop=True)
            nc.tensor.matmul(ps[:, 4, 8:16], ones, chosen[:, 0, :], start=True, stop=False)
            nc.tensor.matmul(ps[:, 4, 8:16], c("strict0"), chosen[:, 1, :], start=False, stop=True)
            nc.tensor.matmul(ps[:, 4, 16:24], ones, chosen[:, 0, :], start=True, stop=False)
            pe_done.by(nc.tensor.matmul(ps[:, 4, 16:24], ones, chosen[:, 1, :], start=False, stop=True))

        @block.vector
        def _(dve):
            after_all(dve)
            nc.vector.tensor_reduce(over[:, 0:1], ps[:, 4, 16:24], AXX, ALU.max)
            link(dve, dve_done, nc.vector.tensor_copy(rank.rearrange("p t n -> p (t n)"), ps[:, 4, 0:16]))
            link(dve, dve_done, nc.vector.tensor_scalar(flag, over[:, 0:1], float(CAP), None, ALU.is_gt))
            link(dve, dve_done, nc.vector.tensor_scalar(rest, rank, float(CAP), None, ALU.is_ge))
            link(dve, dve_done, nc.vector.tensor_tensor(rest, rest, gates, ALU.mult))
            nc.vector.memset(pick[:, :, EXPERTS, :], 0.0)
            for e in range(EXPERTS):
                for t in range(TT):
                    ins = nc.vector.tensor_scalar(pick[:, t, e, :], c("slots"), rank[:, t, e:e + 1],
                                                  chosen[:, t, e:e + 1], ALU.is_equal, ALU.mult)
            link(dve, dve_done, ins)
        flag_known = dve_done.n

        gate_diag = take(TT, EXPERTS, P)

        @block.vector
        def _(dve):
            after_all(dve)
            for t in range(TT):
                dve_done.by(nc.vector.tensor_tensor(
                    gate_diag[:, t, :, :], ident.unsqueeze(1).to_broadcast([P, EXPERTS, P]),
                    gates[:, t, :].unsqueeze(2).to_broadcast([P, EXPERTS, P]), ALU.mult))

        @block.tensor
        def _(pe):
            for t in range(TT):
                for half in range(2):
                    nc.tensor.matmul(ps[:, 2 * t + half, :], ident, h[:, t, half * 512:half * 512 + 512],
                                     start=True, stop=False, skip_group_check=True)
            after_all(pe)
            for e in range(EXPERTS):
                for t in range(TT):
                    last = nc.tensor.matmul(ps[:, 4 + e // 2, (e % 2) * SEQ + t * P:(e % 2) * SEQ + t * P + P],
                                            pick[:, t, e, :], gate_diag[:, t, e, :], start=True, stop=True)
            pe_done.by(last)

        @block.vector
        def _(dve):
            after_all(dve)
            dve_done.by(nc.vector.tensor_copy(place[:, 0:4, :].rearrange("p e t -> p (e t)"),
                                              ps[:, 4:6, :].rearrange("p b n -> p (b n)")))

        @block.scalar
        def _(act):
            after_all(act)
            act_done.by(nc.scalar.activation(place[:, 4:8, :].rearrange("p e t -> p (e t)"),
                                             ps[:, 6:8, :].rearrange("p b n -> p (b n)"), ACT.Copy))

        nf = F_MOE
        kd = nf // 4
        per = nf + 2 * kd
        turns_per = per // RING
        BODY = 2 * RING
        assert per % RING == 0 and nf % BODY == 0
        moe_t0 = tile_used.n
        slot = lambda k: (moe_t0 + k) % RING
        wait_of = lambda k: 16 * ((moe_t0 + k) // RING + 1)

        def gather(pe, e):
            for k in range(KT):
                for t in range(TT):
                    last = nc.tensor.matmul(ps[:, 4 + k // 4, (k % 4) * P:(k % 4) * P + CAP],
                                            xn[:, t, k * P:k * P + P],
                                            pick[:, t, bass.ds(e, 1), 0:CAP].rearrange("p a n -> p (a n)"),
                                            start=(t == 0), stop=(t == TT - 1), skip_group_check=True)
            last.then_inc(moe_gathered, 1)

        def copy_tokens(dve):
            for k in range(KT):
                last = nc.vector.tensor_scalar(hTe[:, k, :], ps[:, 4 + k // 4, (k % 4) * P:(k % 4) * P + CAP],
                                               c("ffn1")[:, k:k + 1], None, ALU.mult)
            last.then_inc(moe_tokens, 1)

        @block.tensor
        def _(pe):
            after_all(pe)
            gather(pe, 0)
            with pe.Fori(0, EXPERTS) as e:
                with pe.Fori(0, nf // BODY) as g:
                    pe.wait_ge(moe_tokens, e + 1)
                    for s in range(BODY):
                        pe.wait_ge(landed[slot(s)], e * (16 * turns_per) + g * (16 * BODY // RING) + wait_of(s))
                        w = ring[:, slot(s), :].rearrange("p (k n) -> p k n", k=KT)
                        pe.wait_ge(moe_hid, e * nf + g * BODY + (s + 1))
                        for half in range(2):
                            for k in range(KT):
                                last = nc.tensor.matmul(ps[:, 4 + s % 2, half * P:half * P + CAP],
                                                        w[:, k, half * P:half * P + P], hTe[:, k, :],
                                                        start=(k == 0), stop=(k == KT - 1), skip_group_check=True)
                        last.then_inc(tile_used.sem, 1)
                pe.wait_ge(moe_hid, e * nf + (nf + 2))
                gather(pe, e + 1)
                for half in range(2):
                    for d in range(kd):
                        k0 = nf + half * kd + d
                        pe.wait_ge(landed[slot(k0)], e * (16 * turns_per) + wait_of(k0))
                        w = ring[:, slot(k0), :].rearrange("p (k n) -> p k n", k=4)
                        for j in range(4):
                            last = nc.tensor.matmul(ps[0:CAP, 6 + half, :], hid[:, 4 * d + j, :], w[:, j, :],
                                                    start=(d == j == 0), stop=(d == kd - 1 and j == 3),
                                                    skip_group_check=True)
                        last.then_inc(tile_used.sem, 1)
                pe.wait_ge(moe_y, e * 2 + 2)
                pe.wait_ge(moe_place, e + 1)
                for half in range(2):
                    for t in range(TT):
                        last = nc.tensor.matmul(ps[:, 2 * t + half, :], placed[0:CAP, t * P:t * P + P],
                                                y[0:CAP, half * 512:half * 512 + 512], start=False, stop=False,
                                                skip_group_check=True)
                last.then_inc(moe_spread, 1)

        @block.scalar
        def _(act):
            after_all(act)
            with act.Fori(0, EXPERTS) as e:
                with act.Fori(0, nf // BODY) as g:
                    for s in range(BODY):
                        act.wait_ge(tile_used.sem, e * per + g * BODY + (moe_t0 + s + 1))
                        act.wait_ge(moe_hid, e * nf + g * BODY + (s + 1))
                        nc.scalar.activation(sg[:, s % 2, :], ps[:, 4 + s % 2, 0:CAP], ACT.Silu).then_inc(moe_silu, 1)

        @block.vector
        def _(dve):
            after_all(dve)
            dve.sem_inc(moe_hid, 2)
            dve.wait_ge(moe_gathered, 1)
            copy_tokens(dve)
            with dve.Fori(0, EXPERTS) as e:
                with dve.Fori(0, nf // BODY) as g:
                    for s in range(BODY):
                        dve.wait_ge(moe_silu, e * nf + g * BODY + (s + 1))
                        nc.vector.tensor_tensor(hid[:, g * BODY + s, :], sg[:, s % 2, :],
                                                ps[:, 4 + s % 2, P:P + CAP], ALU.mult).then_inc(moe_hid, 1)
                dve.wait_ge(moe_gathered, e + 2)
                copy_tokens(dve)
                for half in range(2):
                    dve.wait_ge(tile_used.sem, e * per + (moe_t0 + nf + (half + 1) * kd))
                    nc.vector.tensor_copy(y[0:CAP, half * 512:half * 512 + 512],
                                          ps[0:CAP, 6 + half, :]).then_inc(moe_y, 1)

        @block.gpsimd
        def _(pool):
            after_all(pool)
            pool.sem_inc(moe_spread, 1)
            with pool.Fori(0, EXPERTS) as e:
                pool.wait_ge(moe_spread, e + 1)
                nc.gpsimd.tensor_copy(placed, place[:, bass.ds(e, 1), :].rearrange("p a t -> p (a t)"))\
                    .then_inc(moe_place, 1)
        tile_used.n += EXPERTS * per

        @block.vector
        def _(dve):
            dve.wait_ge(moe_spread, EXPERTS + 1)
            for t in range(TT):
                ins = nc.vector.tensor_copy(h[:, t, :], ps[:, 2 * t:2 * t + 2, :].rearrange("p b n -> p (b n)"))
            dve.wait_ge(moe_tokens, EXPERTS + 1)
            dve_done.by(ins)
        for b in range(8):
            freed[b] = [(dve_done, dve_done.n)]

        over_landed = [sem(f"over_landed{n}") for n in range(2)]
        over_used = sem("over_used")
        over_silu = sem("over_silu")
        over_hid = sem("over_hid")
        over_gate = sem("over_gate")
        over_out = sem("over_out")
        main_end = {d: d.n for d in everyone}
        reset()
        oring = take(2, TILE)
        ohid = take(nf, SEQ)
        osg = take(2, SEQ)
        ogate = take(TT, 1)
        moe_turn = -(-tile_used.n // RING)

        def flag_set(eng):
            eng.wait_ge(dve_done.sem, flag_known)
            return eng.value_load(flag[0:1, 0:1], min_val=0, max_val=1) > 0

        @block.sync
        def _(sp):
            load_turns(sp, 1, moe_turn)
            with sp.If(flag_set(sp)):
                for d in everyone:
                    if main_end[d]:
                        sp.wait_ge(d.sem, main_end[d])
                with sp.Fori(0, EXPERTS * per // 2) as i:
                    for s in range(2):
                        sp.wait_ge(over_used, i * 2 + (s + 1))
                        sp.dma_start(oring[:, s, :], stream[i * 2 + (moe_t0 + s)]).then_inc(over_landed[s], 16)

        @block.tensor
        def _(pe):
            after_all(pe)
            with pe.If(flag_set(pe)):
                pe.sem_inc(over_used, 2)
                with pe.Fori(0, EXPERTS) as e:
                    with pe.Fori(0, nf // 2) as g:
                        for s in range(2):
                            pe.wait_ge(over_landed[s], e * (8 * per) + g * 16 + 16)
                            w = oring[:, s, :].rearrange("p (k n) -> p k n", k=KT)
                            pe.wait_ge(over_hid, e * nf + g * 2 + (s + 1))
                            for half in range(2):
                                for k in range(KT):
                                    last = nc.tensor.matmul(ps[:, 4 + s, half * SEQ:half * SEQ + SEQ],
                                                            w[:, k, half * P:half * P + P], hT[:, k, 0:SEQ],
                                                            start=(k == 0), stop=(k == KT - 1))
                            last.then_inc(over_used, 1)
                    pe.wait_ge(over_hid, e * nf + (nf + 2))
                    pe.wait_ge(over_out, e * 4 + 4)
                    for half in range(2):
                        for d in range(kd):
                            k0 = nf + half * kd + d
                            pe.wait_ge(over_landed[k0 % 2], e * (8 * per) + 16 * (k0 // 2 + 1))
                            w = oring[:, k0 % 2, :].rearrange("p (k n) -> p k n", k=4)
                            for t in range(TT):
                                for j in range(4):
                                    last = nc.tensor.matmul(ps[:, 2 * half + t, :],
                                                            ohid[:, 4 * d + j, t * P:t * P + P], w[:, j, :],
                                                            start=(d == j == 0), stop=(d == kd - 1 and j == 3))
                            last.then_inc(over_used, 1)

        @block.scalar
        def _(act):
            after_all(act)
            with act.If(flag_set(act)):
                with act.Fori(0, EXPERTS) as e:
                    with act.Fori(0, nf // 2) as g:
                        for s in range(2):
                            act.wait_ge(over_used, e * per + g * 2 + (s + 3))
                            act.wait_ge(over_hid, e * nf + g * 2 + (s + 1))
                            nc.scalar.activation(osg[:, s, :], ps[:, 4 + s, 0:SEQ], ACT.Silu).then_inc(over_silu, 1)

        @block.vector
        def _(dve):
            after_all(dve)
            with dve.If(flag_set(dve)):
                dve.sem_inc(over_hid, 2)
                dve.sem_inc(over_out, 4)
                with dve.Fori(0, EXPERTS) as e:
                    with dve.Fori(0, nf // 2) as g:
                        for s in range(2):
                            dve.wait_ge(over_silu, e * nf + g * 2 + (s + 1))
                            nc.vector.tensor_tensor(ohid[:, g * 2 + s, :], osg[:, s, :],
                                                    ps[:, 4 + s, SEQ:2 * SEQ], ALU.mult).then_inc(over_hid, 1)
                    dve.wait_ge(over_out, e * 4 + 4)
                    nc.vector.tensor_copy(ogate, rest[:, :, bass.ds(e, 1)]).then_inc(over_gate, 1)
                    dve.wait_ge(over_gate, e + 1)
                    for half in range(2):
                        dve.wait_ge(over_used, e * per + (2 + nf + (half + 1) * kd))
                        for t in range(TT):
                            hs = h[:, t, half * 512:half * 512 + 512]
                            nc.vector.scalar_tensor_tensor(hs, ps[:, 2 * half + t, :], ogate[:, t, :], hs,
                                                           ALU.mult, ALU.add).then_inc(over_out, 1)
                dve.wait_ge(over_out, EXPERTS * 4 + 4)

        @block.vector
        def _(dve):
            dve_done.by(nc.vector.tensor_copy(small[:, 480:481], small[:, 481:482]))

        def final_norm(gain_row):
            @block.scalar
            def _(act):
                after_all(act)
                for t in range(TT):
                    link(act, act_done, nc.scalar.activation(arena[:, 0:D], h[:, t, :], ACT.Square,
                                                             accum_out=small[:, 8 + t:9 + t]))
            rstd_of((8, 10), D)

            @block.vector
            def _(dve):
                after_all(dve)
                for t in range(TT):
                    dve_done.by(nc.vector.scalar_tensor_tensor(h[:, t, :], h[:, t, :], small[:, 24 + t:25 + t],
                                                               gain_row, ALU.mult, ALU.mult))

        final_norm(c("final1"))

        mod = small[:, 64:64 + 64].rearrange("p (a k) -> p a k", k=KT)

        def modulation(layer, which, gain, streams=2):
            out_ = []

            @block.vector
            def _(dve):
                after_all(dve)
                for s in range(2):
                    shift = ada[:, layer, 24 * which:24 * which + 8, s]
                    scale = ada[:, layer, 24 * which + 8:24 * which + 16, s]
                    dst = mod[:, s, :]
                    link(dve, dve_done, nc.vector.tensor_copy(mod[:, 2 + s, :], shift))
                    link(dve, dve_done, nc.vector.scalar_tensor_tensor(dst, scale, 1.0, gain, ALU.add, ALU.mult))
                    out_.append((dst, mod[:, 2 + s, :]))
            return out_

        def gate_rows(layer, which, dst, diag, streams=(0, 1)):
            groups = [(s, q) for s in streams for q in range(2)]
            for n, (s, q) in enumerate(groups):
                @block.vector
                def _(dve):
                    after_all(dve)
                    col = 24 * which + 16 + 4 * q
                    dve_done.by(nc.vector.tensor_tensor(
                        diag[:, n, :, :], ident.unsqueeze(1).to_broadcast([P, 4, P]),
                        ada[:, layer, col:col + 4, s].unsqueeze(2).to_broadcast([P, 4, P]), ALU.mult))
                yield
            for n, (s, q) in enumerate(groups):
                @block.tensor
                def _(pe):
                    after_all(pe)
                    pe_done.by(nc.tensor.matmul(ps[:, 6 + n % 2, :], ones,
                                                diag[:, n, :, :].rearrange("p a b -> p (a b)"),
                                                start=True, stop=True))

                @block.scalar
                def _(act):
                    after_all(act)
                    act_done.by(nc.scalar.activation(dst[:, s, q * 512:q * 512 + 512], ps[:, 6 + n % 2, :], ACT.Copy))
                yield

        def gate_buffers():
            return take(2, D), take(4, 512)

        def gate_lane_of(layer, which, rows, scr, streams):
            return gate_rows(layer, which, rows, scr.rearrange("p t (a b) -> p t a b", a=4), streams)

        def norm_both(context, latent, *others):
            side_by_side([norm_T_steps(cx, [(hT, *context)], 0, take(TT, D)),
                          norm_T_steps(h, [(hT, *latent)], SEQ, take(TT, D), 3, 440), *others])

        (sc_l, sh_l), (sc_c, sh_c) = modulation(0, 0, c("norm1_0"))
        reset()
        norm_both((sc_c, sh_c), (sc_l, sh_l))

        reset()
        T4 = 4
        uT = take(4, 512)
        vn = take(T4, 512)
        qT, kT = take(GH, 512), take(GH, 512)
        kt, vt = take(T4, GH * P), take(T4, GH * P)
        gT = take(GH, 512)
        settle()
        for n in range(2):
            feature_tile([2 * n, 2 * n + 1], hT, 0, 512)
            for i in range(2):
                @block.scalar
                def _(act):
                    act.wait_ge(tile_used.sem, tile_used.n)
                    act_done.by(nc.scalar.activation(uT[:, 2 * n + i, :], ps[:, 2 * n + i, :], ACT.Gelu))
                    freed[2 * n + i] = [(act_done, act_done.n)]
        token_rows([4, 5, 6, 7], hT, 0, KT)
        for t in range(T4):
            @block.scalar
            def _(act):
                act.wait_ge(tile_used.sem, tile_used.n)
                act_done.by(nc.scalar.activation(vn[:, t, :], ps[:, 4 + t, :], ACT.Gelu,
                                                 accum_out=small[:, 8 + t:9 + t]))
                freed[4 + t] = [(act_done, act_done.n)]

        abv = take(T4, 16)
        lal, beta, t8 = take(T4, 8), take(T4, 8), take(T4, 8)
        gcs, bgs = take(T4, 8), take(T4, 8)
        mark_gdn = cur[0]
        scratch512 = take(512)
        cbs = [take(2, 512) for _ in range(3)]
        seg = lambda x, a, b_: x.rearrange("p (s t) -> p s t", s=2)[:, :, a:b_]
        bc8 = lambda x: x.unsqueeze(1).to_broadcast([P, T4, 8])

        def layer_norm_lane():
            @block.vector
            def _(dve):
                after_all(dve)
                link(dve, dve_done, nc.vector.tensor_scalar(small[:, 12:16], small[:, 8:12], 1.0 / 512, None,
                                                            ALU.mult))
                for t in range(T4):
                    last = nc.vector.tensor_scalar(vn[:, t, :], vn[:, t, :], small[:, 12 + t:13 + t],
                                                   None, ALU.subtract)
                dve_done.by(last)
            yield

            @block.scalar
            def _(act):
                after_all(act)
                for t in range(T4):
                    link(act, act_done, nc.scalar.activation(scratch512, vn[:, t, :], ACT.Square,
                                                             accum_out=small[:, 8 + t:9 + t]))
            yield
            rstd_of((8, 12), 512)
            yield

            @block.vector
            def _(dve):
                after_all(dve)
                for t in range(T4):
                    last = nc.vector.scalar_tensor_tensor(vn[:, t, :], vn[:, t, :], small[:, 24 + t:25 + t],
                                                          c("ln_g"), ALU.mult, ALU.mult)
                link(dve, dve_done, last)
            yield

            @block.vector
            def _(dve):
                for t in range(T4):
                    last = nc.vector.tensor_tensor(vn[:, t, :], vn[:, t, :], c("ln_b"), ALU.add)
                normed["v"] = dve_done.by(last)
            yield

        def gate_lane():
            for n in range(2):
                @block.tensor
                def _(pe):
                    after_all(pe)
                feature_tile([6, 7], hT, 0, 512, "out_gate")

                @block.scalar
                def _(act):
                    after_all(act)
                    for i in range(2):
                        act_done.by(nc.scalar.activation(gT[:, 2 * n + i, :], ps[:, 6 + i, :], ACT.Silu))
                yield

            @block.tensor
            def _(pe):
                after_all(pe)
                wab = c("w_ab").rearrange("p (k n) -> p k n", k=KT)
                for t in range(T4):
                    for k in range(KT):
                        last = nc.tensor.matmul(ps[:, 6, t * 16:t * 16 + 16], hT[:, k, t * P:t * P + P],
                                                wab[:, k, :], start=(k == 0), stop=(k == KT - 1))
                pe_done.by(last)
            yield

            @block.vector
            def _(dve):
                after_all(dve)
                link(dve, dve_done, nc.vector.tensor_copy(abv.rearrange("p t n -> p (t n)"), ps[:, 6, 0:64]))
                dve_done.by(nc.vector.tensor_tensor(lal, abv[:, :, 0:8], bc8(c("dt_bias")), ALU.add))
            yield

            @block.scalar
            def _(act):
                after_all(act)
                act_done.by(nc.scalar.activation(c("a_log"), c("a_log"), ACT.Exp))
                act_done.by(nc.scalar.activation(beta, abv[:, :, 8:16], ACT.Exp, scale=-1.0))
                link(act, act_done, nc.scalar.activation(t8, lal, ACT.Abs))
                link(act, act_done, nc.scalar.activation(t8, t8, ACT.Exp, scale=-1.0))
                link(act, act_done, nc.scalar.activation(t8, t8, ACT.Ln, bias=1.0))
            yield

            @block.vector
            def _(dve):
                after_all(dve)
                link(dve, dve_done, nc.vector.scalar_tensor_tensor(lal, lal, 0.0, t8, ALU.max, ALU.add))
                link(dve, dve_done, nc.vector.tensor_tensor(lal, lal, bc8(c("a_log")), ALU.mult))
                link(dve, dve_done, nc.vector.tensor_scalar(lal, lal, -1.0, None, ALU.mult))
                link(dve, dve_done, nc.vector.tensor_scalar(beta, beta, 1.0, None, ALU.add))
                link(dve, dve_done, nc.vector.reciprocal(beta, beta))
            yield

        def conv_lane(lane):
            cb = cbs[lane]
            bank = (2 * lane, 2 * lane + 1)
            for n in ((2, 4), (3, 5), (0, 1))[lane]:
                kind = n // 2
                tap = lambda j, i: c("conv_qkv")[:, j * 12 + 2 * n + i:j * 12 + 2 * n + i + 1]
                full = [(qT, kT, cb)[kind][:, (2 * n + i) % 4 if kind < 2 else i, :] for i in range(2)]

                @block.tensor
                def _(pe):
                    after_all(pe)
                feature_tile(bank, hT, 0, 512, f"qkv{n}")

                @block.scalar
                def _(act):
                    after_all(act)
                    for i in range(2):
                        act_done.by(nc.scalar.activation(cb[:, i, :], ps[:, bank[i], :], ACT.Copy, scale=tap(1, i)))
                yield

                for side in range(2):
                    @block.vector
                    def _(dve):
                        after_all(dve)
                        for i in range(2):
                            src, dst = ps[:, bank[i], :], cb[:, i, :]
                            a, b_ = (seg(dst, 1, SEQ), seg(src, 0, SEQ - 1)) if side == 0 else \
                                (seg(dst, 0, SEQ - 1), seg(src, 1, SEQ))
                            last = nc.vector.scalar_tensor_tensor(a, b_, tap(2 * side, i), a, ALU.mult, ALU.add)
                        dve_done.by(last)
                yield

                @block.scalar
                def _(act):
                    after_all(act)
                    for i in range(2):
                        act_done.by(nc.scalar.activation(full[i], cb[:, i, :], ACT.Silu))
                yield
                if kind < 2:
                    @block.scalar
                    def _(act):
                        after_all(act)
                        for i in range(2):
                            act_done.by(nc.scalar.activation(cb[:, i, :], full[i], ACT.Square))
                    yield

                    st = small[:, 448 + 8 * lane:456 + 8 * lane]

                    @block.tensor
                    def _(pe):
                        after_all(pe)
                        for i in range(2):
                            for t in range(T4):
                                last = nc.tensor.matmul(ps[:, bank[0], T4 * i + t:T4 * i + t + 1],
                                                        cb[:, i, t * P:t * P + P], ones[:, 0:1],
                                                        start=True, stop=True)
                        pe_done.by(last)
                    yield

                    @block.vector
                    def _(dve):
                        after_all(dve)
                        dve_done.by(nc.vector.tensor_scalar(st, ps[:, bank[0], 0:2 * T4], EPS, None, ALU.add))

                    @block.gpsimd
                    def _(pool):
                        after_all(pool)
                        inverse_root(pool, st, st)
                    yield

                    @block.vector
                    def _(dve):
                        after_all(dve)
                        for i in range(2):
                            last = nc.vector.tensor_tensor(
                                cb[:, i, :].rearrange("p (t n) -> p t n", t=T4),
                                ident.unsqueeze(1).to_broadcast([P, T4, P]),
                                st[:, T4 * i:T4 * i + T4].unsqueeze(2).to_broadcast([P, T4, P]), ALU.mult)
                        dve_done.by(last)
                    yield

                    @block.tensor
                    def _(pe):
                        after_all(pe)
                        for i in range(2):
                            last = nc.tensor.matmul(ps[:, bank[i], :], ones, cb[:, i, :], start=True, stop=True)
                        pe_done.by(last)
                    yield

                    @block.vector
                    def _(dve):
                        after_all(dve)
                        for i in range(2):
                            last = nc.vector.scalar_tensor_tensor(
                                full[i], full[i], float(P) ** -0.5 if kind == 0 else 1.0, ps[:, bank[i], :],
                                ALU.mult, ALU.mult)
                        dve_done.by(last)
                    yield
                if kind > 0:
                    row = (kt, vt)[kind - 1]

                    @block.tensor
                    def _(pe):
                        after_all(pe)
                        for i in range(2):
                            for t in range(T4):
                                last = nc.tensor.transpose(ps[:, bank[i], t * P:t * P + P],
                                                           full[i][:, t * P:t * P + P], ident)
                        pe_done.by(last)
                    yield

                    @block.vector
                    def _(dve):
                        after_all(dve)
                        for i in range(2):
                            hh = (2 * n + i) % 4
                            last = nc.vector.tensor_copy(row[:, :, hh * P:hh * P + P],
                                                         ps[:, bank[i], :].rearrange("p (t n) -> p t n", t=T4))
                        dve_done.by(last)
                    yield

        def spatial_steps():
            for g in range(4):
                b = 6 + g % 2

                @block.tensor
                def _(pe):
                    after_all(pe)
                    pe.wait_ge(dve_done.sem, normed["v"])
                    for t in range(T4):
                        last = nc.tensor.matmul(ps[:, b, t * P:t * P + P], vn[:, t, g * P:g * P + P],
                                                c("ws", g * P, g * P + P), start=True, stop=True)
                    pe_done.by(last)
                yield

                @block.vector
                def _(dve):
                    after_all(dve)
                    bsr = c("bs", g * P, g * P + P).unsqueeze(1).to_broadcast([P, T4, P])
                    pg = ps[:, b, :].rearrange("p (t n) -> p t n", t=T4)
                    tg = scratch512.rearrange("p (t n) -> p t n", t=T4)
                    link(dve, dve_done, nc.vector.tensor_tensor(tg, pg, bsr, ALU.add))
                    dve_done.by(nc.vector.tensor_tensor(uT[:, g, :], uT[:, g, :], scratch512, ALU.mult))
                yield

        def decay_steps():
            @block.tensor
            def _(pe):
                after_all(pe)
                for d in range(2):
                    for t in range(T4):
                        last = nc.tensor.matmul(ps[:, 6, t * 8 + 4 * d:t * 8 + 4 * d + 4], c(f"tri{d}"),
                                                lal[:, t, 4 * d:4 * d + 4], start=True, stop=True)
                pe_done.by(last)
            yield

            @block.vector
            def _(dve):
                after_all(dve)
                dve_done.by(nc.vector.tensor_copy(gcs.rearrange("p t n -> p (t n)"), ps[:, 6, 0:32]))
            yield

            @block.scalar
            def _(act):
                after_all(act)
                act_done.by(nc.scalar.activation(bgs, gcs, ACT.Exp))
            yield

            @block.vector
            def _(dve):
                after_all(dve)
                dve_done.by(nc.vector.scalar_tensor_tensor(bgs, bgs, -1.0, beta, ALU.mult, ALU.mult))
            yield

        def small_lane():
            yield from gate_lane()
            yield from decay_steps()
            yield from spatial_steps()

        normed = {}
        side_by_side([conv_lane(0), conv_lane(1), conv_lane(2), small_lane(), layer_norm_lane()])

        osum = vn
        PAIR = 2
        STAGGER = 5
        W = PAIR * P
        vecs = lambda x: x.unsqueeze(2).to_broadcast([P, PAIR, P])
        heads = lambda x: x.rearrange("p (h n) -> p h n", h=PAIR)
        both = lambda m: m.unsqueeze(1).to_broadcast([P, PAIR, P])
        reset(mark_gdn)
        ends = [take(2, PAIR) for _ in range(4)]
        scratch512 = small[:, 304:432]
        room = [take(W) for _ in range((ARENA - cur[0]) // W)]
        room += [hT[:, n, a:a + W] for n in range(KT) for a in (0, W)]
        room += [c("final1", a, a + W) for a in range(0, D, W)]
        room += [c(name, a, a + W) for name in ("gate_up", "gate_b") for a in (0, W)]

        @block.gpsimd
        def _(pool):
            after_all(pool)
            pool_done.by(nc.gpsimd.memset(osum, 0.0))

        def delta_pair(d, pair):
            lane = 2 * d + pair
            At, X, TM, UM, attn, qg, kdec, beb, S, lab, eg = (room.pop(0) for _ in range(11))
            DT = X
            r_, vnew = eg, beb
            ba, bb = 2 * lane, 2 * lane + 1
            h0 = PAIR * pair
            lo, hi = slice(0, W), slice(W, 2 * W)
            tri = c(f"tri{d}")
            end = P - 1 if d == 0 else 0
            ed, ge = ends[lane][:, 0, :], ends[lane][:, 1, :]

            @block.gpsimd
            def _(pool):
                after_all(pool)
                pool_done.by(nc.gpsimd.memset(S, 0.0))
            for _ in range(STAGGER * lane):
                yield
            for T in ((0, 1, 2, 3), (1, 0, 3, 2))[d]:
                tok = slice(T * P, T * P + P)
                cols = slice(4 * d + h0, 4 * d + h0 + PAIR)
                la2, be2, gc2, bg2 = lal[:, T, cols], beta[:, T, cols], gcs[:, T, cols], bgs[:, T, cols]
                hs_of = lambda n: slice(n * P, n * P + P)
                hcols = slice(h0 * P, (h0 + PAIR) * P)

                @block.scalar
                def _(act):
                    after_all(act)
                    act_done.by(nc.scalar.activation(heads(lab), vecs(la2), ACT.Copy))
                    act_done.by(nc.scalar.activation(heads(beb), vecs(be2), ACT.Copy))
                yield

                @block.tensor
                def _(pe):
                    after_all(pe)
                    for n in range(PAIR):
                        k_, q_ = kT[:, h0 + n, tok], qT[:, h0 + n, tok]
                        hs, hs2 = hs_of(n), hs_of(PAIR + n)
                        nc.tensor.matmul(ps[:, ba, hs], lab[:, hs], tri, start=True, stop=True)
                        nc.tensor.matmul(ps[:, ba, hs2], beb[:, hs], ident, start=True, stop=True)
                        nc.tensor.matmul(ps[:, bb, hs], k_, k_, start=True, stop=True)
                        last = nc.tensor.matmul(ps[:, bb, hs2], k_, q_, start=True, stop=True)
                    pe_done.by(last)
                yield

                @block.vector
                def _(dve):
                    after_all(dve)
                    for n in range(PAIR):
                        nc.vector.tensor_scalar(DT[:, hs_of(n)], ps[:, ba, hs_of(n)], gc2[:, n:n + 1], 0.0,
                                                ALU.subtract, ALU.min)
                    nc.vector.tensor_copy(ge, heads(ps[:, ba, lo])[:, :, end])
                    dve_done.by(nc.vector.tensor_tensor(ed, heads(ps[:, ba, lo])[:, :, end], gc2, ALU.subtract))
                yield

                @block.scalar
                def _(act):
                    after_all(act)
                    act_done.by(nc.scalar.activation(DT, DT, ACT.Exp))
                    act_done.by(nc.scalar.activation(eg, ps[:, ba, lo], ACT.Exp))
                    act_done.by(nc.scalar.activation(ends[lane], ends[lane], ACT.Exp))
                yield

                @block.vector
                def _(dve):
                    after_all(dve)
                    nc.vector.tensor_tensor(At, ps[:, bb, lo], DT, ALU.mult)
                    link(dve, dve_done, nc.vector.tensor_tensor(attn, ps[:, bb, hi], DT, ALU.mult))
                    link(dve, dve_done, nc.vector.tensor_tensor(At, At, ps[:, ba, hi], ALU.mult))
                    link(dve, dve_done, nc.vector.tensor_tensor(heads(X), heads(At), both(c(f"lev{d}_0")), ALU.mult))
                    dve_done.by(nc.vector.tensor_tensor(heads(UM), both(ident), heads(X), ALU.subtract))
                yield

                @block.tensor
                def _(pe):
                    after_all(pe)
                    for n in range(PAIR):
                        last = nc.tensor.matmul(ps[:, ba, hs_of(n)], X[:, hs_of(n)], ident, start=True, stop=True)
                    pe_done.by(last)

                @block.vector
                def _(dve):
                    nc.vector.tensor_tensor(heads(qg), qT[:, h0:h0 + PAIR, tok], heads(eg), ALU.mult)
                    dve_done.by(nc.vector.tensor_tensor(heads(attn), heads(attn), both(tri), ALU.mult))
                yield

                @block.vector
                def _(dve):
                    after_all(dve)
                    nc.vector.tensor_tensor(heads(TM), both(ident), heads(ps[:, ba, lo]), ALU.subtract)
                    dve_done.by(nc.vector.tensor_tensor(heads(X), heads(At), both(c(f"lev{d}_1")), ALU.mult))

                @block.scalar
                def _(act):
                    after_all(act)
                    for n in range(PAIR):
                        hc = slice((h0 + n) * P, (h0 + n + 1) * P)
                        act_done.by(nc.scalar.activation(kdec[:, hs_of(n)], kt[:, T, hc], ACT.Copy,
                                                         scale=ed[:, n:n + 1]))
                        act_done.by(nc.scalar.activation(r_[:, hs_of(n)], vt[:, T, hc], ACT.Copy,
                                                         scale=be2[:, n:n + 1]))
                yield

                for lev in range(1, 7):
                    @block.tensor
                    def _(pe):
                        after_all(pe)
                        for n in range(PAIR):
                            last = nc.tensor.matmul(ps[:, ba, hs_of(n)], X[:, hs_of(n)], TM[:, hs_of(n)],
                                                    start=True, stop=True)
                        pe_done.by(last)
                    yield

                    @block.scalar
                    def _(act):
                        after_all(act)
                        act_done.by(nc.scalar.activation(lab, ps[:, ba, lo], ACT.Copy))

                    if lev < 6:
                        @block.vector
                        def _(dve):
                            after_all(dve)
                            dve_done.by(nc.vector.tensor_tensor(heads(X), heads(At), both(c(f"lev{d}_{lev + 1}")),
                                                                ALU.mult))
                    yield

                    @block.tensor
                    def _(pe):
                        after_all(pe)
                        for n in range(PAIR):
                            hs = hs_of(n)
                            last = nc.tensor.matmul(ps[:, bb, hs], lab[:, hs], UM[:, hs], start=True, stop=True)
                            if lev < 6:
                                last = nc.tensor.matmul(ps[:, bb, hs_of(PAIR + n)], UM[:, hs], lab[:, hs],
                                                        start=True, stop=True)
                        pe_done.by(last)
                    yield

                    @block.vector
                    def _(dve):
                        after_all(dve)
                        if lev < 6:
                            nc.vector.tensor_tensor(TM, TM, ps[:, bb, hi], ALU.subtract)
                        dve_done.by(nc.vector.tensor_tensor(UM, UM, ps[:, bb, lo], ALU.subtract))
                    yield

                @block.tensor
                def _(pe):
                    after_all(pe)
                    for n in range(PAIR):
                        last = nc.tensor.matmul(ps[:, ba, hs_of(n)], kT[:, h0 + n, tok], S[:, hs_of(n)],
                                                start=True, stop=True)
                    pe_done.by(last)
                yield

                @block.vector
                def _(dve):
                    after_all(dve)
                    for n in range(PAIR):
                        hs = hs_of(n)
                        last = nc.vector.scalar_tensor_tensor(r_[:, hs], ps[:, ba, hs], bg2[:, n:n + 1], r_[:, hs],
                                                              ALU.mult, ALU.add)
                    dve_done.by(last)
                yield

                @block.tensor
                def _(pe):
                    after_all(pe)
                    for n in range(PAIR):
                        last = nc.tensor.matmul(ps[:, bb, hs_of(n)], UM[:, hs_of(n)], r_[:, hs_of(n)],
                                                start=True, stop=True)
                    pe_done.by(last)
                yield

                @block.scalar
                def _(act):
                    after_all(act)
                    act_done.by(nc.scalar.activation(vnew, ps[:, bb, lo], ACT.Copy))
                yield

                @block.tensor
                def _(pe):
                    after_all(pe)
                    for n in range(PAIR):
                        hs, hs2 = hs_of(n), hs_of(PAIR + n)
                        nc.tensor.matmul(ps[:, ba, hs], qg[:, hs], S[:, hs], start=True, stop=False)
                        nc.tensor.matmul(ps[:, ba, hs], attn[:, hs], vnew[:, hs], start=False, stop=True)
                        last = nc.tensor.matmul(ps[:, ba, hs2], kdec[:, hs], vnew[:, hs], start=True, stop=True)
                    pe_done.by(last)
                yield

                @block.vector
                def _(dve):
                    after_all(dve)
                    for n in range(PAIR):
                        hs = hs_of(n)
                        last = nc.vector.scalar_tensor_tensor(S[:, hs], S[:, hs], ge[:, n:n + 1],
                                                              ps[:, ba, hs_of(PAIR + n)], ALU.mult, ALU.add)
                    dve_done.by(last)
                    dve.wait_ge(dve_done.sem, dve_done.n)
                    o_ = osum[:, T, hcols]
                    dve_done.by(nc.vector.tensor_tensor(o_, o_, ps[:, ba, lo], ALU.add))
                yield

        side_by_side([delta_pair(d, pair) for d in range(2) for pair in range(2)])
        as4 = lambda x: x.rearrange("p (h n) -> p h n", h=GH)
        vec4 = lambda x: x.unsqueeze(2).to_broadcast([P, GH, P])

        @block.scalar
        def _(act):
            after_all(act)
            for t in range(T4):
                for hh in range(GH):
                    link(act, act_done, nc.scalar.activation(scratch512[:, 0:P], osum[:, t, hh * P:hh * P + P], ACT.Square,
                                                             accum_out=small[:, 8 + 4 * t + hh:9 + 4 * t + hh]))

        @block.vector
        def _(dve):
            after_all(dve)
            link(dve, dve_done, nc.vector.tensor_scalar(small[:, 24:40], small[:, 8:24], 1.0 / P, EPS,
                                                        ALU.mult, ALU.add))

        @block.gpsimd
        def _(pool):
            after_all(pool)
            inverse_root(pool, small[:, 8:24], small[:, 24:40])

        @block.vector
        def _(dve):
            after_all(dve)
            for t in range(T4):
                ins = nc.vector.tensor_tensor(as4(osum[:, t, :]), as4(osum[:, t, :]),
                                              vec4(small[:, 8 + 4 * t:12 + 4 * t]), ALU.mult)
            dve_done.by(ins)

        @block.tensor
        def _(pe):
            after_all(pe)
            for hh in range(GH):
                for t in range(T4):
                    last = nc.tensor.transpose(ps[:, hh, t * P:t * P + P], osum[:, t, hh * P:hh * P + P], ident)
            pe_done.by(last)

        yT = arena[:, 0:KT * 512].rearrange("p (k t) -> p k t", k=KT)

        @block.vector
        def _(dve):
            after_all(dve)
            for hh in range(GH):
                last = nc.vector.scalar_tensor_tensor(yT[:, 4 + hh, :], ps[:, hh, :], c("b_norm"),
                                                      gT[:, hh, :], ALU.mult, ALU.mult)
            dve_done.by(last)

        def gated_out(rows, scr, src, ntt, kt_):
            settle()
            strm = (lambda t: (cx if t < 2 else h)[:, t % 2, :]) if ntt == 4 else (lambda t: h[:, t, :])
            gt = (lambda t: rows[:, 1 if t < 2 else 0, :]) if ntt == 4 else (lambda t: rows[:, 0, :])
            for n in range(2):
                banks = [(4 * n + i) for i in range(ntt)]
                token_rows(banks, src, 0, kt_)
                add_rows(banks, strm, n, gt, scr)

        reset(KT * 512)
        gate = gate_buffers()
        side_by_side([gate_lane_of(0, 0, *gate, (0, 1))])
        gated_out(*gate, yT, 4, KT)

        conv_centre = sem("conv_centre")
        conv_side = sem("conv_side")
        conv_silu = sem("conv_silu")
        conv_hid = sem("conv_hid")
        conv_left = sem("conv_left")
        cc = {"n": 0}

        @block.vector
        def _(dve):
            dve.sem_inc(conv_side, 2 * RING)
            dve.sem_inc(conv_hid, RING)

        def conv_feed_forward(layer, ntok):
            nf = F_FFN
            segs = ntok // SEQ
            hid = take(nf, ntok)
            cg, cu = take(3, ntok), take(3, ntok)
            t0, c0 = tile_used.n, cc["n"]
            slot = lambda k: (t0 + k) % RING
            looped = nf // RING
            wofs = where["conv_ffn"][0] + layer * 3 * 2 * nf
            tap = lambda j, half, g, s: par[:, bass.ds(g * RING + (wofs + (j * 2 + half) * nf + s), 1)]
            seg = lambda x, a, b_: x.rearrange("p (s t) -> p s t", s=segs)[:, :, a:b_]

            @block.tensor
            def _(pe):
                after_all(pe)

                def up(g, s):
                    pe.wait_ge(landed[slot(s)], g * 16 + 16 * ((t0 + s) // RING + 1))
                    w = ring[:, slot(s), :].rearrange("p (k n) -> p k n", k=KT)
                    pe.wait_ge(conv_side, g * (2 * RING) + 2 * (RING + c0 + s - since(BANKS_CONV, s) + 1))
                    for half in range(2):
                        for k in range(KT):
                            last = nc.tensor.matmul(ps[:, 2 * BANKS_CONV[s] + half, 0:ntok],
                                                    w[:, k, half * P:half * P + P], hT[:, k, 0:ntok],
                                                    start=(k == 0), stop=(k == KT - 1))
                    last.then_inc(tile_used.sem, 1)
                turns(pe, nf, looped, up)

            @block.scalar
            def _(act):
                after_all(act)

                def gate(g, s):
                    b = BANKS_CONV[s]
                    act.wait_ge(tile_used.sem, g * RING + (t0 + s + 1))
                    act.wait_ge(conv_hid, g * RING + (RING + c0 + s - since(BANKS_CONV, s) + 1))
                    for half, buf in enumerate((cg, cu)):
                        nc.scalar.activation(buf[:, b, :], ps[:, 2 * b + half, 0:ntok], ACT.Copy,
                                             scale=tap(1, half, g, s)).then_inc(conv_centre, 1)
                    act.wait_ge(conv_side, g * (2 * RING) + 2 * (RING + c0 + s + 1))
                    nc.scalar.activation(cg[:, b, :], cg[:, b, :], ACT.Silu).then_inc(conv_silu, 1)
                turns(act, nf, looped, gate)

            @block.vector
            def _(dve):
                after_all(dve)

                def hidden(g, s):
                    b = BANKS_CONV[s]
                    dve.wait_ge(conv_centre, g * (2 * RING) + 2 * (c0 + s + 1))
                    for half, buf in enumerate((cg, cu)):
                        x, o = ps[:, 2 * b + half, 0:ntok], buf[:, b, :]
                        nc.vector.scalar_tensor_tensor(seg(o, 1, SEQ), seg(x, 0, SEQ - 1), tap(0, half, g, s),
                                                       seg(o, 1, SEQ), ALU.mult, ALU.add).then_inc(conv_left, 1)
                    dve.wait_ge(conv_left, g * (2 * RING) + 2 * (c0 + s + 1))
                    for half, buf in enumerate((cg, cu)):
                        x, o = ps[:, 2 * b + half, 0:ntok], buf[:, b, :]
                        nc.vector.scalar_tensor_tensor(seg(o, 0, SEQ - 1), seg(x, 1, SEQ), tap(2, half, g, s),
                                                       seg(o, 0, SEQ - 1), ALU.mult, ALU.add).then_inc(conv_side, 1)
                    dve.wait_ge(conv_side, g * (2 * RING) + 2 * (RING + c0 + s + 1))
                    dve.wait_ge(conv_silu, g * RING + (c0 + s + 1))
                    nc.vector.tensor_tensor(hid[:, g * RING + s, :], cg[:, b, :], cu[:, b, :],
                                            ALU.mult).then_inc(conv_hid, 1)
                turns(dve, nf, looped, hidden)
                dve.wait_ge(conv_hid, RING + c0 + nf)
                dve_done.by(nc.vector.tensor_copy(small[:, 480:481], small[:, 481:482]))
            tile_used.n += nf
            cc["n"] += nf
            for b in range(8):
                freed[b] = [(dve_done, dve_done.n)]
            return hid

        def second_ffn(layer, both):
            nonlocal hT
            reset()
            gate = gate_buffers()
            mark = cur[0]
            gates_ = gate_lane_of(layer, 1, *gate, (0, 1) if both else (0,))
            (sc_l, sh_l), (sc_c, sh_c) = modulation(layer, 1, c(f"norm2_{layer}"))
            if both:
                norm_both((sc_c, sh_c), (sc_l, sh_l), gates_)
            else:
                side_by_side([norm_T_steps(h, [(hT, sc_l, sh_l)], 0, take(TT, D)), gates_])
            reset(mark)
            hid = conv_feed_forward(layer, 512 if both else 256)
            gated_out(*gate, hid, 4 if both else 2, F_FFN)

        second_ffn(0, True)

        (sc_l, sh_l), (sc_c, sh_c) = modulation(1, 0, c("norm1_1"))
        reset()
        norm_both((sc_c, sh_c), (sc_l, sh_l))
        reset()
        zkv = take(T4, 320)
        zq = take(TT, 384)
        kr2 = take(T4, P)
        ckvT = take(2, 512)
        krT = take(512)
        cqT = take(3, SEQ)
        qnT = take(MH, SEQ)
        qr = take(TT, 512)
        qrT = take(4, SEQ)
        ra, rb = take(8, 32), take(8, 32)
        v = take(T4, D)
        MLA_LANES = 4
        lane_pp = [take(512) for _ in range(MLA_LANES)]
        lane_pT = [take(T4, SEQ) for _ in range(MLA_LANES)]
        knT = [hT[:, n, :] for n in range(MH)]
        oT = qnT

        def rotate(dve, dst, src, t, n, a_, b_):
            cos = c("cos", 32 * t, 32 * t + 32).unsqueeze(1).to_broadcast([P, n, 32])
            sin = c("sin", 32 * t, 32 * t + 32).unsqueeze(1).to_broadcast([P, n, 32])
            x1, x2 = src[:, :, 0:32], src[:, :, 32:64]
            nc.vector.tensor_tensor(a_, x1, cos, ALU.mult)
            link(dve, dve_done, nc.vector.tensor_tensor(b_, x2, sin, ALU.mult))
            link(dve, dve_done, nc.vector.tensor_tensor(dst[:, :, 0:32], a_, b_, ALU.subtract))
            nc.vector.tensor_tensor(a_, x2, cos, ALU.mult)
            link(dve, dve_done, nc.vector.tensor_tensor(b_, x1, sin, ALU.mult))
            link(dve, dve_done, nc.vector.tensor_tensor(dst[:, :, 32:64], a_, b_, ALU.add))

        def key_lane():
            sq = lane_pp[0]
            ka, kb = (lane_pp[2][:, a:a + 32].unsqueeze(1) for a in (0, 32))

            @block.tensor
            def _(pe):
                after_all(pe)
            token_rows([0, 1, 2, 3], hT, 0, KT, cols=320, kind="keys")

            @block.vector
            def _(dve):
                after_all(dve)
                for t in range(T4):
                    dve_done.by(nc.vector.tensor_copy(zkv[:, t, :], ps[:, t, 0:320]))

            @block.scalar
            def _(act):
                after_all(act)
                for t in range(T4):
                    link(act, act_done, nc.scalar.activation(sq[:, 0:256], ps[:, t, 0:256], ACT.Square,
                                                             accum_out=small[:, 8 + t:9 + t]))
            yield
            rstd_of((8, 12), 256)
            yield

            @block.vector
            def _(dve):
                after_all(dve)
                for t in range(T4):
                    nc.vector.tensor_scalar(zkv[:, t, 0:256], zkv[:, t, 0:256], small[:, 24 + t:25 + t], None,
                                            ALU.mult)
                nc.vector.tensor_copy(kr2[:, 0:2, 0:64], zkv[:, 0:2, 256:320])
                for t in range(2, T4):
                    rotate(dve, kr2[:, t, 0:64].unsqueeze(1), zkv[:, t, 256:320].unsqueeze(1), t - 2, 1, ka, kb)
                dve_done.by(nc.vector.tensor_copy(kr2[:, :, 64:128], kr2[:, :, 0:64]))
            yield

            @block.tensor
            def _(pe):
                after_all(pe)
                for t in range(T4):
                    for k in range(2):
                        nc.tensor.transpose(ps[:, k, t * P:t * P + P], zkv[:, t, k * P:k * P + P], ident)
                    last = nc.tensor.transpose(ps[:, 2, t * P:t * P + P], kr2[:, t, :], ident)
                pe_done.by(last)
            yield

            @block.vector
            def _(dve):
                after_all(dve)
                for k in range(2):
                    nc.vector.tensor_scalar(ckvT[:, k, :], ps[:, k, :], c("kv_n")[:, k:k + 1], None, ALU.mult)
                dve_done.by(nc.vector.tensor_copy(krT, ps[:, 2, :]))
            yield

            for what in range(2):
                for part in range(2):
                    @block.tensor
                    def _(pe):
                        after_all(pe)
                        w = (weights(pe, "keys") if part == 0 else ring[:, tile_used.n % RING, :])
                        w = w.rearrange("p (k n) -> p k n", k=2)
                        for b in range(4):
                            i = 4 * part + b
                            for k in range(2):
                                if what == 0:
                                    lhs, rhs = w[:, k, i * P:i * P + P], ckvT[:, k, :]
                                else:
                                    t, n = i // 2, i % 2
                                    lhs, rhs = ckvT[:, k, t * P:t * P + P], w[:, k, n * 512:n * 512 + 512]
                                last = nc.tensor.matmul(ps[:, b, :], lhs, rhs, start=(k == 0), stop=(k == 1))
                        (tile_used if part == 1 else pe_done).by(last)

                    def copy(eng_copy, done, banks):
                        for b in banks:
                            i = 4 * part + b
                            dst = knT[i] if what == 0 else v[:, i // 2, (i % 2) * 512:(i % 2) * 512 + 512]
                            done.by(eng_copy(dst, ps[:, b, :]))

                    @block.vector
                    def _(dve):
                        after_all(dve)
                        copy(nc.vector.tensor_copy, dve_done, (0, 1))

                    @block.scalar
                    def _(act):
                        after_all(act)
                        copy(lambda o, x: nc.scalar.activation(o, x, ACT.Copy), act_done, (2, 3))
                yield

        def query_lane():
            sq = lane_pp[1]

            @block.tensor
            def _(pe):
                after_all(pe)
            token_rows([4, 5], hT, SEQ, KT, cols=384, kind="queries")

            @block.vector
            def _(dve):
                after_all(dve)
                for t in range(TT):
                    dve_done.by(nc.vector.tensor_copy(zq[:, t, :], ps[:, 4 + t, 0:384]))

            @block.scalar
            def _(act):
                after_all(act)
                for t in range(TT):
                    link(act, act_done, nc.scalar.activation(sq[:, 0:384], ps[:, 4 + t, 0:384], ACT.Square,
                                                             accum_out=small[:, 12 + t:13 + t]))
            yield
            rstd_of((12, 14), 384)
            yield

            @block.vector
            def _(dve):
                after_all(dve)
                for t in range(TT):
                    last = nc.vector.tensor_scalar(zq[:, t, :], zq[:, t, :], small[:, 28 + t:29 + t], None, ALU.mult)
                dve_done.by(last)
            yield

            @block.tensor
            def _(pe):
                after_all(pe)
                for t in range(TT):
                    for k in range(3):
                        last = nc.tensor.transpose(ps[:, 4 + k, t * P:t * P + P], zq[:, t, k * P:k * P + P], ident)
                pe_done.by(last)
            yield

            @block.vector
            def _(dve):
                after_all(dve)
                for k in range(3):
                    last = nc.vector.tensor_scalar(cqT[:, k, :], ps[:, 4 + k, 0:SEQ], c("q_n")[:, k:k + 1], None,
                                                   ALU.mult)
                dve_done.by(last)
            yield

            @block.tensor
            def _(pe):
                after_all(pe)
            token_rows([4, 5], cqT, 0, 3, kind="queries")
            yield

            @block.vector
            def _(dve):
                after_all(dve)
                for t in range(TT):
                    rotate(dve, qr[:, t, :].rearrange("p (h n) -> p h n", h=8),
                           ps[:, 4 + t, :].rearrange("p (h n) -> p h n", h=8), t, 8, ra, rb)

            for n in range(2):
                @block.tensor
                def _(pe):
                    if n:
                        after_all(pe)
                    w = weights(pe, "queries").rearrange("p (k n) -> p k n", k=4)
                    for i in range(4):
                        for k in range(3):
                            last = nc.tensor.matmul(ps[:, 6 + i // 2, (i % 2) * SEQ:(i % 2) * SEQ + SEQ],
                                                    w[:, k, i * P:i * P + P], cqT[:, k, :],
                                                    start=(k == 0), stop=(k == 2))
                    tile_used.by(last)

                @block.scalar
                def _(act):
                    after_all(act)
                    act_done.by(nc.scalar.activation(qnT[:, 4 * n:4 * n + 4, :].rearrange("p h t -> p (h t)"),
                                                     ps[:, 6:8, :].rearrange("p b n -> p (b n)"), ACT.Copy))
                yield

            @block.tensor
            def _(pe):
                after_all(pe)
                for k in range(4):
                    for t in range(TT):
                        last = nc.tensor.transpose(ps[:, 4 + k // 2, (k % 2) * SEQ + t * P:(k % 2) * SEQ + t * P + P],
                                                   qr[:, t, k * P:k * P + P], ident)
                pe_done.by(last)
            yield

            @block.vector
            def _(dve):
                after_all(dve)
                dve_done.by(nc.vector.tensor_copy(qrT.rearrange("p k t -> p (k t)"), ps[:, 4:6, :]))
            yield

        side_by_side([key_lane(), query_lane()])
        scale = float(128 + 64) ** -0.5

        def latent_lane(lane):
            pp, pT = lane_pp[lane], lane_pT[lane]
            b0, b1 = 2 * lane, 2 * lane + 1
            st = small[:, 64 + 8 * lane:72 + 8 * lane]
            for hh in range(lane, MH, MLA_LANES):
                ro = 64 * (hh % 2)
                for t in range(TT):
                    @block.tensor
                    def _(pe):
                        after_all(pe)
                        nc.tensor.matmul(ps[:, b0, :], qnT[:, hh, t * P:t * P + P], knT[hh],
                                         start=True, stop=False)
                        pe_done.by(nc.tensor.matmul(ps[:, b0, :], qrT[ro:ro + 64, hh // 2, t * P:t * P + P],
                                                    krT[ro:ro + 64, :], start=False, stop=True))
                    yield

                    @block.vector
                    def _(dve):
                        after_all(dve)
                        link(dve, dve_done, nc.vector.reduce_max(st[:, 0:1], ps[:, b0, :], AXX))
                        dve_done.by(nc.vector.tensor_scalar(st[:, 1:2], st[:, 0:1], -scale, None, ALU.mult))
                    yield

                    @block.scalar
                    def _(act):
                        after_all(act)
                        act_done.by(nc.scalar.activation(pp, ps[:, b0, :], ACT.Exp, bias=st[:, 1:2], scale=scale,
                                                         accum_out=st[:, 2:3]))
                    yield

                    @block.vector
                    def _(dve):
                        after_all(dve)
                        link(dve, dve_done, nc.vector.reciprocal(st[:, 3:4], st[:, 2:3]))
                        dve_done.by(nc.vector.tensor_scalar(pp, pp, st[:, 3:4], None, ALU.mult))
                    yield

                    @block.tensor
                    def _(pe):
                        after_all(pe)
                        for j in range(T4):
                            last = nc.tensor.transpose(ps[:, b1, j * P:j * P + P], pp[:, j * P:j * P + P], ident)
                        pe_done.by(last)
                    yield

                    @block.scalar
                    def _(act):
                        after_all(act)
                        act_done.by(nc.scalar.activation(pT[:, :, t * P:t * P + P],
                                                         ps[:, b1, :].rearrange("p (j n) -> p j n", j=T4), ACT.Copy))
                    yield

                @block.tensor
                def _(pe):
                    after_all(pe)
                    for j in range(T4):
                        last = nc.tensor.matmul(ps[:, b0, 0:SEQ], v[:, j, hh * P:hh * P + P], pT[:, j, :],
                                                start=(j == 0), stop=(j == T4 - 1))
                    pe_done.by(last)
                yield

                @block.vector
                def _(dve):
                    after_all(dve)
                    dve_done.by(nc.vector.tensor_copy(oT[:, hh, :], ps[:, b0, 0:SEQ]))
                yield

        side_by_side([latent_lane(n) for n in range(MLA_LANES)])

        @block.vector
        def _(dve):
            after_all(dve)
            dve_done.by(nc.vector.tensor_copy(hT[:, :, 0:SEQ], oT))
        reset()
        for eng in (block.vector, block.tensor):
            @eng
            def _(e):
                after_all(e)
        gate = gate_buffers()
        side_by_side([gate_lane_of(1, 0, *gate, (0,))])
        gated_out(*gate, hT, 2, KT)
        second_ffn(1, False)
        final_norm(c("final2"))
        assert tile_used.n == n_tiles, (tile_used.n, n_tiles)

        @block.sync
        def _(sp):
            load_turns(sp, moe_turn, n_tiles // RING)
            for t in range(n_tiles // RING * RING, n_tiles):
                sp.wait_ge(tile_used.sem, t - RING + 1)
                sp.dma_start(ring[:, t % RING, :], stream[t]).then_inc(landed[t % RING], 16)
            sp.wait_ge(dve_done.sem, dve_done.n)
            for t in range(TT):
                sp.dma_start(out["out"][t * P:t * P + P, :], h[:, t, :]).then_inc(stored, 16)
            sp.wait_ge(stored, 16 * TT)
    return order




def weight_stream(i, order):
    tiles = []

    def features(w, *firsts):
        w8 = w.reshape(KT, P, -1)
        t = np.stack([w8[:, :, f:f + P] for f in firsts], axis=2)
        tiles.append(t.transpose(1, 0, 2, 3).reshape(P, TILE))

    def rows(w, col, cols=512, kper=4):
        k = w.shape[0] // P
        wide = TILE // kper
        wk = w.reshape(k, P, -1)[:, :, col:col + cols]
        for k0 in range(0, k, kper):
            t = np.zeros((kper, P, wide), np.float32)
            part = wk[k0:k0 + kper]
            t[:part.shape[0], :, :part.shape[2]] = part
            tiles.append(t.transpose(1, 0, 2).reshape(P, TILE))

    def span(w, a, b):
        for n in range(a, b, 2 * P):
            features(w, n, n + P)

    def both_halves(w):
        rows(w, 0)
        rows(w, 512)

    for layer in range(2):
        span(i["ada_w_2"][layer], 0, 6 * D)
    of_ada, tiles[:] = list(tiles), []
    w = i["gla_w_in"][0]
    span(w, 0, 1024)
    rows(w, 1024), rows(w, 1536)
    span(w, 2064, 3088)
    of_gla, tiles[:] = list(tiles), []

    def in_turn(**lists):
        turn = {kind: iter(tiles_) for kind, tiles_ in lists.items()}
        return [next(turn[kind]) for kind in order if kind in turn]

    tiles.extend(in_turn(ada=of_ada, gla=of_gla))
    both_halves(i["gla_w_out"][0])
    g, u = i["ffn_w_gate"][0], i["ffn_w_up"][0]
    gu = np.concatenate([g, u], axis=1)
    for f in range(F_FFN):
        features(gu, f * P, FF + f * P)
    both_halves(i["ffn_w_down"][0])
    span(i["sb_w_kv"], 0, 1024)
    rows(i["sb_w_kv"], 1024), rows(i["sb_w_kv"], 1536)
    span(i["sb_w_q"][0], 0, 1024)
    both_halves(i["sb_w_out"][0])
    for e in range(EXPERTS):
        gu = np.concatenate([i["moe_w_gate"][0, e], i["moe_w_up"][0, e]], axis=1)
        for f in range(F_MOE):
            features(gu, f * P, F_MOE * P + f * P)
        both_halves(i["moe_w_down"][0, e])
    w = i["ab_w_in_2"][0]
    span(w, 0, 512)
    rows(w, 512)
    before, tiles[:] = list(tiles), []
    span(w, 1024, 3072)
    mixer, tiles[:] = list(tiles), before
    tiles.extend(in_turn(out_gate=mixer[6:], **{f"qkv{n}": [mixer[n]] for n in range(6)}))
    both_halves(i["ab_w_out_2"][0])

    def conv_ffn(layer):
        for f in range(F_FFN):
            features(i["ffn_w_up_2"][layer], f * P, FF + f * P)
        both_halves(i["ffn_w_down_2"][layer])

    conv_ffn(0)
    w = i["mla_w_in_2"][0]
    before, tiles[:] = list(tiles), []
    rows(w, 384, 320)
    ukv = i["mla_w_ukv_2"][0].reshape(256, MH, 256)
    rows(ukv[:, :, 0:128].reshape(256, D), 0, D, 2)
    rows(ukv[:, :, 128:256].reshape(256, D), 0, D, 2)
    keys, tiles[:] = list(tiles), []
    rows(w, 0, 384)
    uq = i["mla_w_uq_2"][0].reshape(384, MH, 192)
    nope = uq[:, :, 0:128].reshape(384, MH * 128)
    rows(uq[:, :, 128:192].reshape(384, MH * 64), 0)
    rows(nope, 0), rows(nope, 512)
    queries, tiles[:] = list(tiles), before
    tiles.extend(in_turn(keys=keys, queries=queries))
    both_halves(i["mla_w_out_2"][0])
    conv_ffn(1)
    return np.stack(tiles)


def parameters(i):
    out = {}
    f32 = np.float32

    def col(v):
        return v.reshape(-1, P).T

    def rep(v):
        return np.broadcast_to(v.reshape(1, -1), (P, v.size))

    def padded(a):
        z = np.zeros((P, a.shape[1]), f32)
        z[:a.shape[0]] = a
        return z

    def ktiles(w):
        return w.reshape(KT, P, -1).transpose(1, 0, 2).reshape(P, -1)

    r = np.arange(P)
    out["ident"] = np.eye(P, dtype=f32)
    out["ones"] = np.ones((P, P), f32)
    out["minus"] = -np.ones((P, P), f32)
    out["attn0"], out["attn1"] = col(i["attn_norm"][0]), col(i["attn_norm"][1])
    out["ffn0"], out["ffn1"] = col(i["ffn_norm"][0]), col(i["ffn_norm"][1])
    out["kvn"] = col(i["kv_norm"])
    for layer in range(2):
        out[f"norm1_{layer}"] = col(i["norm1_g_2"][layer])
        out[f"norm2_{layer}"] = col(i["norm2_g_2"][layer])
    out["gla_head"] = col(i["gla_head_norm"][0])
    out["b_norm"] = col(i["b_norm_g_2"][0])
    out["q_n"], out["kv_n"] = col(i["mla_q_norm_g_2"][0]), col(i["mla_kv_norm_g_2"][0])
    b = i["ada_b_2"].reshape(2 * 48, P).T
    out["ada_b"] = np.repeat(b, 2, axis=1)
    out["cond"] = np.stack([i["c_2"][0], i["c_ctx_2"]], axis=1).reshape(KT, P, 2).transpose(1, 0, 2).reshape(P, -1)
    out["w_glr"] = ktiles(i["gla_w_in"][0][:, 2048:2064])
    out["gate_up"] = padded(i["gla_w_gate_up"][0])
    out["gate_b"] = padded(i["gla_b_gate"])
    same = (r[:, None] // CHUNK) == (r[None, :] // CHUNK)
    out["gla_mask"] = (same & (r[:, None] <= r[None, :])).astype(f32)
    out["gla_sum"] = out["gla_mask"] / f32(16)
    out["router"] = ktiles(i["moe_w_router"][0])
    slots = np.arange(P, dtype=f32)
    slots[CAP:] = -1
    out["slots"] = rep(slots)
    out["iota8"] = rep(np.arange(8, dtype=f32))
    t = np.arange(SEQ)
    out["sb_mask"] = np.concatenate([(r[:, None] + P * j < t[None, :]) for j in range(TT)], axis=1).astype(f32)
    out["sb_later"] = -(r[:, None] > r[None, :]).astype(f32)
    out["w_ab"] = ktiles(i["ab_w_in_2"][0][:, 3072:3088])
    out["ln_g"], out["ln_b"] = rep(i["a_ln_g_2"][0]), rep(i["a_ln_b_2"][0])
    out["ws"] = i["a_ws_2"][0].transpose(2, 0, 1).reshape(P, -1)
    out["bs"] = rep(i["a_bs_2"][0])
    out["conv_qkv"] = i["b_conv_w_2"][0].reshape(3 * 12, P).T
    out["conv_ffn"] = i["ffn_conv_w_2"].reshape(2 * 3 * 2 * F_FFN, P).T
    out["a_log"], out["dt_bias"] = rep(i["b_a_log_2"][0]), rep(i["b_dt_bias_2"][0])
    out["final1"], out["final2"] = rep(i["final_norm"]), rep(i["final_g_2"])
    j, k = r[:, None], r[None, :]
    for d in range(2):
        before = (j < k) if d == 0 else (j > k)
        out[f"tri{d}"] = (before | (j == k)).astype(f32)
        out[f"strict{d}"] = before.astype(f32)
        for lev in range(7):
            s = 1 << lev
            out[f"lev{d}_{lev}"] = (before & (j // (2 * s) == k // (2 * s)) & (j // s != k // s)).astype(f32)
    rows_, grid = SEQ // 64, 64
    row = np.repeat(np.arange(rows_, dtype=f32), grid)
    colv = np.tile(np.arange(grid, dtype=f32), rows_)
    inv = (f32(10000.0) ** (-np.arange(16, dtype=f32) / f32(16))).astype(f32)
    ang = np.concatenate([row[:, None] * inv, colv[:, None] * inv], axis=-1)
    out["cos"] = np.cos(ang).astype(f32).reshape(TT, P, 32).transpose(1, 0, 2).reshape(P, -1)
    out["sin"] = np.sin(ang).astype(f32).reshape(TT, P, 32).transpose(1, 0, 2).reshape(P, -1)
    early = ["ident", "ones", "cond", "attn0", "ada_b", "w_glr", "gate_up", "gate_b", "gla_sum", "gla_mask", "gla_head"]
    out = {name: out[name] for name in early} | out
    where, at = {"first": sum(out[name].shape[1] for name in early)}, 0
    for name, a in out.items():
        where[name] = (at, a.shape[1])
        at += a.shape[1]
    return np.concatenate(list(out.values()), axis=1).astype(f32), where


def kernel(**inputs):
    import concourse.bacc as _bacc
    from concourse.bass_utils import run_bass_kernel_spmd as _run

    i = {k: np.asarray(v) for k, v in inputs.items()}
    par, where = parameters(i)
    arrays = {
        "in_params": np.ascontiguousarray(par),
        "in_x": np.ascontiguousarray(i["x"][0]),
        "in_ctx": np.ascontiguousarray(i["ctx_2"][0]),
    }
    shapes = {"in_stream": (TILES, P, TILE)} | {n: a.shape for n, a in arrays.items()}
    nc = _bacc.Bacc("TRN2", target_bir_lowering=False, num_devices=1)
    aps = {n: nc.dram_tensor(n, a, F32, kind="ExternalInput").ap() for n, a in shapes.items()}
    out = nc.dram_tensor("out_0", (SEQ, D), F32, kind="ExternalOutput").ap()
    order = build(nc, aps["in_stream"], aps["in_params"], where,
                  {"x": aps["in_x"], "ctx": aps["in_ctx"], "out": out})
    arrays["in_stream"] = weight_stream(i, order)
    r = _run(nc, [arrays], core_ids=[0])
    return r.results[0]["out_0"].reshape(1, SEQ, D)
```
